# Optimizing a Trainium2 kernel written in Bass

```python
import jax, jax.numpy as jnp
from jax import lax
import numpy as np

D_MODEL = 1024
BATCH = 1
SEQ = 512
DEPTH = 1

D_POOL = D_MODEL
POOL_GROUPS = 4
POOL_GROUP_DIM = D_POOL // POOL_GROUPS
POOL_WINDOWS = (2, 4, 8, 16)
D_MLSTM = D_MODEL
MLSTM_HEADS = 4
HEAD_DIM = D_MLSTM // MLSTM_HEADS
N_DIRS = 2
CONV_WIDTH = 5
CHUNK = 128
N_BRANCHES = 2
EPS = 1e-6
NEG_INIT = -1e30
SPLIT_SIZES = (D_POOL, D_POOL, D_MLSTM, D_MLSTM, D_MLSTM, D_MLSTM, D_MLSTM,
               2 * N_DIRS * MLSTM_HEADS, D_MODEL, D_MODEL)
D_IN = 2 * D_POOL + 5 * D_MLSTM + 2 * N_DIRS * MLSTM_HEADS + N_BRANCHES * D_MODEL


def rms_norm(x, g):
    xf = x.astype(jnp.float32)
    y = xf * lax.rsqrt(jnp.mean(xf * xf, axis=-1, keepdims=True) + EPS)
    return (y * g.astype(jnp.float32)).astype(x.dtype)

def multiscale_pool(u):
    B, S, _ = u.shape
    uf = u.astype(jnp.float32)
    cs = jnp.concatenate([jnp.zeros((B, 1, D_POOL), jnp.float32), jnp.cumsum(uf, axis=1)], axis=1)
    t = jnp.arange(S)
    outs = []
    for g, w in enumerate(POOL_WINDOWS):
        lo = jnp.clip(t - w // 2, 0, S - 1)
        hi = jnp.clip(t + (w - 1 - w // 2), 0, S - 1)
        sl = slice(g * POOL_GROUP_DIM, (g + 1) * POOL_GROUP_DIM)
        csg = cs[:, :, sl]
        window_sum = jnp.take(csg, hi + 1, axis=1) - jnp.take(csg, lo, axis=1)
        count = (hi - lo + 1).astype(jnp.float32)[None, :, None]
        outs.append(window_sum / count - uf[:, :, sl])
    return jnp.concatenate(outs, axis=-1)

def centred_depthwise_conv(x, w, b):
    C = x.shape[-1]
    y = lax.conv_general_dilated(
        x, w[:, None, :].astype(x.dtype), window_strides=(1,),
        padding=[(CONV_WIDTH // 2, CONV_WIDTH // 2)],
        dimension_numbers=('NWC', 'WIO', 'NWC'), feature_group_count=C)
    return y + b.astype(x.dtype)

def mlstm_direction(q, k, v, i_pre, f_pre):
    B, H, S, Dh = q.shape
    nc = S // CHUNK
    qc = q.reshape(B, H, nc, CHUNK, Dh) * (Dh ** -0.5)
    kc = k.reshape(B, H, nc, CHUNK, Dh)
    vc = v.reshape(B, H, nc, CHUNK, Dh)
    log_f = jax.nn.log_sigmoid(f_pre).reshape(B, H, nc, CHUNK)
    log_i = i_pre.reshape(B, H, nc, CHUNK)
    b = jnp.cumsum(log_f, axis=-1)
    b_last = b[..., -1]

    w_end = b_last[..., None] - b + log_i
    m_chunk = jnp.max(w_end, axis=-1)
    kw = kc * jnp.exp(w_end - m_chunk[..., None])[..., None]
    c_chunk = jnp.einsum('bhcld,bhcle->bhcde', kw, vc)
    n_chunk = jnp.sum(kw, axis=3)

    def step(carry, xs):
        c_st, n_st, m_st = carry
        c_add, n_add, m_add, bl, q_blk = xs
        num_inter = jnp.einsum('bhld,bhde->bhle', q_blk, c_st)
        den_inter = jnp.einsum('bhld,bhd->bhl', q_blk, n_st)
        m_new = jnp.maximum(bl + m_st, m_add)
        keep = jnp.exp(bl + m_st - m_new)
        add = jnp.exp(m_add - m_new)
        c_new = keep[..., None, None] * c_st + add[..., None, None] * c_add
        n_new = keep[..., None] * n_st + add[..., None] * n_add
        return (c_new, n_new, m_new), (num_inter, den_inter, m_st)

    init = (jnp.zeros((B, H, Dh, Dh), jnp.float32),
            jnp.zeros((B, H, Dh), jnp.float32),
            jnp.full((B, H), NEG_INIT, jnp.float32))
    xs = (jnp.moveaxis(c_chunk, 2, 0), jnp.moveaxis(n_chunk, 2, 0), jnp.moveaxis(m_chunk, 2, 0),
          jnp.moveaxis(b_last, 2, 0), jnp.moveaxis(qc, 2, 0))
    _, (num_inter, den_inter, m_prev) = lax.scan(step, init, xs)
    num_inter = jnp.moveaxis(num_inter, 0, 2)
    den_inter = jnp.moveaxis(den_inter, 0, 2)
    m_prev = jnp.moveaxis(m_prev, 0, 2)

    mask = jnp.tril(jnp.ones((CHUNK, CHUNK), dtype=bool))
    log_d = jnp.where(mask, b[..., :, None] - b[..., None, :] + log_i[..., None, :], -jnp.inf)
    log_inter = b + m_prev[..., None]
    m_t = jnp.maximum(jnp.max(log_d, axis=-1), log_inter)
    d = jnp.exp(log_d - m_t[..., None])
    inter_scale = jnp.exp(log_inter - m_t)
    scores = jnp.einsum('bhcld,bhcsd->bhcls', qc, kc) * d
    num = jnp.einsum('bhcls,bhcsd->bhcld', scores, vc) + inter_scale[..., None] * num_inter
    den = jnp.sum(scores, axis=-1) + inter_scale * den_inter
    h = num / jnp.maximum(jnp.abs(den), jnp.exp(-m_t))[..., None]
    return h.reshape(B, H, S, Dh)

def hybrid_layer(x, norm_pre_g, w_in, conv_qk_w, conv_qk_b, b_igate, b_fgate, pool_mix_w,
                 pool_scale, mlstm_norm_g, w_proj_pool, w_proj_mlstm, b_merge, w_out, norm_post_g):
    B, S, _ = x.shape
    h = rms_norm(x, norm_pre_g)
    proj = jnp.einsum('bsd,de->bse', h, w_in.astype(h.dtype))
    split_points = [int(p) for p in np.cumsum(SPLIT_SIZES)[:-1]]
    u_a, z_a, q, k, v, o, z_b, gates, g_a, g_b = jnp.split(proj, split_points, axis=-1)

    pooled = multiscale_pool(u_a)
    mixed = jnp.einsum('bsgc,gcd->bsgd', pooled.reshape(B, S, POOL_GROUPS, POOL_GROUP_DIM),
                       pool_mix_w.astype(jnp.float32)).reshape(B, S, D_POOL)
    y_a = (mixed * pool_scale.astype(jnp.float32)).astype(x.dtype) * jax.nn.silu(z_a)

    qk = jax.nn.silu(centred_depthwise_conv(jnp.concatenate([q, k], axis=-1), conv_qk_w, conv_qk_b))
    q, k = jnp.split(qk, 2, axis=-1)

    def to_heads(t):
        return t.astype(jnp.float32).reshape(B, S, MLSTM_HEADS, HEAD_DIM).transpose(0, 2, 1, 3)

    qh, kh, vh = to_heads(q), to_heads(k), to_heads(v)
    gates = gates.astype(jnp.float32).reshape(B, S, N_DIRS, 2, MLSTM_HEADS)
    i_pre = (gates[:, :, :, 0, :] + b_igate.astype(jnp.float32)).transpose(2, 0, 3, 1)
    f_pre = (gates[:, :, :, 1, :] + b_fgate.astype(jnp.float32)).transpose(2, 0, 3, 1)
    h_fwd = mlstm_direction(qh, kh, vh, i_pre[0], f_pre[0])
    flip = lambda t: jnp.flip(t, axis=2)
    h_bwd = flip(mlstm_direction(flip(qh), flip(kh), flip(vh), flip(i_pre[1]), flip(f_pre[1])))
    hb = h_fwd + h_bwd
    hb = hb * lax.rsqrt(jnp.mean(hb * hb, axis=-1, keepdims=True) + EPS)
    hb = hb.transpose(0, 2, 1, 3).reshape(B, S, D_MLSTM) * mlstm_norm_g.astype(jnp.float32)
    y_b = hb.astype(x.dtype) * jax.nn.sigmoid(o) * jax.nn.silu(z_b)

    p_a = jnp.einsum('bsc,cd->bsd', y_a, w_proj_pool.astype(y_a.dtype))
    p_b = jnp.einsum('bsc,cd->bsd', y_b, w_proj_mlstm.astype(y_b.dtype))
    merged = jax.nn.sigmoid(g_a + b_merge[0]) * p_a + jax.nn.sigmoid(g_b + b_merge[1]) * p_b
    out = jnp.einsum('bsd,de->bse', merged, w_out.astype(merged.dtype))
    return x + rms_norm(out, norm_post_g)

def first_inputs(seed: int = 0) -> dict:
    key = jax.random.key(seed)
    ks = jax.random.split(key, 16)
    n = jax.random.normal
    f32 = jnp.float32
    x = n(ks[0], (BATCH, SEQ, D_MODEL), f32)
    norm_pre_g = 1.0 + 0.1 * n(ks[1], (DEPTH, D_MODEL), f32)
    w_in = n(ks[2], (DEPTH, D_MODEL, D_IN), f32) * D_MODEL ** -0.5
    conv_qk_w = n(ks[3], (DEPTH, CONV_WIDTH, 2 * D_MLSTM), f32) * CONV_WIDTH ** -0.5
    conv_qk_b = 0.02 * n(ks[4], (DEPTH, 2 * D_MLSTM), f32)
    b_igate = 0.1 * n(ks[5], (DEPTH, N_DIRS, MLSTM_HEADS), f32)
    b_fgate = jnp.linspace(3.0, 6.0, MLSTM_HEADS, dtype=f32)[None, None, :] + 0.1 * n(ks[6], (DEPTH, N_DIRS, MLSTM_HEADS), f32)
    pool_mix_w = n(ks[7], (DEPTH, POOL_GROUPS, POOL_GROUP_DIM, POOL_GROUP_DIM), f32) * POOL_GROUP_DIM ** -0.5
    pool_scale = 1.0 + 0.1 * n(ks[8], (DEPTH, D_POOL), f32)
    mlstm_norm_g = 1.0 + 0.1 * n(ks[9], (DEPTH, D_MLSTM), f32)
    w_proj_pool = n(ks[10], (DEPTH, D_POOL, D_MODEL), f32) * D_POOL ** -0.5
    w_proj_mlstm = n(ks[11], (DEPTH, D_MLSTM, D_MODEL), f32) * D_MLSTM ** -0.5
    b_merge = 0.1 * n(ks[12], (DEPTH, N_BRANCHES, D_MODEL), f32)
    w_out = n(ks[13], (DEPTH, D_MODEL, D_MODEL), f32) * D_MODEL ** -0.5
    norm_post_g = 1.0 + 0.1 * n(ks[14], (DEPTH, D_MODEL), f32)
    return {"x": x, "norm_pre_g": norm_pre_g, "w_in": w_in, "conv_qk_w": conv_qk_w,
            "conv_qk_b": conv_qk_b, "b_igate": b_igate, "b_fgate": b_fgate,
            "pool_mix_w": pool_mix_w, "pool_scale": pool_scale, "mlstm_norm_g": mlstm_norm_g,
            "w_proj_pool": w_proj_pool, "w_proj_mlstm": w_proj_mlstm, "b_merge": b_merge,
            "w_out": w_out, "norm_post_g": norm_post_g}

def first_block(x, norm_pre_g, w_in, conv_qk_w, conv_qk_b, b_igate, b_fgate, pool_mix_w, pool_scale,
              mlstm_norm_g, w_proj_pool, w_proj_mlstm, b_merge, w_out, norm_post_g):
    for l in range(DEPTH):
        x = hybrid_layer(x, norm_pre_g[l], w_in[l], conv_qk_w[l], conv_qk_b[l], b_igate[l], b_fgate[l],
                         pool_mix_w[l], pool_scale[l], mlstm_norm_g[l], w_proj_pool[l], w_proj_mlstm[l],
                         b_merge[l], w_out[l], norm_post_g[l])
    return x


DEPTH_2 = 2

HEAD_DIM_2 = 64
A_Q_HEADS = 6
A_KV_HEADS = 2
WINDOW = 128
B_HEADS = 6
MOBA_BLOCK = 256
MOBA_TOPK = 3
MOBA_Q_CHUNK = 64
C_HEADS = 12
FOX_Q_BLOCK = 128
MEM_HEADS = 4
MEM_LEN = 256
EVEN_MIX = (A_Q_HEADS + B_HEADS + MEM_HEADS) * HEAD_DIM_2
ODD_MIX = (C_HEADS + MEM_HEADS) * HEAD_DIM_2
EVEN_SPLIT = [A_Q_HEADS * HEAD_DIM_2, A_KV_HEADS * HEAD_DIM_2, A_KV_HEADS * HEAD_DIM_2,
              B_HEADS * HEAD_DIM_2, B_HEADS * HEAD_DIM_2, B_HEADS * HEAD_DIM_2,
              MEM_HEADS * HEAD_DIM_2, EVEN_MIX]
ODD_SPLIT = [C_HEADS * HEAD_DIM_2, C_HEADS * HEAD_DIM_2, C_HEADS * HEAD_DIM_2, C_HEADS,
             MEM_HEADS * HEAD_DIM_2, ODD_MIX]
EVEN_IN = sum(EVEN_SPLIT)
ODD_IN = sum(ODD_SPLIT)
N_ALIBI = A_Q_HEADS + B_HEADS
NEG = -1e30
SCALE = HEAD_DIM_2 ** -0.5


def rms_norm_2(x, g):
    xf = x.astype(jnp.float32)
    y = xf * lax.rsqrt(jnp.mean(xf * xf, axis=-1, keepdims=True) + EPS)
    return (y * g.astype(jnp.float32)).astype(x.dtype)

def split_cols(h, sizes):
    return jnp.split(h, np.cumsum(sizes)[:-1].tolist(), axis=-1)

def split_heads(t, n):
    return t.reshape(t.shape[0], t.shape[1], n, HEAD_DIM_2)

def alibi_slopes():
    h = jnp.arange(1, N_ALIBI + 1, dtype=jnp.float32)
    return 2.0 ** (-8.0 * h / N_ALIBI)

def sliding_window_sink_attn(q, k, v, sinks, slopes):
    B, S, HQ, _ = q.shape
    HKV = k.shape[2]
    G = HQ // HKV
    W = WINDOW
    nb = S // W
    qb = q.reshape(B, nb, W, HKV, G, HEAD_DIM_2)

    def band(t):
        tb = t.reshape(B, nb, W, HKV, HEAD_DIM_2)
        prev = jnp.pad(tb, ((0, 0), (1, 0), (0, 0), (0, 0), (0, 0)))[:, :-1]
        return jnp.concatenate([prev, tb], axis=2)

    kb, vb = band(k), band(v)
    logits = jnp.einsum('bnqkgd,bnskd->bnkgqs', qb, kb,
                        preferred_element_type=jnp.float32) * SCALE
    qpos = jnp.arange(nb)[:, None] * W + jnp.arange(W)[None, :]
    kpos = jnp.arange(nb)[:, None] * W - W + jnp.arange(2 * W)[None, :]
    dist = qpos[:, :, None] - kpos[:, None, :]
    allowed = (dist >= 0) & (dist < W) & (kpos[:, None, :] >= 0)
    sl = slopes.reshape(HKV, G)[None, None, :, :, None, None]
    logits = logits - sl * dist[None, :, None, None].astype(jnp.float32)
    logits = jnp.where(allowed[None, :, None, None], logits, NEG)
    sink = jnp.broadcast_to(
        sinks.astype(jnp.float32).reshape(HKV, G)[None, None, :, :, None, None],
        logits.shape[:-1] + (1,))
    p = jax.nn.softmax(jnp.concatenate([logits, sink], axis=-1), axis=-1)[..., :-1]
    o = jnp.einsum('bnkgqs,bnskd->bnqkgd', p.astype(v.dtype), vb)
    return o.reshape(B, S, HQ * HEAD_DIM_2)

def moba_attn(q, k, v, slopes):
    B, S, H, _ = q.shape
    L = MOBA_BLOCK
    nblk = -(-S // L)
    Sp = nblk * L
    pad = ((0, 0), (0, Sp - S), (0, 0), (0, 0))
    q, k, v = [jnp.pad(t, pad).transpose(0, 2, 1, 3) for t in (q, k, v)]
    kblk = k.reshape(B, H, nblk, L, HEAD_DIM_2)
    vblk = v.reshape(B, H, nblk, L, HEAD_DIM_2)
    kmean = jnp.mean(kblk.astype(jnp.float32), axis=3)
    gate = jnp.einsum('bhtd,bhnd->bhtn', q.astype(jnp.float32), kmean)
    qblk_id = jnp.arange(Sp) // L
    past = jnp.arange(nblk)[None, :] < qblk_id[:, None]
    gate = jnp.where(past, gate, NEG)
    K = min(MOBA_TOPK, nblk)
    _, sel = lax.top_k(gate, K)
    sel_valid = jnp.arange(K)[None, :] < qblk_id[:, None]

    C = MOBA_Q_CHUNK
    nch = Sp // C
    q_c = q.reshape(B, H, nch, C, HEAD_DIM_2).transpose(2, 0, 1, 3, 4)
    sel_c = sel.reshape(B, H, nch, C, K).transpose(2, 0, 1, 3, 4)
    valid_c = sel_valid.reshape(nch, C, K)
    qpos_c = jnp.arange(Sp).reshape(nch, C)
    bi = jnp.arange(B)[:, None, None, None]
    hi = jnp.arange(H)[None, :, None, None]
    sl = slopes.astype(jnp.float32)
    offs = jnp.arange(L)

    def chunk_fn(args):
        qc, selc, validc, qposc = args
        own = qposc[0] // L
        ksel = kblk[bi, hi, selc]
        vsel = vblk[bi, hi, selc]
        kown = lax.dynamic_index_in_dim(kblk, own, axis=2, keepdims=False)
        vown = lax.dynamic_index_in_dim(vblk, own, axis=2, keepdims=False)
        s_sel = jnp.einsum('bhcd,bhckld->bhckl', qc, ksel,
                           preferred_element_type=jnp.float32) * SCALE
        dist_sel = (qposc[None, None, :, None, None]
                    - (selc[..., None] * L + offs)).astype(jnp.float32)
        s_sel = s_sel - sl[None, :, None, None, None] * dist_sel
        s_sel = jnp.where(validc[None, None, :, :, None], s_sel, NEG)
        s_own = jnp.einsum('bhcd,bhld->bhcl', qc, kown,
                           preferred_element_type=jnp.float32) * SCALE
        dist_own = qposc[:, None] - (own * L + offs)[None, :]
        s_own = s_own - sl[None, :, None, None] * dist_own.astype(jnp.float32)[None, None]
        s_own = jnp.where((dist_own >= 0)[None, None], s_own, NEG)
        logits = jnp.concatenate([s_sel.reshape(B, H, C, K * L), s_own], axis=-1)
        p = jax.nn.softmax(logits, axis=-1).astype(v.dtype)
        p_sel = p[..., :K * L].reshape(B, H, C, K, L)
        p_own = p[..., K * L:]
        return (jnp.einsum('bhckl,bhckld->bhcd', p_sel, vsel)
                + jnp.einsum('bhcl,bhld->bhcd', p_own, vown))

    o = lax.map(chunk_fn, (q_c, sel_c, valid_c, qpos_c))
    o = o.transpose(1, 0, 3, 2, 4).reshape(B, Sp, H * HEAD_DIM_2)
    return o[:, :S]

def forgetting_attn(q, k, v, f_logit):
    B, S, H, _ = q.shape
    logf = jax.nn.log_sigmoid(f_logit.astype(jnp.float32))
    c = jnp.cumsum(logf, axis=1)
    cT = c.transpose(0, 2, 1)
    Q = FOX_Q_BLOCK
    nb = S // Q
    qb = q.reshape(B, nb, Q, H, HEAD_DIM_2).transpose(1, 0, 2, 3, 4)
    cb = c.reshape(B, nb, Q, H).transpose(1, 0, 3, 2)
    kpos = jnp.arange(S)

    def block_fn(args):
        qblk, cblk, n = args
        s = jnp.einsum('bqhd,bshd->bhqs', qblk, k,
                       preferred_element_type=jnp.float32) * SCALE
        s = s + cblk[..., None] - cT[:, :, None, :]
        qpos = n * Q + jnp.arange(Q)
        s = jnp.where((kpos[None, :] <= qpos[:, None])[None, None], s, NEG)
        p = jax.nn.softmax(s, axis=-1).astype(v.dtype)
        return jnp.einsum('bhqs,bshd->bqhd', p, v)

    o = lax.map(block_fn, (qb, cb, jnp.arange(nb)))
    return o.transpose(1, 0, 2, 3, 4).reshape(B, S, H * HEAD_DIM_2)

def head_rms(t, g):
    tf = t.astype(jnp.float32)
    y = tf * lax.rsqrt(jnp.mean(tf * tf, axis=-1, keepdims=True) + EPS)
    return (y * g.astype(jnp.float32)).astype(t.dtype)

def memory_kv(mem, mem_norm_g, w_mem_kv, k_gain):
    hm = rms_norm_2(mem, mem_norm_g)
    mk, mv = jnp.split(hm @ w_mem_kv, 2, axis=-1)
    return head_rms(split_heads(mk, MEM_HEADS), k_gain), split_heads(mv, MEM_HEADS)

def memory_cross_attn(q, mk, mv):
    B, S = q.shape[0], q.shape[1]
    s = jnp.einsum('bshd,bmhd->bhsm', q, mk, preferred_element_type=jnp.float32) * SCALE
    p = jax.nn.softmax(s, axis=-1).astype(mv.dtype)
    return jnp.einsum('bhsm,bmhd->bshd', p, mv).reshape(B, S, MEM_HEADS * HEAD_DIM_2)

def even_layer(x, mem, norm_g, w_in, qk_g, sinks, mem_norm_g, w_mem_kv, w_out):
    h = rms_norm_2(x, norm_g)
    aq, ak, av, bq, bk, bv, mq, z = split_cols(h @ w_in, EVEN_SPLIT)
    aq = head_rms(split_heads(aq, A_Q_HEADS), qk_g[0])
    ak = head_rms(split_heads(ak, A_KV_HEADS), qk_g[1])
    av = split_heads(av, A_KV_HEADS)
    bq = head_rms(split_heads(bq, B_HEADS), qk_g[2])
    bk = head_rms(split_heads(bk, B_HEADS), qk_g[3])
    bv = split_heads(bv, B_HEADS)
    mq = head_rms(split_heads(mq, MEM_HEADS), qk_g[4])
    mk, mv = memory_kv(mem, mem_norm_g, w_mem_kv, qk_g[5])
    slopes = alibi_slopes()
    ya = sliding_window_sink_attn(aq, ak, av, sinks, slopes[:A_Q_HEADS])
    yb = moba_attn(bq, bk, bv, slopes[A_Q_HEADS:])
    ym = memory_cross_attn(mq, mk, mv)
    y = jnp.concatenate([ya, yb, ym], axis=-1) * jax.nn.silu(z)
    return x + y @ w_out

def odd_layer(x, mem, norm_g, w_in, qk_g, b_f, mem_norm_g, w_mem_kv, w_out):
    h = rms_norm_2(x, norm_g)
    cq, ck, cv, cf, mq, z = split_cols(h @ w_in, ODD_SPLIT)
    cq = head_rms(split_heads(cq, C_HEADS), qk_g[0])
    ck = head_rms(split_heads(ck, C_HEADS), qk_g[1])
    cv = split_heads(cv, C_HEADS)
    mq = head_rms(split_heads(mq, MEM_HEADS), qk_g[2])
    mk, mv = memory_kv(mem, mem_norm_g, w_mem_kv, qk_g[3])
    yc = forgetting_attn(cq, ck, cv, cf + b_f)
    ym = memory_cross_attn(mq, mk, mv)
    y = jnp.concatenate([yc, ym], axis=-1) * jax.nn.silu(z)
    return x + y @ w_out

def second_inputs(seed: int = 0) -> dict:
    key = jax.random.key(seed)
    ks = jax.random.split(key, 18)
    NE = (DEPTH_2 + 1) // 2
    NO = DEPTH_2 // 2
    D = D_MODEL
    f32 = jnp.float32

    def w(k, shape, fan_in):
        return jax.random.normal(k, shape, f32) * fan_in ** -0.5

    def gain(k, shape):
        return 1.0 + 0.02 * jax.random.normal(k, shape, f32)

    return {
        'x': jax.random.normal(ks[0], (BATCH, SEQ, D), f32),
        'mem': jax.random.normal(ks[1], (BATCH, MEM_LEN, D), f32),
        'e_norm': gain(ks[2], (NE, D)),
        'e_w_in': w(ks[3], (NE, D, EVEN_IN), D),
        'e_qk_norm': gain(ks[4], (NE, 6, HEAD_DIM_2)),
        'e_sinks': 0.5 * jax.random.normal(ks[5], (NE, A_Q_HEADS), f32),
        'e_mem_norm': gain(ks[6], (NE, D)),
        'e_w_mem_kv': w(ks[7], (NE, D, 2 * MEM_HEADS * HEAD_DIM_2), D),
        'e_w_out': w(ks[8], (NE, EVEN_MIX, D), EVEN_MIX),
        'o_norm': gain(ks[9], (NO, D)),
        'o_w_in': w(ks[10], (NO, D, ODD_IN), D),
        'o_qk_norm': gain(ks[11], (NO, 4, HEAD_DIM_2)),
        'o_b_f': jax.random.uniform(ks[12], (NO, C_HEADS), f32, 1.0, 3.0),
        'o_mem_norm': gain(ks[13], (NO, D)),
        'o_w_mem_kv': w(ks[14], (NO, D, 2 * MEM_HEADS * HEAD_DIM_2), D),
        'o_w_out': w(ks[15], (NO, ODD_MIX, D), ODD_MIX),
    }

def second_block(x, mem, e_norm, e_w_in, e_qk_norm, e_sinks, e_mem_norm, e_w_mem_kv, e_w_out,
              o_norm, o_w_in, o_qk_norm, o_b_f, o_mem_norm, o_w_mem_kv, o_w_out):
    for layer in range(DEPTH_2):
        i = layer // 2
        if layer % 2 == 0:
            x = even_layer(x, mem, e_norm[i], e_w_in[i], e_qk_norm[i], e_sinks[i],
                           e_mem_norm[i], e_w_mem_kv[i], e_w_out[i])
        else:
            x = odd_layer(x, mem, o_norm[i], o_w_in[i], o_qk_norm[i], o_b_f[i],
                          o_mem_norm[i], o_w_mem_kv[i], o_w_out[i])
    return x


def setup_inputs(seed=0):
    out = dict(first_inputs(seed))
    for name, value in second_inputs(seed + 1).items():
        if name != "x":
            out[name + "_2"] = value
    return out


def reference(
    x, norm_pre_g, w_in, conv_qk_w, conv_qk_b, b_igate, b_fgate, pool_mix_w, pool_scale,
    mlstm_norm_g, w_proj_pool, w_proj_mlstm, b_merge, w_out, norm_post_g, mem_2, e_norm_2,
    e_w_in_2, e_qk_norm_2, e_sinks_2, e_mem_norm_2, e_w_mem_kv_2, e_w_out_2, o_norm_2, o_w_in_2,
    o_qk_norm_2, o_b_f_2, o_mem_norm_2, o_w_mem_kv_2, o_w_out_2,
):
    x = first_block(
        x, norm_pre_g, w_in, conv_qk_w, conv_qk_b, b_igate, b_fgate, pool_mix_w, pool_scale,
        mlstm_norm_g, w_proj_pool, w_proj_mlstm, b_merge, w_out, norm_post_g,
    )
    return second_block(
        x, mem_2, e_norm_2, e_w_in_2, e_qk_norm_2, e_sinks_2, e_mem_norm_2, e_w_mem_kv_2,
        e_w_out_2, o_norm_2, o_w_in_2, o_qk_norm_2, o_b_f_2, o_mem_norm_2, o_w_mem_kv_2,
        o_w_out_2,
    )


_drawn_inputs = setup_inputs


def setup_inputs(seed=0):
    import zlib

    import numpy as np

    out = dict(_drawn_inputs(seed))
    spreads = {}
    factors = {'conv_qk_b': 8.0,
     'b_igate': 8.0,
     'e_norm_2': 8.0,
     'e_qk_norm_2': 8.0,
     'e_sinks_2': 5.937,
     'e_mem_norm_2': 8.0,
     'o_norm_2': 8.0,
     'o_qk_norm_2': 8.0,
     'o_mem_norm_2': 8.0}
    for name, (base, spread) in spreads.items():
        noise = np.random.default_rng([zlib.crc32(name.encode()), seed]).standard_normal(out[name].shape)
        drawn = base * np.exp(spread * noise) if base else spread * noise
        out[name] = __import__('jax').numpy.asarray(drawn.astype(out[name].dtype))
    for name, factor in factors.items():
        out[name] = (out[name] * factor).astype(out[name].dtype)
    return out
```

```python
from collections import namedtuple
from contextlib import ExitStack

import numpy as np
import concourse.bass as bass
from concourse import mybir

F32 = mybir.dt.float32
F32R = mybir.dt.float32r
ACT = mybir.ActivationFunctionType
ALU = mybir.AluOpType
AX = mybir.AxisListType

P = 128
D = 1024
KT = D // P
S = 512
TT = S // P
UC = 256
SLOT = KT * UC
EPS = 1e-6
BIG = 1e30
FLOOR = -3e38

HEADS, HD = 4, 256
WINDOWS = (2, 4, 8, 16)
TAPS = 5
PAD = max(WINDOWS) // 2
UW = S + 2 * PAD
CW = S + TAPS - 1
VW = HD + 1
COL_U, COL_ZA, COL_QK, COL_V, COL_O, COL_ZB, COL_GATES, COL_GA, COL_GB = (
    0, D, 2 * D, 4 * D, 5 * D, 6 * D, 7 * D, 7 * D + 16, 8 * D + 16)

HD2 = 64
WIN = 128
MEM = 256
MT = MEM // P
A_HEADS, B_HEADS, C_HEADS, M_HEADS = 6, 6, 12, 4
SLOPES = [2.0 ** (-8.0 * (h + 1) / (A_HEADS + B_HEADS)) for h in range(A_HEADS + B_HEADS)]

_widths = [("pre_g", KT), ("conv_w", 16 * TAPS), ("conv_b", 16), ("pool_scale", KT), ("mlstm_g", KT),
           ("b_merge", 2 * KT), ("e_norm", KT), ("e_mem", KT), ("o_norm", KT), ("o_mem", KT),
           ("e_qk", 6), ("o_qk", 4), ("b_i", 1), ("b_f", 1), ("sinks", A_HEADS), ("o_bf", 1),
           ("eps", 1), ("edge", 2 * PAD * len(WINDOWS))]
VC = {}
_at = 0
for _name, _w in _widths:
    VC[_name] = _at
    _at += _w
NVEC = 256
assert _at <= NVEC


E_COLS = tuple(int(c) for c in np.cumsum([0, A_HEADS * HD2, 2 * HD2, 2 * HD2, B_HEADS * HD2, B_HEADS * HD2,
                                          B_HEADS * HD2, M_HEADS * HD2]))
O_COLS = tuple(int(c) for c in np.cumsum([0, C_HEADS * HD2, C_HEADS * HD2, C_HEADS * HD2, C_HEADS, M_HEADS * HD2]))
Job = namedtuple("Job", "t k0 keys q k bias v sink col")
QK_GAINS = ([0, 0, 0, 1, 2, 2, 2, 3, 3, 3, 4, 4], [0] * 6 + [1] * 6 + [2] * 2)


def shape_constants():
    p = np.arange(P)[:, None]
    c = np.arange(S)[None, :]
    ident = np.eye(P)
    bones = (p // HD2 == np.arange(P)[None, :] // HD2) * 1.0
    fwd = np.where(c >= p, 0.0, BIG)
    bwd = np.where(c - (S - P) <= p, 0.0, BIG)
    dist = np.where(c - (S - P) <= p, c - (S - P) - p, -BIG)
    causal = np.where(c - (S - P) <= p, 0.0, -BIG)
    w = np.arange(2 * WIN)[None, :]
    back = WIN + p - w
    window = np.where((back >= 0) & (back < WIN), -back, -BIG)
    return np.concatenate([ident, bones, fwd, bwd, dist, causal, window], axis=1).astype(np.float32)


def edge_constants():
    out = []
    for w in WINDOWS:
        for t0 in (0, S - PAD):
            for t in range(t0, t0 + PAD):
                lo, hi = max(t - w // 2, 0), min(t + w - 1 - w // 2, S - 1)
                out.append(w / (hi - lo + 1))
    return np.array(out, np.float32)


class Steps:

    def __init__(self, eng, sem):
        self.eng, self.sem, self.n, self.it, self.per = eng, sem, 0, None, 0

    def __call__(self, ins):
        ins.then_inc(self.sem, 1)
        self.n += 1
        self.eng.wait_ge(self.sem, self.n if self.it is None else self.it * self.per + self.n)

    def loop(self, count, per, body):
        n0 = self.n
        with self.eng.Fori(0, count) as i:
            self.it, self.per = i, per
            body(i)
        assert self.n == n0 + per
        self.n, self.it = n0 + per * count, None


def hybrid_block_then_two_attention_layers(nc, A, vecs_d, consts_d, out):
    stack = ExitStack()
    with stack:
        base = (nc.sbuf_base + 63) // 64 * 64
        K = 1024

        def at(name, shape, offset, dt=F32):
            return nc.alloc_sbuf_tensor_at(name, shape, dt, offset=base + offset)

        def sem(name):
            return stack.enter_context(nc.semaphore(name))

        HT, OP, RAW, WHI, WLO, R0, R1, R2, R3, R4, CST = (
            0, 32 * K, 64 * K, 80 * K, 96 * K, 112 * K, 128 * K, 144 * K, 160 * K, 177 * K, 193 * K)
        ht_hi = at("ht_hi", [P, KT, S], HT, F32R)
        ht_lo = at("ht_lo", [P, KT, S], HT + 16 * K, F32R)
        op_hi = at("op_hi", [P, KT, S], OP, F32R)
        op_lo = at("op_lo", [P, KT, S], OP + 16 * K, F32R)
        raw = at("raw", [P, 2, SLOT], RAW)
        whi = at("whi", [P, 2, SLOT], WHI, F32R)
        wlo = at("wlo", [P, 2, SLOT], WLO, F32R)

        ident = at("ident", [P, P], CST)
        bones = at("bones", [P, P], CST + 512)
        vecs = at("vecs", [P, NVEC], CST + K)
        masks1 = at("masks1", [P, 2, S], CST + 2 * K)
        masks2 = at("masks2", [P, 2 * S + 2 * WIN], CST + 2 * K)
        rowmax = at("rowmax", [64, S], CST + 7 * K)
        negc = at("negc", [P, S], CST + 7 * K)
        mkT = at("mkT", [P, 2, MEM], CST + 9 * K)
        mv = at("mv", [P, MT, MEM], CST + 11 * K)
        stats = at("stats", [P, 6, 64], CST + 13 * K)
        gcol = at("gcol", [P, TT, 2, HEADS], CST + 14 * K + 512)
        floorc = at("floorc", [P, TT, 2, HEADS], CST + 14 * K + 640)
        small = at("small", [P, 24], CST + 14 * K + 768)

        xrow = at("xrow", [P, TT, D], R4)
        xnrow = at("xnrow", [P, TT, D], R0)
        zaT = at("zaT", [P, KT, S], R0)
        uT = at("uT", [P, KT, UW], R1)
        win_s = at("win_s", [P, 2, UW], R3)
        win_t = at("win_t", [P, 4, S], R3 + 5 * K)
        grow = at("grow", [P, 7, S], R2 + 2 * K)
        mergedT = at("mergedT", [P, KT, S], R4)
        cpad = at("cpad", [P, 4, CW + 12], OP)
        cacc = at("cacc", [P, 4, S], OP + 10 * K)
        qkT = at("qkT", [P, 2 * KT, S], R1)
        vrow = at("vrow", [P, TT, HEADS * VW], R3)
        ogT = at("ogT", [P, KT, S], R0)
        decay = at("decay", [P, 4, S], OP)
        prob = at("prob", [P, 2, TT, S], OP + 8 * K)
        hrow = at("hrow", [P, TT, HD], OP + 24 * K)
        hfwd = at("hfwd", [P, 2, HD], OP + 28 * K)
        hsq = at("hsq", [P, HD], OP + 30 * K)
        gbT = at("gbT", [P, KT, S], R2)
        orow1 = at("orow1", [P, TT, D], R0)
        xagain = at("xagain", [P, TT, D], R1)
        gpost = at("gpost", [P, D], R2)
        junk = at("junk", [P, D], R2 + 4 * K)
        memrow = at("memrow", [P, MT, D], R3)
        memn = at("memn", [P, MT, D], R3 + 8 * K)
        memT_hi = at("memT_hi", [P, KT, MEM], OP, F32R)
        memT_lo = at("memT_lo", [P, KT, MEM], OP + 8 * K, F32R)
        hn_sq = at("hn_sq", [P, 2, S], OP + 16 * K)
        hn_rs = at("hn_rs", [P, 2, S], OP + 20 * K)
        zT = at("zT", [P, KT, S], R0)
        frow = at("frow", [P, 3, S], R0)
        arow = at("arow", [P, TT, D], HT)
        sc = at("sc", [P, 3, S], HT + 16 * K)
        pr = at("pr", [P, 3, S], HT + 22 * K)
        prT = at("prT", [P, 2, S], HT + 28 * K)
        bias_h = at("bias_h", [P, 2, S], R3)
        LAYERS = []
        for name, ntile, vcols, voff in (("e", 12, 512, 24 * K), ("o", 14, 768, 28 * K)):
            LAYERS.append((at("qk_" + name, [P, ntile, S], R1), at("v_" + name, [P, TT, vcols], R1 + voff)))

        acc = stack.enter_context(nc.psum_tensor("acc", [P, 4, S], F32))
        aux = stack.enter_context(nc.psum_tensor("aux", [P, 4, S], F32))

        def V(name, j=0, n=1):
            return vecs[:, VC[name] + j:VC[name] + j + n]

        def Vd(name, j):
            return vecs[:, bass.ds(j + VC[name], 1)]

        consts_in = sem("consts_in")
        x_in = sem("x_in")
        w_loaded = [sem("w_loaded_0"), sem("w_loaded_1")]
        w_hi = sem("w_hi")
        w_split = sem("w_split")
        acc_ready = sem("acc_ready")
        acc_free = sem("acc_evacuated")
        pool_step = sem("pool_step")
        units_begun = sem("units_begun")
        act_step = sem("act_step")
        dve_step = sem("dve_step")
        rssq_ready = sem("rssq_ready")
        rvar_ready = sem("rvar_ready")
        rsd_ready = sem("rsd_ready")
        xn_ready = sem("xn_ready")
        tr_ready = sem("tr_ready")
        tr_hi = sem("tr_hi")
        tr_lo = sem("tr_lo")
        t_ready = sem("t_ready")
        hi_ready = sem("hi_ready")
        lo_ready = sem("lo_ready")
        conv_ready = sem("conv_ready")
        silu_ready = sem("silu_ready")
        gate_rows = sem("gate_rows")
        gate_exp = sem("gate_exp")
        gm_ready = sem("gm_ready")
        gmT_ready = sem("gmT_ready")
        gcol_ready = sem("gcol_ready")
        floor_ready = sem("floor_ready")
        mbc_ready = sem("mbc_ready")
        s_ready = sem("s_ready")
        arg_ready = sem("arg_ready")
        d_ready = sem("d_ready")
        p_ready = sem("p_ready")
        pv_ready = sem("pv_ready")
        den_ready = sem("den_ready")
        rden_ready = sem("rden_ready")
        hf_ready = sem("hf_ready")
        hb_ready = sem("hb_ready")
        hssq_ready = sem("hssq_ready")
        hrs_ready = sem("hrs_ready")
        hbn_ready = sem("hbn_ready")
        hT_ready = sem("hT_ready")
        zb_ready = sem("zb_ready")
        post_in = sem("post_in")
        post_ssq = sem("post_ssq")
        post_var = sem("post_var")
        post_sd = sem("post_sd")
        mem_in = sem("mem_in")
        sq_ready = sem("sq_ready")
        ssq_ready = sem("ssq_ready")
        ln_done = sem("ln_done")
        rs_ready = sem("rs_ready")
        hn_done = sem("hn_done")
        negc_ready = sem("negc_ready")
        sc_ready = sem("sc_ready")
        nm_ready = sem("nm_ready")
        es_ready = sem("es_ready")
        pr_ready = sem("pr_ready")
        prT_ready = sem("prT_ready")
        prT_copied = sem("prT_copied")
        ri_ready = sem("ri_ready")
        o_ready = sem("o_ready")
        o_done = sem("o_done")
        arow_T = sem("arow_T")
        x_rows = sem("x_rows")
        logit_ready = sem("logit_ready")
        stored = sem("stored")
        masks2_in = sem("masks2_in")

        block = stack.enter_context(nc.Block())

        plan = {}
        n_, a_ = 0, 0
        for name, units, accs in (("gates", 1, 1), ("u", 4, 4), ("za", 4, 4), ("mix", 1, 4), ("ga", 4, 4), ("pa", 4, 4),
                                  ("qk", 8, 8), ("v", 4, 4), ("ozb", 8, 8), ("gb", 4, 4), ("pb", 4, 4),
                                  ("wout", 4, 4), ("e_mem", 2, 2), ("e_qk", 6, 6), ("e_v", 2, 2),
                                  ("e_z", 4, 4), ("e_out", 4, 4), ("o_mem", 2, 2), ("o_f", 1, 1),
                                  ("o_qk", 7, 7), ("o_v", 3, 3), ("o_z", 4, 4), ("o_out", 4, 4)):
            plan[name] = (n_, a_, units)
            n_ += units
            a_ += accs
        UNITS = n_

        def pairs(eng, units, body, peel=0):
            for i in range(min(peel, units // 2)):
                body(2 * i, 0)
                body(2 * i + 1, 1)
            if units // 2 > peel:
                with eng.Fori(peel, units // 2) as i:
                    body(2 * i, 0)
                    body(2 * i + 1, 1)
            if units % 2:
                body(units - 1, 0)

        last_a = a_

        def wview(w):
            return w.rearrange("(k p) n -> p k n", p=P)

        W1 = wview(A["w_in"][0])
        E_IN, O_IN = wview(A["e_w_in_2"][0]), wview(A["o_w_in_2"][0])
        raw3 = raw[:, :, :].rearrange("p s (k c) -> p s k c", k=KT)

        def logit_bank(i):
            return acc[:, i % 3, :]

        def trans_bank(i):
            return acc[:, 3, :] if i % 2 == 0 else aux[:, 0, :]

        def out_bank(i):
            return aux[:, 1 + i % 3, :]

        JOBS = [[], []]
        for h in range(A_HEADS):
            kv = h // (A_HEADS // 2)
            for t in range(TT):
                k0 = max(t - 1, 0)
                keys = P * (t + 1 - k0)
                JOBS[0].append(Job(t, k0, keys, (h % 3, HD2 * kv), (3, HD2 * kv), ("window", h, SLOPES[h]),
                                   HD2 * kv, h, HD2 * h))
        for h in range(B_HEADS):
            for t in range(TT):
                JOBS[0].append(Job(t, 0, P * (t + 1), (4 + h // 2, HD2 * (h % 2)), (7 + h // 2, HD2 * (h % 2)),
                                   ("dist", A_HEADS + h, SLOPES[A_HEADS + h]), P + HD2 * h, None, HD2 * (A_HEADS + h)))
        for h in range(C_HEADS):
            for t in range(TT):
                JOBS[1].append(Job(t, 0, P * (t + 1), (h // 2, HD2 * (h % 2)), (6 + h // 2, HD2 * (h % 2)),
                                   ("forget", h, 1.0), HD2 * h, None, HD2 * h))
        for L, q0 in enumerate((10, 12)):
            for h in range(M_HEADS):
                for t in range(TT):
                    JOBS[L].append(Job(t, 0, MEM, (q0 + h // 2, HD2 * (h % 2)), (h // 2, HD2 * (h % 2)), None,
                                       HD2 * h, None, HD2 * (C_HEADS + h)))

        @block.sync
        def _(sp):
            def slot_free(n):
                if isinstance(n, int) and n < 2:
                    return
                sp.wait_ge(w_split, n - 1)

            def load(view, col, n, slot):
                slot_free(n)
                for kh in range(2):
                    sp.dma_start(raw3[:, slot, 4 * kh:4 * kh + 4, :],
                                 view[:, 4 * kh:4 * kh + 4, bass.ds(col, UC)]).then_inc(w_loaded[slot], 16)

            def stage(name, view, col0, step=UC, peel=0):
                n0, _, units = plan[name]
                pairs(sp, units, lambda u, q: load(view, u * step + col0, u + n0, (n0 + q) % 2), peel)

            def halves(n, view, cols):
                slot_free(n)
                for half, col in enumerate(cols):
                    dst = raw3[:, n % 2, :, P * half:P * half + P]
                    if isinstance(col, tuple):
                        for part, c in enumerate(col):
                            sp.dma_start(dst[:, :, HD2 * part:HD2 * part + HD2],
                                         view[:, :, c:c + HD2]).then_inc(w_loaded[n % 2], 16)
                    else:
                        sp.dma_start(dst, view[:, :, col:col + P]).then_inc(w_loaded[n % 2], 16)

            def narrow(n, view, col, width):
                slot_free(n)
                dst = raw[:, n % 2, 0:KT * width].rearrange("p (k c) -> p k c", k=KT)
                for kh in range(2):
                    sp.dma_start(dst[:, 4 * kh:4 * kh + 4, :],
                                 view[:, 4 * kh:4 * kh + 4, col:col + width]).then_inc(w_loaded[n % 2], 16)

            narrow(0, W1, COL_GATES, 16)
            stage("u", W1, COL_U, peel=1)
            stage("za", W1, COL_ZA)
            n = plan["mix"][0]
            slot_free(n)
            mixw = A["pool_mix_w"][0].rearrange("g (kk p) n -> p (g kk) n", p=P)
            for kh in range(2):
                sp.dma_start(raw3[:, n % 2, 4 * kh:4 * kh + 4, :], mixw[:, 4 * kh:4 * kh + 4, :]).then_inc(w_loaded[n % 2], 16)
            stage("ga", W1, COL_GA)
            stage("pa", wview(A["w_proj_pool"][0]), 0)
            stage("qk", W1, COL_QK)
            stage("v", W1, COL_V)
            n = plan["ozb"][0]
            with sp.Fori(0, HEADS) as h:
                load(W1, h * UC + COL_O, 2 * h + n, n % 2)
                load(W1, h * UC + COL_ZB, 2 * h + n + 1, (n + 1) % 2)
            stage("gb", W1, COL_GB)
            stage("pb", wview(A["w_proj_mlstm"][0]), 0)
            stage("wout", wview(A["w_out"][0]), 0)

            stage("e_mem", wview(A["e_w_mem_kv_2"][0]), 0)
            n = plan["e_qk"][0]
            AQ, AK, AV, BQ, BK, BV, MQ, Z = E_COLS
            tiles = [(AQ + HD2 * j, AQ + HD2 * (j + 3)) for j in range(3)] + [AK]
            tiles += [BQ + P * j for j in range(3)] + [BK + P * j for j in range(3)] + [MQ, MQ + P]
            for u in range(6):
                halves(n + u, E_IN, tiles[2 * u:2 * u + 2])
            halves(plan["e_v"][0], E_IN, [AV, BV])
            halves(plan["e_v"][0] + 1, E_IN, [BV + P, BV + 2 * P])
            stage("e_z", E_IN, Z)
            stage("e_out", wview(A["e_w_out_2"][0]), 0)

            stage("o_mem", wview(A["o_w_mem_kv_2"][0]), 0)
            CQ, CK, CV, CF, MQ, Z = O_COLS
            narrow(plan["o_f"][0], O_IN, CF, C_HEADS)
            n = plan["o_qk"][0]
            for u in range(6):
                load(O_IN, CQ + UC * u, n + u, (n + u) % 2)
            load(O_IN, MQ, n + 6, (n + 6) % 2)
            n0 = plan["o_v"][0]
            for u in range(3):
                load(O_IN, CV + UC * u, n0 + u, (n0 + u) % 2)
            stage("o_z", O_IN, Z)
            stage("o_out", wview(A["o_w_out_2"][0]), 0)

            outv = out[0].rearrange("(t p) d -> p t d", p=P)
            for u in range(4):
                sp.wait_ge(acc_free, plan["o_out"][1] + u + 1)
                sp.dma_start(outv[:, :, UC * u:UC * u + UC], xrow[:, :, UC * u:UC * u + UC]).then_inc(stored, 16)
            sp.wait_ge(stored, 64)

        @block.gpsimd
        def _(pool):
            step = Steps(pool, pool_step)

            def split(n, slot, round_, a_before, extra=0):
                pool.wait_ge(w_loaded[slot], round_ * 32 + 32 + extra)
                if a_before is not None:
                    pool.wait_ge(acc_ready, a_before * 2 + 2)
                pool.sem_inc(units_begun, 1)
                nc.gpsimd.tensor_scalar(whi[:, slot, :], raw[:, slot, :], 1.0, 1.0, ALU.mult, ALU.mult).then_inc(w_hi, 1)
                pool.wait_ge(w_hi, n + 1)
                nc.gpsimd.tensor_tensor(wlo[:, slot, :], raw[:, slot, :], whi[:, slot, :].bitcast(F32),
                                        ALU.subtract).then_inc(w_split, 1)

            def split_narrow(n, a_before, width, groups, extra=0):
                slot = n % 2
                pool.wait_ge(w_loaded[slot], 32 * (n // 2 + 1) + extra)
                if a_before is not None:
                    pool.wait_ge(acc_ready, 2 * (a_before + 1))
                nc.gpsimd.memset(whi[:, slot, 0:KT * P].bitcast(F32), 0.0)
                step(nc.gpsimd.memset(wlo[:, slot, 0:KT * P].bitcast(F32), 0.0))
                src = raw[:, slot, 0:KT * width].rearrange("p (k c) -> p k c", k=KT)
                hi = whi[:, slot, 0:KT * P].rearrange("p (k c) -> p k c", k=KT)
                lo = wlo[:, slot, 0:KT * P].rearrange("p (k c) -> p k c", k=KT)
                for g, (c, d, w) in enumerate(groups):
                    ins = nc.gpsimd.tensor_copy(hi[:, :, d:d + w], src[:, :, c:c + w])
                    if g == len(groups) - 1:
                        ins.then_inc(w_hi, 1)
                pool.wait_ge(w_hi, n + 1)
                for g, (c, d, w) in enumerate(groups):
                    ins = nc.gpsimd.tensor_tensor(lo[:, :, d:d + w], src[:, :, c:c + w],
                                                  hi[:, :, d:d + w].bitcast(F32), ALU.subtract)
                    if g == len(groups) - 1:
                        ins.then_inc(w_split, 1)

            split_narrow(0, None, 16, [(8 * d + 4 * kind, 64 * kind + 32 * d, 4) for d in range(2) for kind in range(2)])
            mix = plan["mix"][0]
            split(1, 1, 0, None)
            split(2, 0, 1, 0)
            with pool.Fori(0, (mix - 3) // 2) as i:
                split(2 * i + 3, 1, i + 1, 2 * i + 1)
                split(2 * i + 4, 0, i + 2, 2 * i + 2)
            assert mix % 2
            for n in (mix, mix + 1):
                split(n, n % 2, n // 2, n - 2)

            def run(lo, hi, extra):
                def one(i, d):
                    split(2 * i + lo + d, (lo + d) % 2, i + (lo + d) // 2, 2 * i + lo + d + 1, extra[(lo + d) % 2])
                if (hi - lo) // 2:
                    with pool.Fori(0, (hi - lo) // 2) as i:
                        one(i, 0)
                        one(i, 1)
                if (hi - lo) % 2:
                    one((hi - lo) // 2, 0)
            eqk, n = plan["e_qk"][0], plan["o_f"][0]
            assert eqk % 2 == 0
            run(mix + 2, eqk, (0, 0))
            run(eqk, eqk + 1, (32, 0))
            run(eqk + 1, n, (32, 16))
            split_narrow(n, n + 1, C_HEADS, [(0, 0, C_HEADS)], (32, 16)[n % 2])
            run(n + 1, UNITS, (32, 16))

        @block.scalar
        def _(act):
            step = Steps(act, act_step)
            xv = A["x"][0].rearrange("(t p) d -> p t d", p=P)
            for t in range(TT):
                act.dma_start(xrow[:, t, :], xv[:, t, :]).then_inc(x_in, 16)
            act.dma_start(vecs[:], vecs_d).then_inc(consts_in, 16)
            act.dma_start(ident[:], consts_d[:, 0:P]).then_inc(consts_in, 16)
            act.dma_start(bones[:], consts_d[:, P:2 * P]).then_inc(consts_in, 16)
            act.dma_start(masks1[:], consts_d[:, 2 * P:2 * P + 2 * S].rearrange("p (a c) -> p a c", a=2)).then_inc(consts_in, 16)

            seen = {"rssq": 0, "rvar": 0, "tr": 0, "hi": 0, "hn": 0, "exp": 0}

            def squares(src, dst, tiles, col, wait=None):
                for t in range(tiles):
                    if wait:
                        wait(t)
                    nc.scalar.activation(dst[:, t, :], src[:, t, :], ACT.Square,
                                         accum_out=small[:, col + t:col + t + 1]).then_inc(rssq_ready, 1)
                seen["rvar"] += 1
                act.wait_ge(rvar_ready, seen["rvar"])
                nc.scalar.activation(small[:, col:col + tiles], small[:, col:col + tiles], ACT.Sqrt).then_inc(rsd_ready, 1)

            def heads_of_transposes(gain, dst, cols):
                for k in range(KT):
                    seen["tr"] += 1
                    act.wait_ge(tr_ready, seen["tr"])
                    nc.scalar.activation(dst[:, k, :], aux[:, k % 4, 0:cols], ACT.Copy,
                                         scale=V(gain, k)).then_inc(tr_hi, 1)

            def head(src, dst):
                seen["hi"] += 1
                act.wait_ge(t_ready, seen["hi"])
                nc.scalar.activation(dst, src, ACT.Copy).then_inc(hi_ready, 1)

            def evac(a, s, half, dst, func, **kw):
                act.wait_ge(acc_ready, a * 2 + 1 + half)
                ins = nc.scalar.activation(dst, acc[:, 2 * s + half:2 * s + half + 1, :], func, **kw)
                if half:
                    ins.then_inc(acc_free, 1)

            def stage(name, dst, func, bias=None, peel=0):
                _, a0, units = plan[name]
                act.wait_ge(acc_free, a0)

                def body(u, q):
                    for half in range(2):
                        kw = {} if bias is None else {"bias": Vd(*bias, u * 2 + half)} if len(bias) == 1 else \
                            {"bias": Vd(bias[0], u * 2 + half + bias[1])}
                        evac(u + a0, (a0 + q) % 2, half, dst[:, bass.ds(u * 2 + half, 1), :], func, **kw)
                pairs(act, units, body, peel)

            squares(xrow, xnrow, TT, 0, lambda t: act.wait_ge(x_in, 16 * TT))
            act.wait_ge(consts_in, 64)
            heads_of_transposes("pre_g", ht_hi, S)

            def softplus_of_minus_abs(src, tmp):
                step(nc.scalar.activation(tmp, src, ACT.Abs))
                step(nc.scalar.activation(tmp, tmp, ACT.Exp, scale=-1.0))
                nc.scalar.activation(tmp, tmp, ACT.Ln, bias=1.0).then_inc(gate_exp, 1)
            act.wait_ge(gate_rows, 1)
            softplus_of_minus_abs(grow[0:64, 1, :], grow[0:64, 2, :])

            _, a0, units = plan["u"]
            act.wait_ge(acc_free, a0)
            for u in range(units):
                for half in range(2):
                    evac(a0 + u, (a0 + u) % 2, half, uT[:, 2 * u + half:2 * u + half + 1, PAD:PAD + S], ACT.Copy)
                if u:
                    for j in (2 * u - 2, 2 * u - 1):
                        head(win_t[:, j % 4, :], op_hi[:, j, :])
            for j in (2 * units - 2, 2 * units - 1):
                head(win_t[:, j % 4, :], op_hi[:, j, :])
            act.wait_ge(gmT_ready, 1)
            act.wait_ge(gcol_ready, 1)
            gmT = aux[:, 3, :].rearrange("p (t k d r) -> p t k d r", t=TT, k=2, d=2)
            for d in range(2):
                nc.scalar.activation(floorc[:, :, d, :], gmT[:, :, 1, d, 0:HEADS], ACT.Exp, scale=-1.0).then_inc(floor_ready, 1)

            stage("za", zaT, ACT.Silu)
            for j in range(KT):
                head(win_t[:, j % 4, :], op_hi[:, j, :])
            stage("ga", mergedT, ACT.Sigmoid, ("b_merge", 0))

            _, a0, units = plan["qk"]

            def qk_body(u, q, first=False):
                for half in range(2):
                    slot = 2 * q + half
                    if not first:
                        act.wait_ge(conv_ready, u * 2 + half - 3)
                    evac(u + a0, (a0 + q) % 2, half, cpad[:, slot:slot + 1, 2:2 + S], ACT.Copy)

            def qk_silu(u, q):
                for half in range(2):
                    slot = 2 * q + half
                    act.wait_ge(conv_ready, u * 2 + half + 1)
                    nc.scalar.activation(qkT[:, bass.ds(u * 2 + half, 1), :], cacc[:, slot:slot + 1, :], ACT.Silu,
                                         bias=Vd("conv_b", u * 2 + half)).then_inc(silu_ready, 1)
            act.wait_ge(lo_ready, 16)
            act.wait_ge(acc_free, a0)
            qk_body(0, 0, True)
            qk_body(1, 1, True)
            qk_silu(0, 0)
            with act.Fori(1, units // 2) as i:
                qk_body(2 * i, 0)
                qk_silu(2 * i - 1, 1)
                qk_body(2 * i + 1, 1)
                qk_silu(2 * i, 0)
            qk_silu(units - 1, 1)

            _, a0, units = plan["v"]

            def v_body(u, q):
                s = (a0 + q) % 2
                for half in range(2):
                    act.wait_ge(acc_ready, u * 2 + 2 * a0 + 1 + half)
                    ins = nc.scalar.activation(vrow[:, 2 * half:2 * half + 2, bass.ds(u * VW, HD)],
                                               acc[:, 2 * s + half, :].rearrange("p (t c) -> p t c", t=2), ACT.Copy)
                    if half:
                        ins.then_inc(acc_free, 1)
            pairs(act, units, v_body)

            def decays():
                for j in range(TT):
                    for d in range(2):
                        n = seen["exp"]
                        seen["exp"] += 1
                        w = S - P * j if d == 0 else P * (j + 1)
                        act.wait_ge(arg_ready, n + 1)
                        tile = decay[:, n % 4, 0:w]
                        nc.scalar.activation(tile, tile, ACT.Exp, scale=-1.0).then_inc(d_ready, 1)

            _, a0, _ = plan["ozb"]
            decays()
            for h in range(HEADS):
                a = a0 + 2 * h
                act.wait_ge(acc_free, a)
                for half in range(2):
                    evac(a, a % 2, half, ogT[:, 2 * h + half:2 * h + half + 1, :], ACT.Sigmoid)
                for t in range(TT):
                    i = TT * h + t
                    b = 2 * (t % 2)
                    act.wait_ge(pv_ready, i + 1)
                    nc.scalar.activation(small[:, 16 + 2 * (t % 2):18 + 2 * (t % 2)], aux[:, b:b + 2, HD],
                                         ACT.Abs).then_inc(den_ready, 1)
                    act.wait_ge(rden_ready, i + 1)
                    nc.scalar.activation(hfwd[:, t % 2, :], aux[:, b, 0:HD], ACT.Copy,
                                         scale=small[:, 16 + 2 * (t % 2):17 + 2 * (t % 2)]).then_inc(hf_ready, 1)
                    act.wait_ge(hb_ready, i + 1)
                    nc.scalar.activation(hsq[:], hrow[:, t, :], ACT.Square,
                                         accum_out=small[:, t:t + 1]).then_inc(hssq_ready, 1)
                act.wait_ge(hssq_ready, TT * (h + 1))
                step(nc.scalar.activation(small[:, 4:8], small[:, 0:4], ACT.Ln, scale=1.0 / HD, bias=V("eps")))
                nc.scalar.activation(small[:, 8:12], small[:, 4:8], ACT.Exp, scale=-0.5).then_inc(hrs_ready, 1)
                if h + 1 < HEADS:
                    decays()
                a += 1
                for half in range(2):
                    act.wait_ge(acc_ready, 2 * a + 1 + half)
                    bank = acc[:, 2 * (a % 2) + half, :]
                    nc.scalar.activation(bank, bank, ACT.Silu).then_inc(zb_ready, 1)
            for j in range(KT):
                head(ogT[:, j, :], op_hi[:, j, :])
            stage("gb", gbT, ACT.Sigmoid, ("b_merge", KT))
            for j in range(KT):
                head(mergedT[:, j, :], ht_hi[:, j, :])

            act.dma_start(xagain[:], xv).then_inc(post_in, 16)
            act.dma_start(gpost[:], A["norm_post_g"][0:1, :].to_broadcast([P, D])).then_inc(post_in, 16)
            memv = A["mem_2"][0].rearrange("(t p) d -> p t d", p=P)
            act.dma_start(memrow[:], memv).then_inc(mem_in, 16)
            act.dma_start(masks2[:], consts_d[:, 2 * P + 2 * S:]).then_inc(masks2_in, 16)

            _, a0, units = plan["wout"]
            act.wait_ge(acc_free, a0)

            def wout_body(u, q):
                s = (a0 + q) % 2
                for half in range(2):
                    act.wait_ge(acc_ready, u * 2 + 2 * a0 + 1 + half)
                    ins = nc.scalar.activation(orow1[:, 2 * half:2 * half + 2, bass.ds(u * UC, UC)],
                                               acc[:, 2 * s + half, :].rearrange("p (t c) -> p t c", t=2), ACT.Copy)
                    if half:
                        ins.then_inc(acc_free, 1)
            pairs(act, units, wout_body)
            squares(memrow, memn, MT, 20, lambda t: act.wait_ge(mem_in, 16))
            act.wait_ge(acc_free, a0 + units)
            for t in range(TT):
                if t:
                    act.wait_ge(post_ssq, t)
                nc.scalar.activation(junk[:], orow1[:, t, :], ACT.Square,
                                     accum_out=small[:, t:t + 1]).then_inc(post_ssq, 1)
            act.wait_ge(post_var, 1)
            nc.scalar.activation(small[:, 0:4], small[:, 0:4], ACT.Sqrt).then_inc(post_sd, 1)

            def head_norm_squares(a, half, cols):
                n = seen["hn"] + half
                act.wait_ge(acc_ready, 2 * a + 1 + half)
                if n >= 2:
                    act.wait_ge(ssq_ready, n - 1)
                nc.scalar.activation(hn_sq[:, n % 2, 0:cols], acc[:, 2 * (a % 2) + half, 0:cols], ACT.Square).then_inc(sq_ready, 1)

            def head_norm_rsqrt(n, cols):
                act.wait_ge(ssq_ready, n + 1)
                if n >= 2:
                    act.wait_ge(hn_done, n - 1)
                nc.scalar.activation(hn_rs[:, n % 2, 0:cols], aux[:, n % 2, 0:cols], ACT.Ln, scale=1.0 / HD2,
                                     bias=V("eps")).then_inc(ln_done, 1)
                act.wait_ge(ln_done, n + 1)
                nc.scalar.activation(hn_rs[:, n % 2, 0:cols], hn_rs[:, n % 2, 0:cols], ACT.Exp, scale=-0.5).then_inc(rs_ready, 1)

            def value_rows(a, dst, tiles, u):
                act.wait_ge(acc_free, a)
                for half in range(2):
                    act.wait_ge(acc_ready, 2 * a + 1 + half)
                    src = acc[:, 2 * (a % 2) + half, :]
                    if tiles == TT:
                        ins = nc.scalar.activation(dst[:, 2 * half:2 * half + 2, UC * u:UC * u + UC],
                                                   src.rearrange("p (t c) -> p t c", t=2), ACT.Copy)
                    else:
                        ins = nc.scalar.activation(dst[:, half, :], src[:, 0:UC], ACT.Copy)
                    if half:
                        ins.then_inc(acc_free, 1)

            jobs_done = 0
            for L, name in enumerate("eo"):
                qk, vv = LAYERS[L]
                heads_of_transposes(name + "_mem", memT_hi, MEM)
                _, a0, _ = plan[name + "_mem"]
                for half in range(2):
                    head_norm_squares(a0, half, MEM)
                for half in range(2):
                    head_norm_rsqrt(seen["hn"] + half, MEM)
                seen["hn"] += 2
                value_rows(a0 + 1, mv, MT, 0)
                squares(xrow, xnrow, TT, 0, lambda t: act.wait_ge(*((x_rows, t + 1) if L == 0 else (acc_free, plan["e_out"][1] + 4))))
                heads_of_transposes(name + "_norm", ht_hi, S)
                if L:
                    act.wait_ge(gate_rows, 2)
                    softplus_of_minus_abs(frow[0:C_HEADS, 0, :], frow[0:C_HEADS, 1, :])
                _, a0, units = plan[name + "_qk"]
                for u in range(units):
                    for half in range(2):
                        head_norm_squares(a0 + u, half, S)
                    if u:
                        for n in (seen["hn"] - 2, seen["hn"] - 1):
                            head_norm_rsqrt(n, S)
                    seen["hn"] += 2
                _, a0, units = plan[name + "_v"]
                for u in range(units):
                    value_rows(a0 + u, vv, TT, u)
                    if u == 0:
                        for n in (seen["hn"] - 2, seen["hn"] - 1):
                            head_norm_rsqrt(n, S)
                stage(name + "_z", zT, ACT.Silu)

                jobs = JOBS[L]
                for i in range(len(jobs) + 3):
                    if i < len(jobs):
                        job = jobs[i]
                        g = jobs_done + i
                        act.wait_ge(nm_ready, g + 1)
                        src = logit_bank(i)[:, 0:job.keys] if job.bias is None else sc[:, i % 3, 0:job.keys]
                        if g >= 3:
                            act.wait_ge(prT_ready, g - 2)
                        nc.scalar.activation(pr[:, i % 3, 0:job.keys], src, ACT.Exp, bias=stats[:, 1, i:i + 1],
                                             accum_out=stats[:, 2, i:i + 1]).then_inc(pr_ready, 1)
                        if job.sink is not None:
                            nc.scalar.activation(stats[:, 3, i:i + 1], V("sinks", job.sink), ACT.Exp,
                                                 bias=stats[:, 1, i:i + 1]).then_inc(es_ready, 1)
                    if i >= 3:
                        k = i - 3
                        act.wait_ge(o_ready, jobs_done + k + 1)
                        act.wait_ge(ri_ready, jobs_done + k + 1)
                        nc.scalar.activation(arow[:, jobs[k].t, jobs[k].col:jobs[k].col + HD2], out_bank(k)[:, 0:HD2],
                                             ACT.Copy, scale=stats[:, 4, k:k + 1]).then_inc(o_done, 1)
                jobs_done += len(jobs)
                for j in range(KT):
                    head(zT[:, j, :], op_hi[:, j, :])
                if L == 0:
                    act.wait_ge(lo_ready, 48 - 8)
                    act.dma_start(memrow[:], memv).then_inc(mem_in, 16)
                    squares(memrow, memn, MT, 20, lambda t: act.wait_ge(mem_in, 32))

        @block.vector
        def _(dve):
            step = Steps(dve, dve_step)
            seen = {"rssq": 0, "rsd": 0, "tr": 0, "t": 0, "lo": 0, "hn": 0, "arg": 0, "aT": 0}
            v = nc.vector

            def normalise(src, dst, tiles, col):
                seen["rssq"] += tiles
                dve.wait_ge(rssq_ready, seen["rssq"])
                cols = small[:, col:col + tiles]
                v.tensor_scalar(cols, cols, 1.0 / D, EPS, ALU.mult, ALU.add).then_inc(rvar_ready, 1)
                seen["rsd"] += 1
                dve.wait_ge(rsd_ready, seen["rsd"])
                step(v.reciprocal(cols, cols))
                for t in range(tiles):
                    v.tensor_scalar(dst[:, t, :], src[:, t, :], small[:, col + t:col + t + 1], None,
                                    ALU.mult).then_inc(xn_ready, 1)

            def rests_of_transposes(gain, hi, lo, cols):
                for k in range(KT):
                    seen["tr"] += 1
                    dve.wait_ge(tr_hi, seen["tr"])
                    v.scalar_tensor_tensor(lo[:, k, :], aux[:, k % 4, 0:cols], V(gain, k),
                                           hi[:, k, :].bitcast(F32), ALU.mult, ALU.subtract).then_inc(tr_lo, 1)

            def rest(src, hi, lo):
                seen["lo"] += 1
                dve.wait_ge(hi_ready, seen["lo"])
                v.tensor_tensor(lo, src, hi.bitcast(F32), ALU.subtract).then_inc(lo_ready, 1)

            def tile_written(ins):
                ins.then_inc(t_ready, 1)
                seen["t"] += 1

            v.memset(uT[:, :, 0:PAD], 0.0)
            step(v.memset(uT[:, :, PAD + S:UW], 0.0))
            dve.wait_ge(consts_in, 64)
            for name, j in (("e_qk", 0), ("e_qk", 2), ("e_qk", 4), ("o_qk", 0), ("o_qk", 2)):
                step(v.tensor_scalar(V(name, j), V(name, j), HD2 ** -0.5, None, ALU.mult))
            normalise(xrow, xnrow, TT, 0)
            rests_of_transposes("pre_g", ht_hi, ht_lo, S)

            G = lambda i, lo=0, hi=64: grow[lo:hi, i, :]
            dve.wait_ge(acc_ready, 2)
            v.tensor_scalar(G(0), acc[0:64, 0, :], vecs[0:64, VC["b_i"]:VC["b_i"] + 1], None, ALU.add)
            v.tensor_copy(G(1), acc[64:128, 0, :]).then_inc(acc_free, 1)
            dve.wait_ge(acc_free, 1)
            v.tensor_scalar(G(1), G(1), vecs[0:64, VC["b_f"]:VC["b_f"] + 1], None, ALU.add).then_inc(gate_rows, 1)
            dve.wait_ge(gate_rows, 1)
            dve.wait_ge(gate_exp, 1)
            step(v.scalar_tensor_tensor(G(1), G(1), 0.0, G(2), ALU.min, ALU.subtract))
            step(v.tensor_tensor_scan(G(3), G(1), G(1), 0.0, ALU.add, ALU.bypass))
            v.tensor_copy(G(4, 0, 32), G(3, 0, 32))
            step(v.tensor_tensor(G(4, 32, 64), G(1, 32, 64), G(3, 32, 64), ALU.subtract))
            step(v.tensor_tensor(G(5), G(0), G(4), ALU.subtract))
            v.tensor_tensor_scan(rowmax[0:32, :], G(5, 0, 32), G(5, 0, 32), FLOOR, ALU.max, ALU.bypass)
            back = G(5, 32, 64)[:, ::-1]
            step(v.tensor_tensor_scan(rowmax[32:64, ::-1], back, back, FLOOR, ALU.max, ALU.bypass))
            v.tensor_tensor(G(5, 64, 128), G(4), rowmax[:], ALU.add).then_inc(gm_ready, 1)

            _, a0, units = plan["u"]
            for g, w in enumerate(WINDOWS):
                dve.wait_ge(acc_free, a0 + g + 1)
                for j in (2 * g, 2 * g + 1):
                    u = uT[:, j, :]
                    src, margin = u, 1
                    step(v.tensor_tensor(win_s[:, 0, 1:UW], u[:, 0:UW - 1], u[:, 1:UW], ALU.add))
                    cur, lo, hi, shift = 0, 1, UW, 1
                    while 2 * shift < w:
                        lo, hi = lo + shift, hi - shift
                        step(v.tensor_tensor(win_s[:, 1 - cur, lo:hi], win_s[:, cur, lo - shift:hi - shift],
                                             win_s[:, cur, lo + shift:hi + shift], ALU.add))
                        cur, shift = 1 - cur, 2 * shift
                    sums = win_s[:, cur, PAD:PAD + S]
                    ends = sums.rearrange("p (b c) -> p b c", c=PAD)[:, 0:S // PAD:S // PAD - 1, :]
                    edge = V("edge", 2 * PAD * g, 2 * PAD).rearrange("p (b c) -> p b c", c=PAD)
                    step(v.tensor_tensor(ends, ends, edge, ALU.mult))
                    if j >= 4:
                        dve.wait_ge(hi_ready, j - 3)
                    tile_written(v.scalar_tensor_tensor(win_t[:, j % 4, :], sums, 1.0 / w, u[:, PAD:PAD + S],
                                                        ALU.mult, ALU.subtract))
                    dve.wait_ge(t_ready, seen["t"])
                    if j:
                        rest(win_t[:, (j - 1) % 4, :], op_hi[:, j - 1, :], op_lo[:, j - 1, :])
            rest(win_t[:, (KT - 1) % 4, :], op_hi[:, KT - 1, :], op_lo[:, KT - 1, :])
            dve.wait_ge(gmT_ready, 1)
            gmT = aux[:, 3, :].rearrange("p (t k d r) -> p t k d r", t=TT, k=2, d=2)
            for d in range(2):
                ins = v.tensor_copy(gcol[:, :, d, :], gmT[:, :, 0, d, 0:HEADS])
            ins.then_inc(gcol_ready, 1)

            _, a0, _ = plan["mix"]
            dve.wait_ge(acc_free, a0)
            for g in range(4):
                s = (a0 + g) % 2
                dve.wait_ge(acc_ready, 2 * (a0 + g + 1))
                for half in range(2):
                    j = 2 * g + half
                    dve.wait_ge(hi_ready, 8 + j - 3)
                    tile_written(v.scalar_tensor_tensor(win_t[:, j % 4, :], acc[:, 2 * s + half, :], V("pool_scale", j),
                                                        zaT[:, j, :], ALU.mult, ALU.mult))
                dve.wait_ge(t_ready, seen["t"])
                dve.sem_inc(acc_free, 1)
                for j in (2 * g, 2 * g + 1):
                    rest(win_t[:, j % 4, :], op_hi[:, j, :], op_lo[:, j, :])

            _, a0, units = plan["pa"]
            dve.wait_ge(acc_free, a0)

            def pa_body(u, q):
                for half in range(2):
                    dve.wait_ge(acc_ready, u * 2 + 2 * a0 + 1 + half)
                    m = mergedT[:, bass.ds(u * 2 + half, 1), :]
                    b = 2 * ((a0 + q) % 2) + half
                    ins = v.tensor_tensor(m, acc[:, b:b + 1, :], m, ALU.mult)
                    if half:
                        ins.then_inc(acc_free, 1)
            pairs(dve, units, pa_body)

            _, a0, units = plan["qk"]
            dve.wait_ge(acc_free, a0)
            v.memset(cpad[:, :, 0:2], 0.0)
            step(v.memset(cpad[:, :, 2 + S:CW], 0.0))

            def conv(u, q, first=False):
                dve.wait_ge(acc_free, u + a0 + 1)
                for half in range(2):
                    slot = 2 * q + half
                    if not first:
                        dve.wait_ge(silu_ready, u * 2 + half - 3)
                    out_ = cacc[:, slot, :]
                    tap = lambda k: Vd("conv_w", u * (2 * TAPS) + half * TAPS + k)
                    step(v.tensor_scalar(out_, cpad[:, slot, 0:S], tap(0), None, ALU.mult))
                    for k in range(1, TAPS):
                        ins = v.scalar_tensor_tensor(out_, cpad[:, slot, k:k + S], tap(k), out_, ALU.mult, ALU.add)
                        if k < TAPS - 1:
                            step(ins)
                        else:
                            ins.then_inc(conv_ready, 1)
            conv(0, 0, True)
            conv(1, 1, True)

            def conv_pair(i):
                conv(2 * i + 2, 0)
                conv(2 * i + 3, 1)
            step.loop(units // 2 - 1, 4 * (TAPS - 1), conv_pair)
            step(v.memset(vrow[:, :, :].rearrange("p t (h c) -> p t h c", h=HEADS)[:, :, :, HD:VW], 1.0))

            def decay_args(h, j):
                if TT * h + j >= 2:
                    dve.wait_ge(p_ready, TT * h + j - 1)
                for d in range(2):
                    lo, hi = (P * j, S) if d == 0 else (0, P * (j + 1))
                    w = hi - lo
                    dve.wait_ge(mbc_ready, h + 1)
                    mask = masks1[:, 0, 0:w] if d == 0 else masks1[:, 1, S - w:S]
                    v.scalar_tensor_tensor(decay[:, seen["arg"] % 4, 0:w], aux[:, d, lo:hi], gcol[:, j, d, h:h + 1],
                                           mask, ALU.subtract, ALU.max).then_inc(arg_ready, 1)
                    seen["arg"] += 1

            def probabilities(h):
                if h:
                    dve.wait_ge(pv_ready, TT * h)
                decay_args(h, 0)
                for j in range(TT):
                    if j + 1 < TT:
                        decay_args(h, j + 1)
                    dve.wait_ge(s_ready, TT * h + j + 1)
                    for d in range(2):
                        n = 2 * (TT * h + j) + d
                        lo, hi = (P * j, S) if d == 0 else (0, P * (j + 1))
                        dve.wait_ge(d_ready, n + 1)
                        ins = v.scalar_tensor_tensor(prob[:, d, j, lo:hi], aux[:, 2 + j % 2, lo:hi], HD ** -0.5,
                                                     decay[:, n % 4, 0:hi - lo], ALU.mult, ALU.mult)
                    ins.then_inc(p_ready, 1)

            probabilities(0)
            _, a0, _ = plan["ozb"]
            for h in range(HEADS):
                for t in range(TT):
                    i = TT * h + t
                    b = 2 * (t % 2)
                    c = 16 + 2 * (t % 2)
                    dve.wait_ge(den_ready, i + 1)
                    if i == 0:
                        dve.wait_ge(floor_ready, 2)
                    step(v.tensor_tensor(small[:, c:c + 2], small[:, c:c + 2], floorc[:, t, :, h], ALU.max))
                    v.reciprocal(small[:, c:c + 2], small[:, c:c + 2]).then_inc(rden_ready, 1)
                    dve.wait_ge(rden_ready, i + 1)
                    dve.wait_ge(hf_ready, i + 1)
                    v.scalar_tensor_tensor(hrow[:, t, :], aux[:, b + 1, 0:HD], small[:, c + 1:c + 2], hfwd[:, t % 2, :],
                                           ALU.mult, ALU.add).then_inc(hb_ready, 1)
                dve.wait_ge(hrs_ready, h + 1)
                for t in range(TT):
                    ins = v.tensor_scalar(hrow[:, t, :], hrow[:, t, :], small[:, 8 + t:9 + t], None, ALU.mult)
                ins.then_inc(hbn_ready, 1)
                if h + 1 < HEADS:
                    probabilities(h + 1)
                a = a0 + 2 * h + 1
                dve.wait_ge(acc_free, a)
                for half in range(2):
                    dve.wait_ge(zb_ready, 2 * h + half + 1)
                    og = ogT[:, 2 * h + half, :]
                    ins = v.tensor_tensor(og, acc[:, 2 * (a % 2) + half, :], og, ALU.mult)
                ins.then_inc(acc_free, 1)
                dve.wait_ge(acc_free, a + 1)
                for e in range(2):
                    j = 2 * h + e
                    dve.wait_ge(hT_ready, j + 1)
                    tile_written(v.scalar_tensor_tensor(ogT[:, j, :], aux[:, e, :], V("mlstm_g", j), ogT[:, j, :],
                                                        ALU.mult, ALU.mult))
            for j in range(KT):
                rest(ogT[:, j, :], op_hi[:, j, :], op_lo[:, j, :])

            _, a0, units = plan["pb"]
            dve.wait_ge(acc_free, a0)
            for u in range(units):
                for half in range(2):
                    j = 2 * u + half
                    dve.wait_ge(acc_ready, 2 * (a0 + u) + 1 + half)
                    ins = v.tensor_tensor(gbT[:, j, :], acc[:, 2 * ((a0 + u) % 2) + half, :], gbT[:, j, :], ALU.mult)
                    if half:
                        ins.then_inc(acc_free, 1)
                        dve.wait_ge(acc_free, a0 + u + 1)
                    else:
                        step(ins)
                    tile_written(v.tensor_tensor(mergedT[:, j, :], mergedT[:, j, :], gbT[:, j, :], ALU.add))
                for j in (2 * u, 2 * u + 1):
                    rest(mergedT[:, j, :], ht_hi[:, j, :], ht_lo[:, j, :])
            normalise(memrow, memn, MT, 20)

            dve.wait_ge(post_ssq, TT)
            v.tensor_scalar(small[:, 0:4], small[:, 0:4], 1.0 / D, EPS, ALU.mult, ALU.add).then_inc(post_var, 1)
            dve.wait_ge(post_sd, 1)
            step(v.reciprocal(small[:, 4:8], small[:, 0:4]))
            dve.wait_ge(post_in, 32)
            for t in range(TT):
                step(v.scalar_tensor_tensor(xrow[:, t, :], orow1[:, t, :], small[:, 4 + t:5 + t], gpost[:],
                                            ALU.mult, ALU.mult))
                v.tensor_tensor(xrow[:, t, :], xrow[:, t, :], xagain[:, t, :], ALU.add).then_inc(x_rows, 1)

            def head_norm_raw(a, half, dst):
                n = seen["hn"] + half
                dve.wait_ge(sq_ready, n + 1)
                dve.wait_ge(acc_free, a)
                ins = v.tensor_copy(dst, acc[:, 2 * (a % 2) + half, 0:dst.shape[-1]])
                if half:
                    ins.then_inc(acc_free, 1)

            def head_norm_scale(n, a, dst, gain):
                dve.wait_ge(acc_free, a + 1)
                dve.wait_ge(rs_ready, n + 1)
                v.scalar_tensor_tensor(dst, dst, gain, hn_rs[:, n % 2, 0:dst.shape[-1]],
                                       ALU.mult, ALU.mult).then_inc(hn_done, 1)

            done = 0
            for L, name in enumerate("eo"):
                qk, _ = LAYERS[L]
                rests_of_transposes(name + "_mem", memT_hi, memT_lo, MEM)
                a0 = plan[name + "_mem"][1]
                for half in range(2):
                    head_norm_raw(a0, half, mkT[:, half, :])
                for half in range(2):
                    head_norm_scale(seen["hn"] + half, a0, mkT[:, half, :], V(name + "_qk", 5 if L == 0 else 3))
                seen["hn"] += 2
                if L == 0:
                    dve.wait_ge(x_rows, TT)
                normalise(xrow, xnrow, TT, 0)
                rests_of_transposes(name + "_norm", ht_hi, ht_lo, S)
                if L:
                    a = plan["o_f"][1]
                    step(v.memset(negc[:], 0.0))
                    dve.wait_ge(acc_ready, 2 * (a + 1))
                    dve.wait_ge(acc_free, a)
                    R = lambda i: frow[0:C_HEADS, i, :]
                    v.tensor_copy(R(0), acc[0:C_HEADS, 2 * (a % 2), :]).then_inc(acc_free, 1)
                    dve.wait_ge(acc_free, a + 1)
                    v.tensor_scalar(R(0), R(0), vecs[0:C_HEADS, VC["o_bf"]:VC["o_bf"] + 1], None, ALU.add).then_inc(gate_rows, 1)
                    dve.wait_ge(gate_rows, 2)
                    dve.wait_ge(gate_exp, 2)
                    step(v.scalar_tensor_tensor(R(1), R(0), 0.0, R(1), ALU.min, ALU.subtract))
                    step(v.tensor_tensor_scan(R(2), R(1), R(1), 0.0, ALU.add, ALU.bypass))
                    v.tensor_scalar(negc[0:C_HEADS, :], R(2), -1.0, None, ALU.mult).then_inc(negc_ready, 1)
                _, a0, units = plan[name + "_qk"]

                def scale_unit(u):
                    for half in range(2):
                        j = 2 * u + half
                        head_norm_scale(seen["hn"] - 2 + half, a0 + u, qk[:, j, :], V(name + "_qk", QK_GAINS[L][j]))
                for u in range(units):
                    for half in range(2):
                        head_norm_raw(a0 + u, half, qk[:, 2 * u + half, :])
                    if u:
                        scale_unit(u - 1)
                    seen["hn"] += 2
                scale_unit(units - 1)

                jobs = JOBS[L]
                if L == 0:
                    dve.wait_ge(masks2_in, 16)
                DIST, CAUSAL, WINDOW = (masks2[:, 0:S], masks2[:, S:2 * S], masks2[:, 2 * S:2 * S + 2 * WIN])
                for i in range(len(jobs) + 2):
                    if i < len(jobs):
                        job, g = jobs[i], done + i
                        logits = logit_bank(i)[:, 0:job.keys]
                        if job.bias is not None:
                            kind, h, slope = job.bias
                            if kind == "forget":
                                tile = CAUSAL
                            else:
                                full = DIST if kind == "dist" else WINDOW
                                tile = bias_h[:, h % 2, 0:full.shape[-1]]
                                if job.t == 0:
                                    step(v.tensor_scalar(tile, full, slope, None, ALU.mult))
                            width = tile.shape[-1]
                            if g >= 3:
                                dve.wait_ge(pr_ready, g - 2)
                            dve.wait_ge(logit_ready, g + 1)
                            step(v.tensor_tensor_reduce(out=sc[:, i % 3, 0:job.keys], in0=logits,
                                                        in1=tile[:, width - job.keys:width], scale=1.0, scalar=FLOOR,
                                                        op0=ALU.add, op1=ALU.max, accum_out=stats[:, 0, i:i + 1]))
                        else:
                            dve.wait_ge(logit_ready, g + 1)
                            step(v.reduce_max(stats[:, 0, i:i + 1], logits, AX.X))
                        if job.sink is None:
                            v.tensor_scalar(stats[:, 1, i:i + 1], stats[:, 0, i:i + 1], -1.0, None,
                                            ALU.mult).then_inc(nm_ready, 1)
                        else:
                            v.tensor_scalar(stats[:, 1, i:i + 1], stats[:, 0, i:i + 1], V("sinks", job.sink), -1.0,
                                            ALU.max, ALU.mult).then_inc(nm_ready, 1)
                    if 1 <= i <= len(jobs):
                        k = i - 1
                        dve.wait_ge(pr_ready, done + k + 1)
                        if jobs[k].sink is not None:
                            dve.wait_ge(es_ready, k + 1)
                            step(v.tensor_tensor(stats[:, 2, k:k + 1], stats[:, 2, k:k + 1], stats[:, 3, k:k + 1], ALU.add))
                        v.reciprocal(stats[:, 4, k:k + 1], stats[:, 2, k:k + 1]).then_inc(ri_ready, 1)
                    if i >= 2:
                        k = i - 2
                        dve.wait_ge(prT_ready, done + k + 1)
                        if done + k >= 2:
                            dve.wait_ge(o_ready, done + k - 1)
                        v.tensor_copy(prT[:, k % 2, 0:jobs[k].keys], trans_bank(k)[:, 0:jobs[k].keys]).then_inc(prT_copied, 1)
                done += len(jobs)

                dve.wait_ge(acc_free, plan[name + "_out"][1])
                for j in range(KT):
                    seen["aT"] += 1
                    dve.wait_ge(arow_T, seen["aT"])
                    tile_written(v.tensor_tensor(zT[:, j, :], aux[:, j % 4, :], zT[:, j, :], ALU.mult))
                    if j:
                        rest(zT[:, j - 1, :], op_hi[:, j - 1, :], op_lo[:, j - 1, :])
                rest(zT[:, KT - 1, :], op_hi[:, KT - 1, :], op_lo[:, KT - 1, :])
                if L == 0:
                    normalise(memrow, memn, MT, 20)
                _, a0, units = plan[name + "_out"]

                def residual(u, q):
                    for half in range(2):
                        dve.wait_ge(acc_ready, u * 2 + 2 * a0 + 1 + half)
                        rows = xrow[:, 2 * half:2 * half + 2, bass.ds(u * UC, UC)]
                        bank = acc[:, 2 * ((a0 + q) % 2) + half, :].rearrange("p (t c) -> p t c", t=2)
                        ins = v.tensor_tensor(rows, bank, rows, ALU.add)
                        if half:
                            ins.then_inc(acc_free, 1)
                pairs(dve, units, residual)

        @block.tensor
        def _(pe):
            seen = {"xn": 0, "tr": 0, "hn": 0, "aT": 0}
            mm = nc.tensor.matmul

            def product(out_, w_hi_, w_lo_, x_hi, x_lo, first, last):
                mm(out_, w_hi_, x_hi, start=first, stop=False)
                mm(out_, w_hi_, x_lo, start=False, stop=False)
                return mm(out_, w_lo_, x_hi, start=False, stop=last)

            def unit_waits(n, a):
                pe.wait_ge(w_split, n + 1)
                if not (isinstance(a, int) and a < 2):
                    pe.wait_ge(acc_free, a - 1)

            def by_channels(n, a, s, b, x_hi, x_lo, cols=S):
                unit_waits(n, a)
                for half in range(2):
                    for k in range(KT):
                        c = k * UC + half * P
                        ins = product(acc[:, 2 * b + half, 0:cols], whi[:, s, c:c + P], wlo[:, s, c:c + P],
                                      x_hi[:, k, :], x_lo[:, k, :], k == 0, k == KT - 1)
                    ins.then_inc(acc_ready, 1)

            def by_rows(n, a, s, b, x_hi, x_lo, tiles=TT):
                unit_waits(n, a)
                per = tiles // 2
                for t in range(tiles):
                    out_ = acc[:, 2 * b + t // per, UC * (t % per):UC * (t % per) + UC]
                    for k in range(KT):
                        ins = product(out_, x_hi[:, k, P * t:P * t + P], x_lo[:, k, P * t:P * t + P],
                                      whi[:, s, k * UC:k * UC + UC], wlo[:, s, k * UC:k * UC + UC], k == 0, k == KT - 1)
                    if t % per == per - 1:
                        ins.then_inc(acc_ready, 1)

            def stage(name, kind, x_hi, x_lo, peel=0):
                n0, a0, units = plan[name]
                pairs(pe, units, lambda u, q: kind(u + n0, u + a0, (n0 + q) % 2, (a0 + q) % 2, x_hi, x_lo), peel)

            def transposes(rows, tiles):
                seen["xn"] += tiles
                pe.wait_ge(xn_ready, seen["xn"])
                for k in range(KT):
                    if seen["tr"] >= 4:
                        pe.wait_ge(tr_lo, seen["tr"] - 3)
                    for t in range(tiles):
                        ins = nc.tensor.transpose(aux[:, k % 4, P * t:P * t + P], rows[:, t, P * k:P * k + P], ident[:])
                    ins.then_inc(tr_ready, 1)
                    seen["tr"] += 1

            pe.wait_ge(consts_in, 64)
            transposes(xnrow, TT)
            pe.wait_ge(tr_lo, KT)
            pe.wait_ge(w_split, 1)
            for k in range(KT):
                ins = product(acc[:, 0, :], whi[:, 0, P * k:P * k + P], wlo[:, 0, P * k:P * k + P],
                              ht_hi[:, k, :], ht_lo[:, k, :], k == 0, k == KT - 1)
            ins.then_inc(acc_ready, 2)
            stage("u", by_channels, ht_hi, ht_lo, peel=1)
            pe.wait_ge(gm_ready, 1)
            for t in range(TT):
                ins = nc.tensor.transpose(aux[:, 3, P * t:P * t + P], grow[:, 5, P * t:P * t + P], ident[:])
            ins.then_inc(gmT_ready, 1)
            stage("za", by_channels, ht_hi, ht_lo)
            n, a0, _ = plan["mix"]
            pe.wait_ge(lo_ready, 8)
            for g in range(4):
                unit_waits(n, a0 + g)
                for m in range(2):
                    for kk in range(2):
                        c = (2 * g + kk) * UC + P * m
                        ins = product(acc[:, 2 * ((a0 + g) % 2) + m, :], whi[:, n % 2, c:c + P], wlo[:, n % 2, c:c + P],
                                      op_hi[:, 2 * g + kk, :], op_lo[:, 2 * g + kk, :], kk == 0, kk == 1)
                    ins.then_inc(acc_ready, 1)
            stage("ga", by_channels, ht_hi, ht_lo)
            pe.wait_ge(lo_ready, 16)
            stage("pa", by_channels, op_hi, op_lo)
            stage("qk", by_channels, ht_hi, ht_lo)
            stage("v", by_rows, ht_hi, ht_lo)

            def scores(h):
                if h:
                    pe.wait_ge(hb_ready, TT * h)
                    if h > 1:
                        pe.wait_ge(t_ready, 16 + 2 * (h - 1))
                else:
                    pe.wait_ge(silu_ready, 2 * KT)
                    pe.wait_ge(floor_ready, 2)
                for d in range(2):
                    r = 32 * d + h
                    ins = mm(aux[:, d, :], ident[0:64, r:r + 1].to_broadcast([64, P]), rowmax[0:64, :], start=True, stop=True)
                ins.then_inc(mbc_ready, 1)
                for j in range(TT):
                    if j >= 2:
                        pe.wait_ge(p_ready, TT * h + j - 1)
                    for kk in range(2):
                        ins = mm(aux[:, 2 + j % 2, :], qkT[:, KT + 2 * h + kk, P * j:P * j + P], qkT[:, 2 * h + kk, :],
                                 start=kk == 0, stop=kk == 1)
                    ins.then_inc(s_ready, 1)

            def values(h):
                pe.wait_ge(p_ready, TT * (h + 1))
                if h:
                    pe.wait_ge(t_ready, 16 + 2 * h)
                for t in range(TT):
                    if t >= 2:
                        pe.wait_ge(hb_ready, TT * h + t - 1)
                    for d in range(2):
                        keys = range(0, t + 1) if d == 0 else range(t, TT)
                        for j in keys:
                            ins = mm(aux[:, 2 * (t % 2) + d, 0:VW], prob[:, d, j, P * t:P * t + P],
                                     vrow[:, j, VW * h:VW * h + VW], start=j == keys[0], stop=j == keys[-1])
                    ins.then_inc(pv_ready, 1)

            def output_transposes(h):
                pe.wait_ge(hbn_ready, h + 1)
                if h + 1 < HEADS:
                    pe.wait_ge(p_ready, TT * (h + 2))
                for e in range(2):
                    for t in range(TT):
                        ins = nc.tensor.transpose(aux[:, e, P * t:P * t + P], hrow[:, t, P * e:P * e + P], ident[:])
                    ins.then_inc(hT_ready, 1)

            n0, a0, _ = plan["ozb"]
            pe.wait_ge(acc_free, a0)
            scores(0)
            for h in range(HEADS):
                n, a = n0 + 2 * h, a0 + 2 * h
                by_channels(n, a, n % 2, a % 2, ht_hi, ht_lo)
                values(h)
                if h + 1 < HEADS:
                    scores(h + 1)
                by_channels(n + 1, a + 1, (n + 1) % 2, (a + 1) % 2, ht_hi, ht_lo)
                output_transposes(h)
            stage("gb", by_channels, ht_hi, ht_lo)
            pe.wait_ge(lo_ready, 24)
            stage("pb", by_channels, op_hi, op_lo)
            pe.wait_ge(lo_ready, 32)
            stage("wout", by_rows, ht_hi, ht_lo)

            def sum_squares(cols):
                n = seen["hn"]
                pe.wait_ge(sq_ready, n + 1)
                if n >= 2:
                    pe.wait_ge(ln_done, n - 1)
                mm(aux[:, n % 2, 0:cols], bones[:], hn_sq[:, n % 2, 0:cols], start=True, stop=True).then_inc(ssq_ready, 1)
                seen["hn"] += 1

            done = 0
            for L, name in enumerate("eo"):
                qk, vv = LAYERS[L]
                transposes(memn, MT)
                pe.wait_ge(tr_lo, seen["tr"])
                n0, a0, _ = plan[name + "_mem"]
                by_channels(n0, a0, n0 % 2, a0 % 2, memT_hi, memT_lo, MEM)
                by_rows(n0 + 1, a0 + 1, (n0 + 1) % 2, (a0 + 1) % 2, memT_hi, memT_lo, MT)
                for half in range(2):
                    sum_squares(MEM)
                pe.wait_ge(ln_done, seen["hn"])
                transposes(xnrow, TT)
                pe.wait_ge(tr_lo, seen["tr"])
                if L:
                    n, a, _ = plan["o_f"]
                    unit_waits(n, a)
                    for k in range(KT):
                        ins = product(acc[:, 2 * (a % 2), :], whi[:, n % 2, P * k:P * k + P],
                                      wlo[:, n % 2, P * k:P * k + P], ht_hi[:, k, :], ht_lo[:, k, :], k == 0, k == KT - 1)
                    ins.then_inc(acc_ready, 2)
                n0, a0, units = plan[name + "_qk"]
                for u in range(units):
                    by_channels(n0 + u, a0 + u, (n0 + u) % 2, (a0 + u) % 2, ht_hi, ht_lo)
                    if u:
                        sum_squares(S)
                        sum_squares(S)
                n0, a0, units = plan[name + "_v"]
                for u in range(units):
                    by_rows(n0 + u, a0 + u, (n0 + u) % 2, (a0 + u) % 2, ht_hi, ht_lo)
                    if u == 0:
                        sum_squares(S)
                        sum_squares(S)
                stage(name + "_z", by_channels, ht_hi, ht_lo)

                jobs = JOBS[L]
                pe.wait_ge(acc_free, plan[name + "_out"][1])
                pe.wait_ge(hn_done, seen["hn"])
                if L:
                    pe.wait_ge(negc_ready, 1)
                for i in range(len(jobs) + 3):
                    if i < len(jobs):
                        job, g = jobs[i], done + i
                        if g >= 3:
                            pe.wait_ge(pr_ready, g - 2)
                        (qt, qp), (kt_, kp) = job.q, job.k
                        keysT = mkT if job.bias is None else qk
                        out_ = logit_bank(i)[:, 0:job.keys]
                        k0 = P * job.k0
                        forget = job.bias is not None and job.bias[0] == "forget"
                        ins = mm(out_, qk[qp:qp + HD2, qt, P * job.t:P * job.t + P],
                                 keysT[kp:kp + HD2, kt_, k0:k0 + job.keys], start=True, stop=not forget)
                        if forget:
                            h = job.bias[1]
                            ins = mm(out_, ident[:, h:h + 1].to_broadcast([P, P]), negc[:, 0:job.keys], start=False, stop=True)
                        ins.then_inc(logit_ready, 1)
                    if 2 <= i < len(jobs) + 2:
                        k = i - 2
                        pe.wait_ge(pr_ready, done + k + 1)
                        if done + k >= 2:
                            pe.wait_ge(prT_copied, done + k - 1)
                        for b in range(jobs[k].keys // P):
                            ins = nc.tensor.transpose(trans_bank(k)[:, P * b:P * b + P], pr[:, k % 3, P * b:P * b + P], ident[:])
                        ins.then_inc(prT_ready, 1)
                    if i >= 3:
                        k = i - 3
                        job = jobs[k]
                        pe.wait_ge(prT_copied, done + k + 1)
                        if done + k >= 3:
                            pe.wait_ge(o_done, done + k - 2)
                        nb = job.keys // P
                        for b in range(nb):
                            vals = (mv if job.bias is None else vv)[:, job.k0 + b, job.v:job.v + HD2]
                            ins = mm(out_bank(k)[:, 0:HD2], prT[:, k % 2, P * b:P * b + P], vals, start=b == 0, stop=b == nb - 1)
                        ins.then_inc(o_ready, 1)
                done += len(jobs)
                pe.wait_ge(o_done, done)
                for k in range(KT):
                    if k >= 4:
                        pe.wait_ge(t_ready, 32 + 8 * L + k - 3)
                    for t in range(TT):
                        ins = nc.tensor.transpose(aux[:, k % 4, P * t:P * t + P], arow[:, t, P * k:P * k + P], ident[:])
                    ins.then_inc(arow_T, 1)
                pe.wait_ge(lo_ready, 40 + 8 * L)
                stage(name + "_out", by_rows, op_hi, op_lo)


def columns(v):
    return np.ascontiguousarray(np.reshape(v, (-1, P)).T)


def pack(inputs):
    vecs = np.zeros((P, NVEC), np.float32)

    def put(name, block, rows=slice(None)):
        vecs[rows, VC[name]:VC[name] + block.shape[1]] = block
    put("pre_g", columns(inputs["norm_pre_g"][0]))
    put("conv_w", inputs["conv_qk_w"][0].reshape(TAPS, 16, P).transpose(2, 1, 0).reshape(P, 16 * TAPS))
    put("conv_b", columns(inputs["conv_qk_b"][0]))
    put("pool_scale", columns(inputs["pool_scale"][0]))
    put("mlstm_g", columns(inputs["mlstm_norm_g"][0]))
    put("b_merge", columns(inputs["b_merge"][0]))
    put("e_norm", columns(inputs["e_norm_2"][0]))
    put("e_mem", columns(inputs["e_mem_norm_2"][0]))
    put("o_norm", columns(inputs["o_norm_2"][0]))
    put("o_mem", columns(inputs["o_mem_norm_2"][0]))
    for half in range(2):
        put("e_qk", inputs["e_qk_norm_2"][0].T, slice(HD2 * half, HD2 * half + HD2))
        put("o_qk", inputs["o_qk_norm_2"][0].T, slice(HD2 * half, HD2 * half + HD2))
        put("b_i", inputs["b_igate"][0, half][:, None], slice(32 * half, 32 * half + HEADS))
        put("b_f", inputs["b_fgate"][0, half][:, None], slice(32 * half, 32 * half + HEADS))
    put("sinks", np.broadcast_to(inputs["e_sinks_2"][0][None, :], (P, A_HEADS)))
    put("o_bf", inputs["o_b_f_2"][0][:, None], slice(0, C_HEADS))
    put("eps", np.full((P, 1), EPS, np.float32))
    put("edge", np.broadcast_to(edge_constants()[None, :], (P, 2 * PAD * len(WINDOWS))))
    return vecs


DIRECT = ["x", "w_in", "pool_mix_w", "w_proj_pool", "w_proj_mlstm", "w_out", "norm_post_g", "mem_2",
          "e_w_in_2", "e_w_mem_kv_2", "e_w_out_2", "o_w_in_2", "o_w_mem_kv_2", "o_w_out_2"]


def kernel(**inputs):
    import concourse.bacc as bacc
    from concourse.bass_utils import run_bass_kernel_spmd

    nc = bacc.Bacc("TRN2", target_bir_lowering=False, num_devices=1)
    inputs = {k: np.asarray(v) for k, v in inputs.items()}
    arrays = {k: np.ascontiguousarray(inputs[k]) for k in DIRECT}
    arrays["vecs"] = pack(inputs)
    arrays["consts"] = shape_constants()
    aps = {k: nc.dram_tensor(k + "_dram", a.shape, F32, kind="ExternalInput").ap() for k, a in arrays.items()}
    out = nc.dram_tensor("out_dram", (1, S, D), F32, kind="ExternalOutput").ap()
    hybrid_block_then_two_attention_layers(nc, aps, aps["vecs"], aps["consts"], out)
    result = run_bass_kernel_spmd(nc, [{k + "_dram": a for k, a in arrays.items()}], core_ids=[0])
    return result.results[0]["out_dram"]
```

```python
from collections import namedtuple
from contextlib import ExitStack

import numpy as np
import concourse.bass as bass
from concourse import mybir

F32 = mybir.dt.float32
F32R = mybir.dt.float32r
ACT = mybir.ActivationFunctionType
ALU = mybir.AluOpType
AX = mybir.AxisListType

P = 128
D = 1024
KT = D // P
S = 512
TT = S // P
UC = 256
SLOT = KT * UC
EPS = 1e-6
BIG = 1e30
FLOOR = -3e38

HEADS, HD = 4, 256
WINDOWS = (2, 4, 8, 16)
TAPS = 5
PAD = max(WINDOWS) // 2
UW = S + 2 * PAD
CW = S + TAPS - 1
VW = HD + 1
COL_U, COL_ZA, COL_QK, COL_V, COL_O, COL_ZB, COL_GATES, COL_GA, COL_GB = (
    0, D, 2 * D, 4 * D, 5 * D, 6 * D, 7 * D, 7 * D + 16, 8 * D + 16)

HD2 = 64
WIN = 128
MEM = 256
MT = MEM // P
A_HEADS, B_HEADS, C_HEADS, M_HEADS = 6, 6, 12, 4
SLOPES = [2.0 ** (-8.0 * (h + 1) / (A_HEADS + B_HEADS)) for h in range(A_HEADS + B_HEADS)]

_widths = [("pre_g", KT), ("conv_w", 16 * TAPS), ("conv_b", 16), ("pool_scale", KT), ("mlstm_g", KT),
           ("b_merge", 2 * KT), ("e_norm", KT), ("e_mem", KT), ("o_norm", KT), ("o_mem", KT),
           ("e_qk", 6), ("o_qk", 4), ("b_i", 1), ("b_f", 1), ("sinks", A_HEADS), ("o_bf", 1),
           ("eps", 1), ("edge", 2 * PAD * len(WINDOWS))]
VC = {}
_at = 0
for _name, _w in _widths:
    VC[_name] = _at
    _at += _w
NVEC = 256
assert _at <= NVEC


E_COLS = tuple(int(c) for c in np.cumsum([0, A_HEADS * HD2, 2 * HD2, 2 * HD2, B_HEADS * HD2, B_HEADS * HD2,
                                          B_HEADS * HD2, M_HEADS * HD2]))
O_COLS = tuple(int(c) for c in np.cumsum([0, C_HEADS * HD2, C_HEADS * HD2, C_HEADS * HD2, C_HEADS, M_HEADS * HD2]))
Job = namedtuple("Job", "t k0 keys q k bias v sink col slot")
QK_GAINS = ([0, 0, 0, 1, 2, 2, 2, 3, 3, 3, 4, 4], [0] * 6 + [1] * 6 + [2] * 2)


def shape_constants():
    p = np.arange(P)[:, None]
    c = np.arange(S)[None, :]
    ident = np.eye(P)
    bones = (p // HD2 == np.arange(P)[None, :] // HD2) * 1.0
    fwd = np.where(c >= p, 0.0, BIG)
    bwd = np.where(c - (S - P) <= p, 0.0, BIG)
    dist = np.where(c - (S - P) <= p, c - (S - P) - p, -BIG)
    causal = np.where(np.arange(P)[None, :] <= p, 0.0, -BIG)
    w = np.arange(2 * WIN)[None, :]
    back = WIN + p - w
    window = np.where((back >= 0) & (back < WIN), -back, -BIG)
    return np.concatenate([ident, bones, fwd, bwd, dist, causal, window], axis=1).astype(np.float32)


def edge_constants():
    out = []
    for w in WINDOWS:
        for t0 in (0, S - PAD):
            for t in range(t0, t0 + PAD):
                lo, hi = max(t - w // 2, 0), min(t + w - 1 - w // 2, S - 1)
                out.append(w / (hi - lo + 1))
    return np.array(out, np.float32)


class Steps:

    def __init__(self, eng, sem):
        self.eng, self.sem, self.n, self.it, self.per = eng, sem, 0, None, 0

    def __call__(self, ins):
        ins.then_inc(self.sem, 1)
        self.n += 1
        self.eng.wait_ge(self.sem, self.n if self.it is None else self.it * self.per + self.n)

    def loop(self, count, per, body):
        n0 = self.n
        with self.eng.Fori(0, count) as i:
            self.it, self.per = i, per
            body(i)
        assert self.n == n0 + per
        self.n, self.it = n0 + per * count, None


def hybrid_block_then_two_attention_layers(nc, A, vecs_d, consts_d, out):
    stack = ExitStack()
    with stack:
        base = (nc.sbuf_base + 63) // 64 * 64
        K = 1024

        def at(name, shape, offset, dt=F32):
            return nc.alloc_sbuf_tensor_at(name, shape, dt, offset=base + offset)

        def sem(name):
            return stack.enter_context(nc.semaphore(name))

        HT, OP, RAW, WHI, WLO, R0, R1, R2, R3, R4, CST = (
            0, 32 * K, 64 * K, 80 * K, 96 * K, 112 * K, 128 * K, 144 * K, 160 * K, 177 * K, 193 * K)
        ht_hi = at("ht_hi", [P, KT, S], HT, F32R)
        ht_lo = at("ht_lo", [P, KT, S], HT + 16 * K, F32R)
        op_hi = at("op_hi", [P, KT, S], OP, F32R)
        op_lo = at("op_lo", [P, KT, S], OP + 16 * K, F32R)
        raw = at("raw", [P, 2, SLOT], RAW)
        whi = at("whi", [P, 2, SLOT], WHI, F32R)
        wlo = at("wlo", [P, 2, SLOT], WLO, F32R)

        ident = at("ident", [P, P], CST)
        bones = at("bones", [P, P], CST + 512)
        vecs = at("vecs", [P, NVEC], CST + K)
        masks1 = at("masks1", [P, 2, S], CST + 2 * K)
        masks2 = at("masks2", [P, S + P + 2 * WIN], CST + 2 * K)
        causal_r = at("causal_r", [P, P], CST + 2 * K + 3584, F32R)
        ident_r = at("ident_r", [P, P], CST + 2 * K + 4096, F32R)
        bones_r = at("bones_r", [P, P], CST + 2 * K + 4608, F32R)
        rowmax = at("rowmax", [64, S], CST + 7 * K)
        negc = at("negc", [P, S], CST + 7 * K)
        mkT = at("mkT", [P, 2, MEM], CST + 9 * K)
        mv = at("mv", [P, MT, MEM], CST + 11 * K)
        stats = at("stats", [P, 6, 64], CST + 13 * K)
        gcol = at("gcol", [P, TT, 2, HEADS], CST + 14 * K + 512)
        floorc = at("floorc", [P, TT, 2, HEADS], CST + 14 * K + 640)
        small = at("small", [P, 24], CST + 14 * K + 768)

        xrow = at("xrow", [P, TT, D], R4)
        xnrow = at("xnrow", [P, TT, D], R0)
        zaT = at("zaT", [P, KT, S], R0)
        uT = at("uT", [P, KT, UW], R1)
        win_s = at("win_s", [P, 2, UW], R3)
        win_t = at("win_t", [P, 4, S], R3 + 5 * K)
        grow = at("grow", [P, 7, S], R2 + 2 * K)
        mergedT = at("mergedT", [P, KT, S], R4)
        cpad = at("cpad", [P, 4, CW + 12], OP)
        cacc = at("cacc", [P, 4, S], OP + 10 * K)
        qkT = at("qkT", [P, 2 * KT, S], R1)
        vrow = at("vrow", [P, TT, HEADS * VW], R3)
        ogT = at("ogT", [P, KT, S], R0)
        decay = at("decay", [P, 4, S], OP)
        prob = at("prob", [P, 2, TT, S], OP + 8 * K)
        hrow = at("hrow", [P, TT, HD], OP + 24 * K)
        hfwd = at("hfwd", [P, 2, HD], OP + 28 * K)
        hsq = at("hsq", [P, HD], OP + 30 * K)
        gbT = at("gbT", [P, KT, S], R2)
        orow1 = at("orow1", [P, TT, D], R0)
        xagain = at("xagain", [P, TT, D], R1)
        gpost = at("gpost", [P, D], R2)
        junk = at("junk", [P, D], R2 + 4 * K)
        memrow = at("memrow", [P, MT, D], R3)
        memn = at("memn", [P, MT, D], R3 + 8 * K)
        memT_hi = at("memT_hi", [P, KT, MEM], OP, F32R)
        memT_lo = at("memT_lo", [P, KT, MEM], OP + 8 * K, F32R)
        hn_sq = at("hn_sq", [P, 2, S], OP + 16 * K)
        hn_rs = at("hn_rs", [P, 2, S], OP + 20 * K)
        hn_hi = at("hn_hi", [P, 2, S], OP + 24 * K, F32R)
        hn_lo = at("hn_lo", [P, 2, S], OP + 28 * K, F32R)
        zT = at("zT", [P, KT, S], R0)
        frow = at("frow", [P, 3, S], R0)
        arow = at("arow", [P, TT, D], OP)
        sc = at("sc", [P, 3, S], OP + 16 * K)
        pr = at("pr", [P, 3, S], OP + 22 * K)
        prT = at("prT", [P, 2, S], OP + 28 * K)
        negc_all = at("negc_all", [P, 4, S], R3 + 8 * K)
        bias_h = at("bias_h", [P, 2, S], R3)
        LAYERS = []
        for name, ntile, vcols, voff in (("e", 12, 512, 24 * K), ("o", 14, 768, 28 * K)):
            LAYERS.append((at("qk_" + name, [P, ntile, S], R1), at("v_" + name, [P, TT, vcols], R1 + voff)))

        negc_dram = nc.dram_tensor("negc_rows", (C_HEADS, S), F32, kind="Internal").ap()
        acc = stack.enter_context(nc.psum_tensor("acc", [P, 4, S], F32))
        aux = stack.enter_context(nc.psum_tensor("aux", [P, 4, S], F32))

        def V(name, j=0, n=1):
            return vecs[:, VC[name] + j:VC[name] + j + n]

        def Vd(name, j):
            return vecs[:, bass.ds(j + VC[name], 1)]

        ident_in = sem("ident_in")
        vecs_in = sem("vecs_in")
        consts_in = sem("consts_in")
        x_in = [sem(f"x_in{t}") for t in range(TT)]
        w_loaded = [sem("w_loaded_0"), sem("w_loaded_1")]
        w_hi = sem("w_hi")
        w_split = sem("w_split")
        acc_ready = sem("acc_ready")
        acc_free = sem("acc_evacuated")
        pool_step = sem("pool_step")
        units_begun = sem("units_begun")
        act_step = sem("act_step")
        dve_step = sem("dve_step")
        rssq_ready = sem("rssq_ready")
        rvar_ready = sem("rvar_ready")
        rsd_ready = sem("rsd_ready")
        xn_ready = sem("xn_ready")
        tr_ready = sem("tr_ready")
        tr_hi = sem("tr_hi")
        tr_lo = sem("tr_lo")
        t_ready = sem("t_ready")
        hi_ready = sem("hi_ready")
        lo_ready = sem("lo_ready")
        conv_ready = sem("conv_ready")
        silu_ready = sem("silu_ready")
        gate_rows = sem("gate_rows")
        gate_exp = sem("gate_exp")
        gm_ready = sem("gm_ready")
        gmT_ready = sem("gmT_ready")
        gcol_ready = sem("gcol_ready")
        floor_ready = sem("floor_ready")
        mbc_ready = sem("mbc_ready")
        s_ready = sem("s_ready")
        arg_ready = sem("arg_ready")
        d_ready = sem("d_ready")
        p_ready = sem("p_ready")
        pv_ready = sem("pv_ready")
        den_ready = sem("den_ready")
        rden_ready = sem("rden_ready")
        hf_ready = sem("hf_ready")
        hb_ready = sem("hb_ready")
        hssq_ready = sem("hssq_ready")
        hrs_ready = sem("hrs_ready")
        hbn_ready = sem("hbn_ready")
        hT_ready = sem("hT_ready")
        zb_ready = sem("zb_ready")
        post_in = sem("post_in")
        post_ssq = sem("post_ssq")
        post_var = sem("post_var")
        post_sd = sem("post_sd")
        mem_in = sem("mem_in")
        sq_ready = sem("sq_ready")
        sq_split = sem("sq_split")
        ssq_ready = sem("ssq_ready")
        ln_done = sem("ln_done")
        rs_ready = sem("rs_ready")
        hn_done = sem("hn_done")
        negc_ready = sem("negc_ready")
        negc_out = sem("negc_out")
        sc_ready = sem("sc_ready")
        nm_ready = sem("nm_ready")
        es_ready = sem("es_ready")
        pr_ready = sem("pr_ready")
        prT_ready = sem("prT_ready")
        prT_copied = sem("prT_copied")
        ri_ready = sem("ri_ready")
        o_ready = sem("o_ready")
        o_done = sem("o_done")
        arow_T = sem("arow_T")
        x_rows = sem("x_rows")
        logit_ready = sem("logit_ready")
        stored = sem("stored")
        masks2_in = sem("masks2_in")
        th_ready = sem("th_ready")
        z_half = sem("z_half")
        masks_r = sem("masks_r")
        negc_in = [sem(f"negc_in{i}") for i in range(4)]

        block = stack.enter_context(nc.Block())

        plan = {}
        n_, a_ = 0, 0
        for name, units, accs in (("gates", 1, 1), ("u", 4, 4), ("za", 4, 4), ("mix", 1, 4), ("ga", 4, 4), ("pa", 4, 4),
                                  ("qk", 8, 8), ("v", 4, 4), ("ozb", 8, 8), ("gb", 4, 4), ("pb", 4, 4),
                                  ("wout", 4, 4), ("e_mem", 2, 2), ("e_qk", 6, 6), ("e_v", 2, 2),
                                  ("e_z", 4, 4), ("e_out", 4, 4), ("o_mem", 2, 2), ("o_f", 1, 1),
                                  ("o_qk", 7, 7), ("o_v", 3, 3), ("o_z", 4, 4), ("o_out", 4, 4)):
            plan[name] = (n_, a_, units)
            n_ += units
            a_ += accs
        UNITS = n_

        def pairs(eng, units, body, peel=0):
            for i in range(min(peel, units // 2)):
                body(2 * i, 0)
                body(2 * i + 1, 1)
            if units // 2 > peel:
                with eng.Fori(peel, units // 2) as i:
                    body(2 * i, 0)
                    body(2 * i + 1, 1)
            if units % 2:
                body(units - 1, 0)

        last_a = a_

        def wview(w):
            return w.rearrange("(k p) n -> p k n", p=P)

        W1 = wview(A["w_in"][0])
        E_IN, O_IN = wview(A["e_w_in_2"][0]), wview(A["o_w_in_2"][0])
        raw3 = raw[:, :, :].rearrange("p s (k c) -> p s k c", k=KT)

        def tr_bank(k):
            return aux[:, k % 4, :]

        def first_bank(k):
            return acc[:, k, :] if k < 4 else aux[:, k - 4, :]

        def logit_bank(i):
            return acc[:, 2 + i % 2, :]

        def trans_bank(i):
            return aux[:, i % 2, :]

        def out_bank(i):
            return aux[:, 2 + i % 2, :]

        JOBS = [[], []]
        for j in range(A_HEADS // 2):
            for t in range(TT):
                for kv in range(2):
                    h = j + kv * (A_HEADS // 2)
                    k0 = max(t - 1, 0)
                    JOBS[0].append(Job(t, k0, P * (t + 1 - k0), (j, HD2 * kv), (3, HD2 * kv),
                                       ("window", h, SLOPES[h]), HD2 * kv, h, HD2 * h, kv))
        for j in range(B_HEADS // 2):
            for t in range(TT):
                for e in range(2):
                    h = 2 * j + e
                    JOBS[0].append(Job(t, 0, P * (t + 1), (4 + j, HD2 * e), (7 + j, HD2 * e),
                                       ("dist", A_HEADS + h, SLOPES[A_HEADS + h]), P + HD2 * h, None,
                                       HD2 * (A_HEADS + h), e))
        for j in range(C_HEADS // 2):
            for t in range(TT):
                for e in range(2):
                    h = 2 * j + e
                    JOBS[1].append(Job(t, 0, P * (t + 1), (j, HD2 * e), (6 + j, HD2 * e), ("forget", h, 1.0),
                                       HD2 * h, None, HD2 * h, h % 4))
        for L, q0 in enumerate((10, 12)):
            for j in range(M_HEADS // 2):
                for t in range(TT):
                    for e in range(2):
                        h = 2 * j + e
                        JOBS[L].append(Job(t, 0, MEM, (q0 + j, HD2 * e), (j, HD2 * e), None,
                                           HD2 * h, None, HD2 * (C_HEADS + h), e))
        assert len(JOBS[0]) == len(JOBS[1]) == 4 * 2 * KT

        def z_due(i):
            return i // KT - 1 if i >= KT and i % KT == 1 and i // KT <= KT else None

        @block.sync
        def _(sp):
            def slot_free(n):
                if isinstance(n, int) and n < 2:
                    return
                sp.wait_ge(w_split, n - 1)

            def load(view, col, n, slot):
                slot_free(n)
                for kh in range(2):
                    sp.dma_start(raw3[:, slot, 4 * kh:4 * kh + 4, :],
                                 view[:, 4 * kh:4 * kh + 4, bass.ds(col, UC)]).then_inc(w_loaded[slot], 16)

            def stage(name, view, col0, step=UC, peel=0):
                n0, _, units = plan[name]
                pairs(sp, units, lambda u, q: load(view, u * step + col0, u + n0, (n0 + q) % 2), peel)

            def halves(n, view, cols):
                slot_free(n)
                for half, col in enumerate(cols):
                    dst = raw3[:, n % 2, :, P * half:P * half + P]
                    if isinstance(col, tuple):
                        for part, c in enumerate(col):
                            sp.dma_start(dst[:, :, HD2 * part:HD2 * part + HD2],
                                         view[:, :, c:c + HD2]).then_inc(w_loaded[n % 2], 16)
                    else:
                        sp.dma_start(dst, view[:, :, col:col + P]).then_inc(w_loaded[n % 2], 16)

            def narrow(n, view, col, width):
                slot_free(n)
                dst = raw[:, n % 2, 0:KT * width].rearrange("p (k c) -> p k c", k=KT)
                for kh in range(2):
                    sp.dma_start(dst[:, 4 * kh:4 * kh + 4, :],
                                 view[:, 4 * kh:4 * kh + 4, col:col + width]).then_inc(w_loaded[n % 2], 16)

            xv = A["x"][0].rearrange("(t p) d -> p t d", p=P)
            for t in range(0, TT, 2):
                sp.dma_start(xrow[:, t, :], xv[:, t, :]).then_inc(x_in[t], 16)
            narrow(0, W1, COL_GATES, 16)
            stage("u", W1, COL_U, peel=1)
            stage("za", W1, COL_ZA)
            n = plan["mix"][0]
            slot_free(n)
            mixw = A["pool_mix_w"][0].rearrange("g (kk p) n -> p (g kk) n", p=P)
            for kh in range(2):
                sp.dma_start(raw3[:, n % 2, 4 * kh:4 * kh + 4, :], mixw[:, 4 * kh:4 * kh + 4, :]).then_inc(w_loaded[n % 2], 16)
            stage("ga", W1, COL_GA)
            stage("pa", wview(A["w_proj_pool"][0]), 0)
            stage("qk", W1, COL_QK)
            stage("v", W1, COL_V)
            n = plan["ozb"][0]
            with sp.Fori(0, HEADS) as h:
                load(W1, h * UC + COL_O, 2 * h + n, n % 2)
                load(W1, h * UC + COL_ZB, 2 * h + n + 1, (n + 1) % 2)
            stage("gb", W1, COL_GB)
            stage("pb", wview(A["w_proj_mlstm"][0]), 0)
            stage("wout", wview(A["w_out"][0]), 0)

            stage("e_mem", wview(A["e_w_mem_kv_2"][0]), 0)
            n = plan["e_qk"][0]
            AQ, AK, AV, BQ, BK, BV, MQ, Z = E_COLS
            tiles = [(AQ + HD2 * j, AQ + HD2 * (j + 3)) for j in range(3)] + [AK]
            tiles += [BQ + P * j for j in range(3)] + [BK + P * j for j in range(3)] + [MQ, MQ + P]
            for u in range(6):
                halves(n + u, E_IN, tiles[2 * u:2 * u + 2])
            halves(plan["e_v"][0], E_IN, [AV, BV])
            halves(plan["e_v"][0] + 1, E_IN, [BV + P, BV + 2 * P])
            stage("e_z", E_IN, Z)
            stage("e_out", wview(A["e_w_out_2"][0]), 0)

            stage("o_mem", wview(A["o_w_mem_kv_2"][0]), 0)
            CQ, CK, CV, CF, MQ, Z = O_COLS
            narrow(plan["o_f"][0], O_IN, CF, C_HEADS)
            n = plan["o_qk"][0]
            for u in range(6):
                load(O_IN, CQ + UC * u, n + u, (n + u) % 2)
            load(O_IN, MQ, n + 6, (n + 6) % 2)
            n0 = plan["o_v"][0]
            for u in range(3):
                load(O_IN, CV + UC * u, n0 + u, (n0 + u) % 2)
            sp.wait_ge(negc_ready, 1)
            sp.dma_start(negc_dram, negc[0:C_HEADS, :]).then_inc(negc_out, 16)
            sp.wait_ge(negc_out, 16)

            def spread(h):
                if h >= 4:
                    last = max(i for i, job in enumerate(JOBS[1]) if job.bias is not None and job.bias[1] == h - 4)
                    sp.wait_ge(nm_ready, len(JOBS[0]) + last + 1)
                sp.dma_start(negc_all[:, h % 4, :], negc_dram[h:h + 1, :].to_broadcast([P, S])).then_inc(negc_in[h % 4], 16)
            for h in range(4):
                spread(h)
            for u in range(4):
                n = plan["o_z"][0] + u
                load(O_IN, Z + UC * u, n, n % 2)
                for h in (4 + 2 * u, 5 + 2 * u):
                    spread(h)
            stage("o_out", wview(A["o_w_out_2"][0]), 0)

            outv = out[0].rearrange("(t p) d -> p t d", p=P)
            for u in range(4):
                sp.wait_ge(acc_free, plan["o_out"][1] + u + 1)
                sp.dma_start(outv[:, :, UC * u:UC * u + UC], xrow[:, :, UC * u:UC * u + UC]).then_inc(stored, 16)
            sp.wait_ge(stored, 64)

        @block.gpsimd
        def _(pool):
            step = Steps(pool, pool_step)

            def split(n, slot, round_, a_before, extra=0):
                pool.wait_ge(w_loaded[slot], round_ * 32 + 32 + extra)
                if a_before is not None:
                    pool.wait_ge(acc_ready, a_before * 2 + 2)
                pool.sem_inc(units_begun, 1)
                nc.gpsimd.tensor_scalar(whi[:, slot, :], raw[:, slot, :], 1.0, 1.0, ALU.mult, ALU.mult).then_inc(w_hi, 1)
                pool.wait_ge(w_hi, n + 1)
                nc.gpsimd.tensor_tensor(wlo[:, slot, :], raw[:, slot, :], whi[:, slot, :].bitcast(F32),
                                        ALU.subtract).then_inc(w_split, 1)

            def split_narrow(n, a_before, width, groups, extra=0):
                slot = n % 2
                pool.wait_ge(w_loaded[slot], 32 * (n // 2 + 1) + extra)
                if a_before is not None:
                    pool.wait_ge(acc_ready, 2 * (a_before + 1))
                nc.gpsimd.memset(whi[:, slot, 0:KT * P].bitcast(F32), 0.0)
                step(nc.gpsimd.memset(wlo[:, slot, 0:KT * P].bitcast(F32), 0.0))
                src = raw[:, slot, 0:KT * width].rearrange("p (k c) -> p k c", k=KT)
                hi = whi[:, slot, 0:KT * P].rearrange("p (k c) -> p k c", k=KT)
                lo = wlo[:, slot, 0:KT * P].rearrange("p (k c) -> p k c", k=KT)
                for g, (c, d, w) in enumerate(groups):
                    ins = nc.gpsimd.tensor_copy(hi[:, :, d:d + w], src[:, :, c:c + w])
                    if g == len(groups) - 1:
                        ins.then_inc(w_hi, 1)
                pool.wait_ge(w_hi, n + 1)
                for g, (c, d, w) in enumerate(groups):
                    ins = nc.gpsimd.tensor_tensor(lo[:, :, d:d + w], src[:, :, c:c + w],
                                                  hi[:, :, d:d + w].bitcast(F32), ALU.subtract)
                    if g == len(groups) - 1:
                        ins.then_inc(w_split, 1)

            split_narrow(0, None, 16, [(8 * d + 4 * kind, 64 * kind + 32 * d, 4) for d in range(2) for kind in range(2)])
            mix = plan["mix"][0]
            split(1, 1, 0, None)
            split(2, 0, 1, 0)
            with pool.Fori(0, (mix - 3) // 2) as i:
                split(2 * i + 3, 1, i + 1, 2 * i + 1)
                split(2 * i + 4, 0, i + 2, 2 * i + 2)
            assert mix % 2
            for n in (mix, mix + 1):
                split(n, n % 2, n // 2, n - 2)

            def run(lo, hi, extra):
                def one(i, d):
                    split(2 * i + lo + d, (lo + d) % 2, i + (lo + d) // 2, 2 * i + lo + d + 1, extra[(lo + d) % 2])
                if (hi - lo) // 2:
                    with pool.Fori(0, (hi - lo) // 2) as i:
                        one(i, 0)
                        one(i, 1)
                if (hi - lo) % 2:
                    one((hi - lo) // 2, 0)
            eqk, n = plan["e_qk"][0], plan["o_f"][0]
            assert eqk % 2 == 0
            run(mix + 2, eqk, (0, 0))
            run(eqk, eqk + 1, (32, 0))
            run(eqk + 1, n, (32, 16))
            split_narrow(n, n + 1, C_HEADS, [(0, 0, C_HEADS)], (32, 16)[n % 2])
            run(n + 1, UNITS, (32, 16))

        @block.scalar
        def _(act):
            step = Steps(act, act_step)
            xv = A["x"][0].rearrange("(t p) d -> p t d", p=P)
            for t in range(1, TT, 2):
                act.dma_start(xrow[:, t, :], xv[:, t, :]).then_inc(x_in[t], 16)
            act.dma_start(ident[:], consts_d[:, 0:P]).then_inc(ident_in, 16)
            act.dma_start(vecs[:], vecs_d).then_inc(vecs_in, 16)
            act.dma_start(bones[:], consts_d[:, P:2 * P]).then_inc(consts_in, 16)
            act.dma_start(masks1[:], consts_d[:, 2 * P:2 * P + 2 * S].rearrange("p (a c) -> p a c", a=2)).then_inc(consts_in, 16)

            seen = {"rssq": 0, "rvar": 0, "tr": 0, "hi": 0, "hn": 0, "exp": 0}

            def squares(src, dst, tiles, col, wait):
                for t in range(tiles):
                    wait(t)
                    nc.scalar.activation(dst[:, t, :], src[:, t, :], ACT.Square,
                                         accum_out=small[:, col + t:col + t + 1]).then_inc(rssq_ready, 1)
                    if t:
                        root(col + t - 1)
                root(col + tiles - 1)

            def root(c):
                seen["rvar"] += 1
                act.wait_ge(rvar_ready, seen["rvar"])
                nc.scalar.activation(small[:, c:c + 1], small[:, c:c + 1], ACT.Sqrt).then_inc(rsd_ready, 1)

            def heads_of_transposes(gain, dst, cols, bank=tr_bank):
                for k in range(KT):
                    seen["tr"] += 1
                    act.wait_ge(tr_ready, seen["tr"])
                    nc.scalar.activation(dst[:, k, :], bank(k)[:, 0:cols], ACT.Copy,
                                         scale=V(gain, k)).then_inc(tr_hi, 1)

            def head(src, dst):
                seen["hi"] += 1
                act.wait_ge(t_ready, seen["hi"])
                nc.scalar.activation(dst, src, ACT.Copy).then_inc(hi_ready, 1)

            def evac(a, s, half, dst, func, **kw):
                act.wait_ge(acc_ready, a * 2 + 1 + half)
                ins = nc.scalar.activation(dst, acc[:, 2 * s + half:2 * s + half + 1, :], func, **kw)
                if half:
                    ins.then_inc(acc_free, 1)

            def stage(name, dst, func, bias=None, peel=0):
                _, a0, units = plan[name]
                act.wait_ge(acc_free, a0)

                def body(u, q):
                    for half in range(2):
                        kw = {} if bias is None else {"bias": Vd(*bias, u * 2 + half)} if len(bias) == 1 else \
                            {"bias": Vd(bias[0], u * 2 + half + bias[1])}
                        evac(u + a0, (a0 + q) % 2, half, dst[:, bass.ds(u * 2 + half, 1), :], func, **kw)
                pairs(act, units, body, peel)

            squares(xrow, xnrow, TT, 0, lambda t: act.wait_ge(x_in[t], 16))
            act.wait_ge(vecs_in, 16)
            heads_of_transposes("pre_g", ht_hi, S, first_bank)

            def softplus_of_minus_abs(src, tmp):
                step(nc.scalar.activation(tmp, src, ACT.Abs))
                step(nc.scalar.activation(tmp, tmp, ACT.Exp, scale=-1.0))
                nc.scalar.activation(tmp, tmp, ACT.Ln, bias=1.0).then_inc(gate_exp, 1)
            act.wait_ge(gate_rows, 1)
            softplus_of_minus_abs(grow[0:64, 1, :], grow[0:64, 2, :])

            _, a0, units = plan["u"]
            act.wait_ge(acc_free, a0)
            for u in range(units):
                for half in range(2):
                    evac(a0 + u, (a0 + u) % 2, half, uT[:, 2 * u + half:2 * u + half + 1, PAD:PAD + S], ACT.Copy)
                if u:
                    for j in (2 * u - 2, 2 * u - 1):
                        head(win_t[:, j % 4, :], op_hi[:, j, :])
            for j in (2 * units - 2, 2 * units - 1):
                head(win_t[:, j % 4, :], op_hi[:, j, :])
            act.wait_ge(gmT_ready, 1)
            act.wait_ge(gcol_ready, 1)
            gmT = aux[:, 3, :].rearrange("p (t k d r) -> p t k d r", t=TT, k=2, d=2)
            for d in range(2):
                nc.scalar.activation(floorc[:, :, d, :], gmT[:, :, 1, d, 0:HEADS], ACT.Exp, scale=-1.0).then_inc(floor_ready, 1)

            stage("za", zaT, ACT.Silu)
            for j in range(KT):
                head(win_t[:, j % 4, :], op_hi[:, j, :])
            stage("ga", mergedT, ACT.Sigmoid, ("b_merge", 0))

            _, a0, units = plan["qk"]

            def qk_body(u, q, first=False):
                for half in range(2):
                    slot = 2 * q + half
                    if not first:
                        act.wait_ge(conv_ready, u * 2 + half - 3)
                    evac(u + a0, (a0 + q) % 2, half, cpad[:, slot:slot + 1, 2:2 + S], ACT.Copy)

            def qk_silu(u, q):
                for half in range(2):
                    slot = 2 * q + half
                    act.wait_ge(conv_ready, u * 2 + half + 1)
                    nc.scalar.activation(qkT[:, bass.ds(u * 2 + half, 1), :], cacc[:, slot:slot + 1, :], ACT.Silu,
                                         bias=Vd("conv_b", u * 2 + half)).then_inc(silu_ready, 1)
            act.wait_ge(lo_ready, 16)
            act.wait_ge(acc_free, a0)
            qk_body(0, 0, True)
            qk_body(1, 1, True)
            qk_silu(0, 0)
            with act.Fori(1, units // 2) as i:
                qk_body(2 * i, 0)
                qk_silu(2 * i - 1, 1)
                qk_body(2 * i + 1, 1)
                qk_silu(2 * i, 0)
            qk_silu(units - 1, 1)

            _, a0, units = plan["v"]

            def v_body(u, q):
                s = (a0 + q) % 2
                for half in range(2):
                    act.wait_ge(acc_ready, u * 2 + 2 * a0 + 1 + half)
                    ins = nc.scalar.activation(vrow[:, 2 * half:2 * half + 2, bass.ds(u * VW, HD)],
                                               acc[:, 2 * s + half, :].rearrange("p (t c) -> p t c", t=2), ACT.Copy)
                    if half:
                        ins.then_inc(acc_free, 1)
            pairs(act, units, v_body)

            def decays():
                for j in range(TT):
                    for d in range(2):
                        n = seen["exp"]
                        seen["exp"] += 1
                        w = S - P * j if d == 0 else P * (j + 1)
                        act.wait_ge(arg_ready, n + 1)
                        tile = decay[:, n % 4, 0:w]
                        nc.scalar.activation(tile, tile, ACT.Exp, scale=-1.0).then_inc(d_ready, 1)

            _, a0, _ = plan["ozb"]
            decays()
            for h in range(HEADS):
                a = a0 + 2 * h
                act.wait_ge(acc_free, a)
                for half in range(2):
                    evac(a, a % 2, half, ogT[:, 2 * h + half:2 * h + half + 1, :], ACT.Sigmoid)
                for t in range(TT):
                    i = TT * h + t
                    b = 2 * (t % 2)
                    act.wait_ge(pv_ready, i + 1)
                    nc.scalar.activation(small[:, 16 + 2 * (t % 2):18 + 2 * (t % 2)], aux[:, b:b + 2, HD],
                                         ACT.Abs).then_inc(den_ready, 1)
                    act.wait_ge(rden_ready, i + 1)
                    nc.scalar.activation(hfwd[:, t % 2, :], aux[:, b, 0:HD], ACT.Copy,
                                         scale=small[:, 16 + 2 * (t % 2):17 + 2 * (t % 2)]).then_inc(hf_ready, 1)
                    act.wait_ge(hb_ready, i + 1)
                    nc.scalar.activation(hsq[:], hrow[:, t, :], ACT.Square,
                                         accum_out=small[:, t:t + 1]).then_inc(hssq_ready, 1)
                act.wait_ge(hssq_ready, TT * (h + 1))
                step(nc.scalar.activation(small[:, 4:8], small[:, 0:4], ACT.Ln, scale=1.0 / HD, bias=V("eps")))
                nc.scalar.activation(small[:, 8:12], small[:, 4:8], ACT.Exp, scale=-0.5).then_inc(hrs_ready, 1)
                if h + 1 < HEADS:
                    decays()
                a += 1
                for half in range(2):
                    act.wait_ge(acc_ready, 2 * a + 1 + half)
                    bank = acc[:, 2 * (a % 2) + half, :]
                    nc.scalar.activation(bank, bank, ACT.Silu).then_inc(zb_ready, 1)
            for j in range(KT):
                head(ogT[:, j, :], op_hi[:, j, :])
            memv = A["mem_2"][0].rearrange("(t p) d -> p t d", p=P)
            act.dma_start(memrow[:], memv).then_inc(mem_in, 16)
            act.dma_start(masks2[:], consts_d[:, 2 * P + 2 * S:]).then_inc(masks2_in, 16)
            stage("gb", gbT, ACT.Sigmoid, ("b_merge", KT))
            squares(memrow, memn, MT, 20, lambda t: act.wait_ge(mem_in, 16))
            for j in range(KT):
                head(mergedT[:, j, :], ht_hi[:, j, :])

            act.dma_start(xagain[:], xv).then_inc(post_in, 16)
            act.dma_start(gpost[:], A["norm_post_g"][0:1, :].to_broadcast([P, D])).then_inc(post_in, 16)
            heads_of_transposes("e_mem", memT_hi, MEM)
            _, a0, units = plan["wout"]
            act.wait_ge(acc_free, a0)

            def wout_body(u, q):
                s = (a0 + q) % 2
                for half in range(2):
                    act.wait_ge(acc_ready, u * 2 + 2 * a0 + 1 + half)
                    ins = nc.scalar.activation(orow1[:, 2 * half:2 * half + 2, bass.ds(u * UC, UC)],
                                               acc[:, 2 * s + half, :].rearrange("p (t c) -> p t c", t=2), ACT.Copy)
                    if half:
                        ins.then_inc(acc_free, 1)
                act.wait_ge(acc_free, u + a0 + 1)
                for t in range(TT):
                    nc.scalar.activation(junk[:, UC * t:UC * t + UC], orow1[:, t, bass.ds(u * UC, UC)], ACT.Square,
                                         accum_out=stats[:, 5, bass.ds(u + units * t, 1)]).then_inc(post_ssq, 1)
            for u in range(units):
                if u:
                    act.wait_ge(post_ssq, TT * u)
                wout_body(u, u % 2)
            act.wait_ge(post_var, 1)
            nc.scalar.activation(small[:, 0:4], small[:, 0:4], ACT.Sqrt).then_inc(post_sd, 1)

            def head_norm_squares(a, half, cols, ahead=0):
                n = seen["hn"] + ahead + half
                act.wait_ge(acc_ready, 2 * a + 1 + half)
                if n >= 2:
                    act.wait_ge(sq_split, n - 1)
                nc.scalar.activation(hn_sq[:, n % 2, 0:cols], acc[:, 2 * (a % 2) + half, 0:cols], ACT.Square).then_inc(sq_ready, 1)

            def head_norm_rsqrt(cols):
                n0 = seen["hn"]
                for n in (n0, n0 + 1):
                    act.wait_ge(ssq_ready, n + 1)
                    if n >= 2:
                        act.wait_ge(hn_done, n - 1)
                    nc.scalar.activation(hn_rs[:, n % 2, 0:cols], aux[:, n % 2, 0:cols], ACT.Ln, scale=1.0 / HD2,
                                         bias=V("eps")).then_inc(ln_done, 1)
                for n in (n0, n0 + 1):
                    act.wait_ge(ln_done, n + 1)
                    nc.scalar.activation(hn_rs[:, n % 2, 0:cols], hn_rs[:, n % 2, 0:cols], ACT.Exp, scale=-0.5).then_inc(rs_ready, 1)
                seen["hn"] += 2

            def value_rows(a, dst, tiles, u):
                act.wait_ge(acc_free, a)
                for half in range(2):
                    act.wait_ge(acc_ready, 2 * a + 1 + half)
                    src = acc[:, 2 * (a % 2) + half, :]
                    if tiles == TT:
                        ins = nc.scalar.activation(dst[:, 2 * half:2 * half + 2, UC * u:UC * u + UC],
                                                   src.rearrange("p (t c) -> p t c", t=2), ACT.Copy)
                    else:
                        ins = nc.scalar.activation(dst[:, half, :], src[:, 0:UC], ACT.Copy)
                    if half:
                        ins.then_inc(acc_free, 1)

            jobs_done = 0
            for L, name in enumerate("eo"):
                qk, vv = LAYERS[L]
                squares(xrow, xnrow, TT, 0,
                        lambda t: act.wait_ge(*((x_rows, t + 1) if L == 0 else (acc_free, plan["e_out"][1] + 4))))
                _, a0, _ = plan[name + "_mem"]
                for half in range(2):
                    head_norm_squares(a0, half, MEM)
                value_rows(a0 + 1, mv, MT, 0)
                heads_of_transposes(name + "_norm", ht_hi, S)
                head_norm_rsqrt(MEM)
                if L:
                    act.wait_ge(gate_rows, 2)
                    softplus_of_minus_abs(frow[0:C_HEADS, 0, :], frow[0:C_HEADS, 1, :])
                _, a0, units = plan[name + "_qk"]
                for u in range(units):
                    for half in range(2):
                        head_norm_squares(a0 + u, half, S, 2 if u else 0)
                    if u:
                        head_norm_rsqrt(S)
                _, a0, units = plan[name + "_v"]
                for u in range(units):
                    value_rows(a0 + u, vv, TT, u)
                    if u == 0:
                        head_norm_rsqrt(S)
                az = plan[name + "_z"][1]

                jobs = JOBS[L]
                for i in range(len(jobs) + 3):
                    if L == 0 and i == 52:
                        act.dma_start(memrow[:], memv).then_inc(mem_in, 16)
                    if i < len(jobs):
                        job = jobs[i]
                        g = jobs_done + i
                        act.wait_ge(nm_ready, g + 1)
                        src = logit_bank(i)[:, 0:job.keys] if job.bias is None else sc[:, i % 3, 0:job.keys]
                        if g >= 3:
                            act.wait_ge(prT_ready, g - 2)
                        nc.scalar.activation(pr[:, i % 3, 0:job.keys], src, ACT.Exp, bias=stats[:, 1, i:i + 1],
                                             accum_out=stats[:, 2, i:i + 1]).then_inc(pr_ready, 1)
                        if job.sink is not None:
                            nc.scalar.activation(stats[:, 3, i:i + 1], V("sinks", job.sink), ACT.Exp,
                                                 bias=stats[:, 1, i:i + 1]).then_inc(es_ready, 1)
                    if i >= 3:
                        k = i - 3
                        act.wait_ge(o_ready, jobs_done + k + 1)
                        act.wait_ge(ri_ready, jobs_done + k + 1)
                        nc.scalar.activation(arow[:, jobs[k].t, jobs[k].col:jobs[k].col + HD2], out_bank(k)[:, 0:HD2],
                                             ACT.Copy, scale=stats[:, 4, k:k + 1]).then_inc(o_done, 1)
                    if z_due(i) is not None:
                        hu = z_due(i)
                        act.wait_ge(acc_ready, 2 * az + hu + 1)
                        nc.scalar.activation(zT[:, hu, :], acc[:, hu % 2, :], ACT.Tanh, scale=0.5).then_inc(th_ready, 1)
                jobs_done += len(jobs)
                for j in range(KT):
                    head(zT[:, j, :], ht_hi[:, j, :])
                if L == 0:
                    squares(memrow, memn, MT, 20, lambda t: act.wait_ge(mem_in, 32))
                    heads_of_transposes("o_mem", memT_hi, MEM)

        @block.vector
        def _(dve):
            step = Steps(dve, dve_step)
            seen = {"rssq": 0, "rsd": 0, "tr": 0, "t": 0, "lo": 0, "hn": 0, "arg": 0, "aT": 0}
            v = nc.vector

            def normalise(src, dst, tiles, col):
                for t in range(tiles):
                    c = small[:, col + t:col + t + 1]
                    seen["rssq"] += 1
                    dve.wait_ge(rssq_ready, seen["rssq"])
                    v.tensor_scalar(c, c, 1.0 / D, EPS, ALU.mult, ALU.add).then_inc(rvar_ready, 1)
                    if t:
                        scale_rows(src, dst, t - 1, col)
                scale_rows(src, dst, tiles - 1, col)

            def scale_rows(src, dst, t, col):
                c = small[:, col + t:col + t + 1]
                seen["rsd"] += 1
                dve.wait_ge(rsd_ready, seen["rsd"])
                step(v.reciprocal(c, c))
                v.tensor_scalar(dst[:, t, :], src[:, t, :], c, None, ALU.mult).then_inc(xn_ready, 1)

            def rests_of_transposes(gain, hi, lo, cols, bank=tr_bank):
                for k in range(KT):
                    seen["tr"] += 1
                    dve.wait_ge(tr_hi, seen["tr"])
                    v.scalar_tensor_tensor(lo[:, k, :], bank(k)[:, 0:cols], V(gain, k),
                                           hi[:, k, :].bitcast(F32), ALU.mult, ALU.subtract).then_inc(tr_lo, 1)

            def rest(src, hi, lo):
                seen["lo"] += 1
                dve.wait_ge(hi_ready, seen["lo"])
                v.tensor_tensor(lo, src, hi.bitcast(F32), ALU.subtract).then_inc(lo_ready, 1)

            def tile_written(ins):
                ins.then_inc(t_ready, 1)
                seen["t"] += 1

            v.memset(uT[:, :, 0:PAD], 0.0)
            step(v.memset(uT[:, :, PAD + S:UW], 0.0))
            normalise(xrow, xnrow, TT, 0)
            dve.wait_ge(vecs_in, 16)
            rests_of_transposes("pre_g", ht_hi, ht_lo, S, first_bank)

            G = lambda i, lo=0, hi=64: grow[lo:hi, i, :]
            dve.wait_ge(acc_ready, 2)
            v.tensor_scalar(G(0), acc[0:64, 0, :], vecs[0:64, VC["b_i"]:VC["b_i"] + 1], None, ALU.add)
            v.tensor_copy(G(1), acc[64:128, 0, :]).then_inc(acc_free, 1)
            dve.wait_ge(acc_free, 1)
            v.tensor_scalar(G(1), G(1), vecs[0:64, VC["b_f"]:VC["b_f"] + 1], None, ALU.add).then_inc(gate_rows, 1)
            dve.wait_ge(gate_rows, 1)
            dve.wait_ge(gate_exp, 1)
            step(v.scalar_tensor_tensor(G(1), G(1), 0.0, G(2), ALU.min, ALU.subtract))
            step(v.tensor_tensor_scan(G(3), G(1), G(1), 0.0, ALU.add, ALU.bypass))
            v.tensor_copy(G(4, 0, 32), G(3, 0, 32))
            step(v.tensor_tensor(G(4, 32, 64), G(1, 32, 64), G(3, 32, 64), ALU.subtract))
            step(v.tensor_tensor(G(5), G(0), G(4), ALU.subtract))
            v.tensor_tensor_scan(rowmax[0:32, :], G(5, 0, 32), G(5, 0, 32), FLOOR, ALU.max, ALU.bypass)
            back = G(5, 32, 64)[:, ::-1]
            step(v.tensor_tensor_scan(rowmax[32:64, ::-1], back, back, FLOOR, ALU.max, ALU.bypass))
            v.tensor_tensor(G(5, 64, 128), G(4), rowmax[:], ALU.add).then_inc(gm_ready, 1)

            _, a0, units = plan["u"]
            for g, w in enumerate(WINDOWS):
                dve.wait_ge(acc_free, a0 + g + 1)
                for j in (2 * g, 2 * g + 1):
                    u = uT[:, j, :]
                    src, margin = u, 1
                    step(v.tensor_tensor(win_s[:, 0, 1:UW], u[:, 0:UW - 1], u[:, 1:UW], ALU.add))
                    cur, lo, hi, shift = 0, 1, UW, 1
                    while 2 * shift < w:
                        lo, hi = lo + shift, hi - shift
                        step(v.tensor_tensor(win_s[:, 1 - cur, lo:hi], win_s[:, cur, lo - shift:hi - shift],
                                             win_s[:, cur, lo + shift:hi + shift], ALU.add))
                        cur, shift = 1 - cur, 2 * shift
                    sums = win_s[:, cur, PAD:PAD + S]
                    ends = sums.rearrange("p (b c) -> p b c", c=PAD)[:, 0:S // PAD:S // PAD - 1, :]
                    edge = V("edge", 2 * PAD * g, 2 * PAD).rearrange("p (b c) -> p b c", c=PAD)
                    step(v.tensor_tensor(ends, ends, edge, ALU.mult))
                    if j >= 4:
                        dve.wait_ge(hi_ready, j - 3)
                    tile_written(v.scalar_tensor_tensor(win_t[:, j % 4, :], sums, 1.0 / w, u[:, PAD:PAD + S],
                                                        ALU.mult, ALU.subtract))
                    dve.wait_ge(t_ready, seen["t"])
                    if j:
                        rest(win_t[:, (j - 1) % 4, :], op_hi[:, j - 1, :], op_lo[:, j - 1, :])
            rest(win_t[:, (KT - 1) % 4, :], op_hi[:, KT - 1, :], op_lo[:, KT - 1, :])
            dve.wait_ge(gmT_ready, 1)
            gmT = aux[:, 3, :].rearrange("p (t k d r) -> p t k d r", t=TT, k=2, d=2)
            for d in range(2):
                ins = v.tensor_copy(gcol[:, :, d, :], gmT[:, :, 0, d, 0:HEADS])
            ins.then_inc(gcol_ready, 1)

            for name, j in (("e_qk", 0), ("e_qk", 2), ("e_qk", 4), ("o_qk", 0), ("o_qk", 2)):
                step(v.tensor_scalar(V(name, j), V(name, j), HD2 ** -0.5, None, ALU.mult))

            _, a0, _ = plan["mix"]
            dve.wait_ge(acc_free, a0)
            for g in range(4):
                s = (a0 + g) % 2
                dve.wait_ge(acc_ready, 2 * (a0 + g + 1))
                for half in range(2):
                    j = 2 * g + half
                    dve.wait_ge(hi_ready, 8 + j - 3)
                    tile_written(v.scalar_tensor_tensor(win_t[:, j % 4, :], acc[:, 2 * s + half, :], V("pool_scale", j),
                                                        zaT[:, j, :], ALU.mult, ALU.mult))
                dve.wait_ge(t_ready, seen["t"])
                dve.sem_inc(acc_free, 1)
                for j in (2 * g, 2 * g + 1):
                    rest(win_t[:, j % 4, :], op_hi[:, j, :], op_lo[:, j, :])

            _, a0, units = plan["pa"]
            dve.wait_ge(acc_free, a0)

            def pa_body(u, q):
                for half in range(2):
                    dve.wait_ge(acc_ready, u * 2 + 2 * a0 + 1 + half)
                    m = mergedT[:, bass.ds(u * 2 + half, 1), :]
                    b = 2 * ((a0 + q) % 2) + half
                    ins = v.tensor_tensor(m, acc[:, b:b + 1, :], m, ALU.mult)
                    if half:
                        ins.then_inc(acc_free, 1)
            pairs(dve, units, pa_body)

            _, a0, units = plan["qk"]
            dve.wait_ge(acc_free, a0)
            v.memset(cpad[:, :, 0:2], 0.0)
            step(v.memset(cpad[:, :, 2 + S:CW], 0.0))

            def conv(u, q, first=False):
                dve.wait_ge(acc_free, u + a0 + 1)
                for half in range(2):
                    slot = 2 * q + half
                    if not first:
                        dve.wait_ge(silu_ready, u * 2 + half - 3)
                    out_ = cacc[:, slot, :]
                    tap = lambda k: Vd("conv_w", u * (2 * TAPS) + half * TAPS + k)
                    step(v.tensor_scalar(out_, cpad[:, slot, 0:S], tap(0), None, ALU.mult))
                    for k in range(1, TAPS):
                        ins = v.scalar_tensor_tensor(out_, cpad[:, slot, k:k + S], tap(k), out_, ALU.mult, ALU.add)
                        if k < TAPS - 1:
                            step(ins)
                        else:
                            ins.then_inc(conv_ready, 1)
            conv(0, 0, True)
            conv(1, 1, True)

            def conv_pair(i):
                conv(2 * i + 2, 0)
                conv(2 * i + 3, 1)
            step.loop(units // 2 - 1, 4 * (TAPS - 1), conv_pair)
            step(v.memset(vrow[:, :, :].rearrange("p t (h c) -> p t h c", h=HEADS)[:, :, :, HD:VW], 1.0))

            def decay_args(h, j):
                if TT * h + j >= 2:
                    dve.wait_ge(p_ready, TT * h + j - 1)
                for d in range(2):
                    lo, hi = (P * j, S) if d == 0 else (0, P * (j + 1))
                    w = hi - lo
                    dve.wait_ge(mbc_ready, h + 1)
                    mask = masks1[:, 0, 0:w] if d == 0 else masks1[:, 1, S - w:S]
                    v.scalar_tensor_tensor(decay[:, seen["arg"] % 4, 0:w], aux[:, d, lo:hi], gcol[:, j, d, h:h + 1],
                                           mask, ALU.subtract, ALU.max).then_inc(arg_ready, 1)
                    seen["arg"] += 1

            def probabilities(h):
                if h:
                    dve.wait_ge(pv_ready, TT * h)
                decay_args(h, 0)
                for j in range(TT):
                    if j + 1 < TT:
                        decay_args(h, j + 1)
                    dve.wait_ge(s_ready, TT * h + j + 1)
                    for d in range(2):
                        n = 2 * (TT * h + j) + d
                        lo, hi = (P * j, S) if d == 0 else (0, P * (j + 1))
                        dve.wait_ge(d_ready, n + 1)
                        ins = v.scalar_tensor_tensor(prob[:, d, j, lo:hi], aux[:, 2 + j % 2, lo:hi], HD ** -0.5,
                                                     decay[:, n % 4, 0:hi - lo], ALU.mult, ALU.mult)
                    ins.then_inc(p_ready, 1)

            dve.wait_ge(consts_in, 32)
            probabilities(0)
            _, a0, _ = plan["ozb"]
            for h in range(HEADS):
                for t in range(TT):
                    i = TT * h + t
                    b = 2 * (t % 2)
                    c = 16 + 2 * (t % 2)
                    dve.wait_ge(den_ready, i + 1)
                    if i == 0:
                        dve.wait_ge(floor_ready, 2)
                    step(v.tensor_tensor(small[:, c:c + 2], small[:, c:c + 2], floorc[:, t, :, h], ALU.max))
                    v.reciprocal(small[:, c:c + 2], small[:, c:c + 2]).then_inc(rden_ready, 1)
                    dve.wait_ge(rden_ready, i + 1)
                    dve.wait_ge(hf_ready, i + 1)
                    v.scalar_tensor_tensor(hrow[:, t, :], aux[:, b + 1, 0:HD], small[:, c + 1:c + 2], hfwd[:, t % 2, :],
                                           ALU.mult, ALU.add).then_inc(hb_ready, 1)
                dve.wait_ge(hrs_ready, h + 1)
                for t in range(TT):
                    ins = v.tensor_scalar(hrow[:, t, :], hrow[:, t, :], small[:, 8 + t:9 + t], None, ALU.mult)
                ins.then_inc(hbn_ready, 1)
                if h + 1 < HEADS:
                    probabilities(h + 1)
                a = a0 + 2 * h + 1
                dve.wait_ge(acc_free, a)
                for half in range(2):
                    dve.wait_ge(zb_ready, 2 * h + half + 1)
                    og = ogT[:, 2 * h + half, :]
                    ins = v.tensor_tensor(og, acc[:, 2 * (a % 2) + half, :], og, ALU.mult)
                ins.then_inc(acc_free, 1)
                dve.wait_ge(acc_free, a + 1)
                for e in range(2):
                    j = 2 * h + e
                    dve.wait_ge(hT_ready, j + 1)
                    tile_written(v.scalar_tensor_tensor(ogT[:, j, :], aux[:, e, :], V("mlstm_g", j), ogT[:, j, :],
                                                        ALU.mult, ALU.mult))
            for j in range(KT):
                rest(ogT[:, j, :], op_hi[:, j, :], op_lo[:, j, :])

            normalise(memrow, memn, MT, 20)
            _, a0, units = plan["pb"]
            dve.wait_ge(acc_free, a0)
            for u in range(units):
                for half in range(2):
                    j = 2 * u + half
                    dve.wait_ge(acc_ready, 2 * (a0 + u) + 1 + half)
                    ins = v.tensor_tensor(gbT[:, j, :], acc[:, 2 * ((a0 + u) % 2) + half, :], gbT[:, j, :], ALU.mult)
                    if half:
                        ins.then_inc(acc_free, 1)
                        dve.wait_ge(acc_free, a0 + u + 1)
                    else:
                        step(ins)
                    tile_written(v.tensor_tensor(mergedT[:, j, :], mergedT[:, j, :], gbT[:, j, :], ALU.add))
                for j in (2 * u, 2 * u + 1):
                    rest(mergedT[:, j, :], ht_hi[:, j, :], ht_lo[:, j, :])
            rests_of_transposes("e_mem", memT_hi, memT_lo, MEM)
            dve.wait_ge(masks2_in, 16)
            v.tensor_copy(causal_r[:], masks2[:, S:S + P])
            v.tensor_copy(bones_r[:], bones[:])
            v.tensor_copy(ident_r[:], ident[:]).then_inc(masks_r, 1)

            def post_gain(u):
                for t in range(TT):
                    cols = slice(UC * u, UC * u + UC)
                    ins = v.tensor_tensor(orow1[:, t, cols], orow1[:, t, cols], gpost[:, cols], ALU.mult)
                return ins
            dve.wait_ge(post_in, 32)
            for u in range(3):
                dve.wait_ge(post_ssq, TT * (u + 1))
                post_gain(u)
            dve.wait_ge(post_ssq, TT * 4)
            step(v.reduce_sum(small[:, 0:4], stats[:, 5, 0:16].rearrange("p (t u) -> p t u", t=TT), AX.X))
            v.tensor_scalar(small[:, 0:4], small[:, 0:4], 1.0 / D, EPS, ALU.mult, ALU.add).then_inc(post_var, 1)
            step(post_gain(3))
            dve.wait_ge(post_sd, 1)
            step(v.reciprocal(small[:, 4:8], small[:, 0:4]))
            for t in range(TT):
                v.scalar_tensor_tensor(xrow[:, t, :], orow1[:, t, :], small[:, 4 + t:5 + t], xagain[:, t, :],
                                       ALU.mult, ALU.add).then_inc(x_rows, 1)

            def head_norm_raw(a, half, dst):
                n = seen["hn"] + half
                dve.wait_ge(sq_ready, n + 1)
                dve.wait_ge(acc_free, a)
                ins = v.tensor_copy(dst, acc[:, 2 * (a % 2) + half, 0:dst.shape[-1]])
                if half:
                    ins.then_inc(acc_free, 1)
                if n >= 2:
                    dve.wait_ge(ssq_ready, n - 1)
                cols = dst.shape[-1]
                step(v.tensor_copy(hn_hi[:, n % 2, 0:cols], hn_sq[:, n % 2, 0:cols]))
                v.tensor_tensor(hn_lo[:, n % 2, 0:cols], hn_sq[:, n % 2, 0:cols], hn_hi[:, n % 2, 0:cols].bitcast(F32),
                                ALU.subtract).then_inc(sq_split, 1)

            def head_norm_scale(n, a, dst, gain):
                dve.wait_ge(acc_free, a + 1)
                dve.wait_ge(rs_ready, n + 1)
                v.scalar_tensor_tensor(dst, dst, gain, hn_rs[:, n % 2, 0:dst.shape[-1]],
                                       ALU.mult, ALU.mult).then_inc(hn_done, 1)

            done = 0
            for L, name in enumerate("eo"):
                qk, _ = LAYERS[L]
                normalise(xrow, xnrow, TT, 0)
                a0 = plan[name + "_mem"][1]
                for half in range(2):
                    head_norm_raw(a0, half, mkT[:, half, :])
                rests_of_transposes(name + "_norm", ht_hi, ht_lo, S)
                for half in range(2):
                    head_norm_scale(seen["hn"] + half, a0, mkT[:, half, :], V(name + "_qk", 5 if L == 0 else 3))
                seen["hn"] += 2
                if L:
                    a = plan["o_f"][1]
                    step(v.memset(negc[:], 0.0))
                    dve.wait_ge(acc_ready, 2 * (a + 1))
                    dve.wait_ge(acc_free, a)
                    R = lambda i: frow[0:C_HEADS, i, :]
                    v.tensor_copy(R(0), acc[0:C_HEADS, 2 * (a % 2), :]).then_inc(acc_free, 1)
                    dve.wait_ge(acc_free, a + 1)
                    v.tensor_scalar(R(0), R(0), vecs[0:C_HEADS, VC["o_bf"]:VC["o_bf"] + 1], None, ALU.add).then_inc(gate_rows, 1)
                    dve.wait_ge(gate_rows, 2)
                    dve.wait_ge(gate_exp, 2)
                    step(v.scalar_tensor_tensor(R(1), R(0), 0.0, R(1), ALU.min, ALU.subtract))
                    step(v.tensor_tensor_scan(R(2), R(1), R(1), 0.0, ALU.add, ALU.bypass))
                    v.tensor_scalar(negc[0:C_HEADS, :], R(2), -1.0, None, ALU.mult).then_inc(negc_ready, 1)
                _, a0, units = plan[name + "_qk"]

                def scale_unit(u):
                    for half in range(2):
                        j = 2 * u + half
                        head_norm_scale(seen["hn"] - 2 + half, a0 + u, qk[:, j, :], V(name + "_qk", QK_GAINS[L][j]))
                for u in range(units):
                    for half in range(2):
                        head_norm_raw(a0 + u, half, qk[:, 2 * u + half, :])
                    if u:
                        scale_unit(u - 1)
                    seen["hn"] += 2
                scale_unit(units - 1)

                jobs = JOBS[L]
                az = plan[name + "_z"][1]
                DIST, WINDOW = masks2[:, 0:S], masks2[:, S + P:S + P + 2 * WIN]
                for i in range(len(jobs) + 2):
                    if i < len(jobs):
                        job, g = jobs[i], done + i
                        logits = logit_bank(i)[:, 0:job.keys]
                        if job.bias is not None:
                            kind, h, slope = job.bias
                            if kind == "forget":
                                if job.t == 0:
                                    dve.wait_ge(negc_in[job.slot], 16 * (h // 4 + 1))
                                tile = negc_all[:, job.slot, 0:job.keys]
                            else:
                                full = DIST if kind == "dist" else WINDOW
                                tile = bias_h[:, job.slot, 0:full.shape[-1]]
                                if job.t == 0:
                                    step(v.tensor_scalar(tile, full, slope, None, ALU.mult))
                            width = tile.shape[-1]
                            if g >= 3:
                                dve.wait_ge(pr_ready, g - 2)
                            dve.wait_ge(logit_ready, g + 1)
                            step(v.tensor_tensor_reduce(out=sc[:, i % 3, 0:job.keys], in0=logits,
                                                        in1=tile[:, width - job.keys:width], scale=1.0, scalar=FLOOR,
                                                        op0=ALU.add, op1=ALU.max, accum_out=stats[:, 0, i:i + 1]))
                        else:
                            dve.wait_ge(logit_ready, g + 1)
                            step(v.reduce_max(stats[:, 0, i:i + 1], logits, AX.X))
                        if job.sink is None:
                            v.tensor_scalar(stats[:, 1, i:i + 1], stats[:, 0, i:i + 1], -1.0, None,
                                            ALU.mult).then_inc(nm_ready, 1)
                        else:
                            v.tensor_scalar(stats[:, 1, i:i + 1], stats[:, 0, i:i + 1], V("sinks", job.sink), -1.0,
                                            ALU.max, ALU.mult).then_inc(nm_ready, 1)
                    if 1 <= i <= len(jobs):
                        k = i - 1
                        dve.wait_ge(pr_ready, done + k + 1)
                        if jobs[k].sink is not None:
                            dve.wait_ge(es_ready, k + 1)
                            step(v.tensor_tensor(stats[:, 2, k:k + 1], stats[:, 2, k:k + 1], stats[:, 3, k:k + 1], ALU.add))
                        v.reciprocal(stats[:, 4, k:k + 1], stats[:, 2, k:k + 1]).then_inc(ri_ready, 1)
                    if i >= 2:
                        k = i - 2
                        dve.wait_ge(prT_ready, done + k + 1)
                        if done + k >= 2:
                            dve.wait_ge(o_ready, done + k - 1)
                        v.tensor_copy(prT[:, k % 2, 0:jobs[k].keys], trans_bank(k)[:, 0:jobs[k].keys]).then_inc(prT_copied, 1)
                    if z_due(i) is not None:
                        hu = z_due(i)
                        dve.wait_ge(th_ready, 8 * L + hu + 1)
                        ins = v.scalar_tensor_tensor(zT[:, hu, :], zT[:, hu, :], 1.0, acc[:, hu % 2, :], ALU.add, ALU.mult)
                        if hu % 2 == 0:
                            ins.then_inc(z_half, 1)
                        else:
                            if hu == 1:
                                dve.wait_ge(acc_free, az)
                            ins.then_inc(acc_free, 1)
                done += len(jobs)

                dve.wait_ge(acc_free, plan[name + "_out"][1])
                for j in range(KT):
                    seen["aT"] += 1
                    dve.wait_ge(arow_T, seen["aT"])
                    tile_written(v.scalar_tensor_tensor(zT[:, j, :], aux[:, j % 4, :], 0.5, zT[:, j, :], ALU.mult, ALU.mult))
                    if j:
                        rest(zT[:, j - 1, :], ht_hi[:, j - 1, :], ht_lo[:, j - 1, :])
                rest(zT[:, KT - 1, :], ht_hi[:, KT - 1, :], ht_lo[:, KT - 1, :])
                if L == 0:
                    normalise(memrow, memn, MT, 20)
                _, a0, units = plan[name + "_out"]

                def residual(u, q):
                    for half in range(2):
                        dve.wait_ge(acc_ready, u * 2 + 2 * a0 + 1 + half)
                        rows = xrow[:, 2 * half:2 * half + 2, bass.ds(u * UC, UC)]
                        bank = acc[:, 2 * ((a0 + q) % 2) + half, :].rearrange("p (t c) -> p t c", t=2)
                        ins = v.tensor_tensor(rows, bank, rows, ALU.add)
                        if half:
                            ins.then_inc(acc_free, 1)
                for u in range(units):
                    residual(u, u % 2)
                    if L == 0 and u == 0:
                        rests_of_transposes("o_mem", memT_hi, memT_lo, MEM)

        @block.tensor
        def _(pe):
            seen = {"xn": 0, "tr": 0, "hn": 0, "aT": 0}
            mm = nc.tensor.matmul

            def product(out_, w_hi_, w_lo_, x_hi, x_lo, first, last):
                mm(out_, w_hi_, x_hi, start=first, stop=False)
                mm(out_, w_hi_, x_lo, start=False, stop=False)
                return mm(out_, w_lo_, x_hi, start=False, stop=last)

            def unit_waits(n, a):
                pe.wait_ge(w_split, n + 1)
                if not (isinstance(a, int) and a < 2):
                    pe.wait_ge(acc_free, a - 1)

            def by_channels(n, a, s, b, x_hi, x_lo, cols=S):
                unit_waits(n, a)
                for half in range(2):
                    channel_half(s, b, half, x_hi, x_lo, cols)

            def channel_half(s, b, half, x_hi, x_lo, cols=S, tiles_split=None):
                for k in range(KT):
                    if tiles_split is not None and half == 0:
                        pe.wait_ge(tr_lo, tiles_split + k + 1)
                    c = k * UC + half * P
                    ins = product(acc[:, 2 * b + half, 0:cols], whi[:, s, c:c + P], wlo[:, s, c:c + P],
                                  x_hi[:, k, :], x_lo[:, k, :], k == 0, k == KT - 1)
                ins.then_inc(acc_ready, 1)

            def by_rows(n, a, s, b, x_hi, x_lo, tiles=TT):
                unit_waits(n, a)
                per = tiles // 2
                for t in range(tiles):
                    out_ = acc[:, 2 * b + t // per, UC * (t % per):UC * (t % per) + UC]
                    for k in range(KT):
                        ins = product(out_, x_hi[:, k, P * t:P * t + P], x_lo[:, k, P * t:P * t + P],
                                      whi[:, s, k * UC:k * UC + UC], wlo[:, s, k * UC:k * UC + UC], k == 0, k == KT - 1)
                    if t % per == per - 1:
                        ins.then_inc(acc_ready, 1)

            def rows_as_tiles_come(n, a, s, b, x_hi, x_lo, rests_before):
                unit_waits(n, a)
                for k in range(KT):
                    pe.wait_ge(lo_ready, rests_before + k + 1)
                    for t in range(TT):
                        ins = product(acc[:, 2 * b + t // 2, UC * (t % 2):UC * (t % 2) + UC],
                                      x_hi[:, k, P * t:P * t + P], x_lo[:, k, P * t:P * t + P],
                                      whi[:, s, k * UC:k * UC + UC], wlo[:, s, k * UC:k * UC + UC],
                                      k == 0 and t % 2 == 0, k == KT - 1 and t % 2 == 1)
                        if k == KT - 1 and t % 2:
                            ins.then_inc(acc_ready, 1)

            def rows_stage(name, rests_before, mem_after):
                n0, a0, units = plan[name]
                for u in range(units):
                    n, a = n0 + u, a0 + u
                    if u == 0:
                        rows_as_tiles_come(n, a, n % 2, a % 2, ht_hi, ht_lo, rests_before)
                    else:
                        by_rows(n, a, n % 2, a % 2, ht_hi, ht_lo)
                    if u == mem_after:
                        transposes(memn, MT)

            def stage(name, kind, x_hi, x_lo, peel=0):
                n0, a0, units = plan[name]
                pairs(pe, units, lambda u, q: kind(u + n0, u + a0, (n0 + q) % 2, (a0 + q) % 2, x_hi, x_lo), peel)

            def transposes(rows, tiles):
                seen["xn"] += tiles
                pe.wait_ge(xn_ready, seen["xn"])
                for k in range(KT):
                    if seen["tr"] >= 4:
                        pe.wait_ge(tr_lo, seen["tr"] - 3)
                    for t in range(tiles):
                        ins = nc.tensor.transpose(aux[:, k % 4, P * t:P * t + P], rows[:, t, P * k:P * k + P], ident[:])
                    ins.then_inc(tr_ready, 1)
                    seen["tr"] += 1

            pe.wait_ge(ident_in, 16)
            for t in range(TT):
                seen["xn"] += 1
                pe.wait_ge(xn_ready, seen["xn"])
                for k in range(KT):
                    ins = nc.tensor.transpose(first_bank(k)[:, P * t:P * t + P], xnrow[:, t, P * k:P * k + P], ident[:])
                    if t == TT - 1:
                        ins.then_inc(tr_ready, 1)
            seen["tr"] += KT
            pe.wait_ge(w_split, 1)
            for k in range(KT):
                pe.wait_ge(tr_lo, k + 1)
                ins = product(acc[:, 0, :], whi[:, 0, P * k:P * k + P], wlo[:, 0, P * k:P * k + P],
                              ht_hi[:, k, :], ht_lo[:, k, :], k == 0, k == KT - 1)
            ins.then_inc(acc_ready, 2)
            stage("u", by_channels, ht_hi, ht_lo, peel=1)
            pe.wait_ge(gm_ready, 1)
            for t in range(TT):
                ins = nc.tensor.transpose(aux[:, 3, P * t:P * t + P], grow[:, 5, P * t:P * t + P], ident[:])
            ins.then_inc(gmT_ready, 1)
            stage("za", by_channels, ht_hi, ht_lo)
            n, a0, _ = plan["mix"]
            pe.wait_ge(lo_ready, 8)
            for g in range(4):
                unit_waits(n, a0 + g)
                for m in range(2):
                    for kk in range(2):
                        c = (2 * g + kk) * UC + P * m
                        ins = product(acc[:, 2 * ((a0 + g) % 2) + m, :], whi[:, n % 2, c:c + P], wlo[:, n % 2, c:c + P],
                                      op_hi[:, 2 * g + kk, :], op_lo[:, 2 * g + kk, :], kk == 0, kk == 1)
                    ins.then_inc(acc_ready, 1)
            stage("ga", by_channels, ht_hi, ht_lo)
            pe.wait_ge(lo_ready, 16)
            stage("pa", by_channels, op_hi, op_lo)
            stage("qk", by_channels, ht_hi, ht_lo)
            stage("v", by_rows, ht_hi, ht_lo)

            def scores(h):
                if h:
                    pe.wait_ge(hb_ready, TT * h)
                    if h > 1:
                        pe.wait_ge(t_ready, 16 + 2 * (h - 1))
                else:
                    pe.wait_ge(silu_ready, 2 * KT)
                    pe.wait_ge(floor_ready, 2)
                for d in range(2):
                    r = 32 * d + h
                    ins = mm(aux[:, d, :], ident[0:64, r:r + 1].to_broadcast([64, P]), rowmax[0:64, :], start=True, stop=True)
                ins.then_inc(mbc_ready, 1)
                score_tiles(h, (0, 1))

            def score_tiles(h, tiles):
                for j in tiles:
                    if j >= 2:
                        pe.wait_ge(p_ready, TT * h + j - 1)
                    for kk in range(2):
                        ins = mm(aux[:, 2 + j % 2, :], qkT[:, KT + 2 * h + kk, P * j:P * j + P], qkT[:, 2 * h + kk, :],
                                 start=kk == 0, stop=kk == 1)
                    ins.then_inc(s_ready, 1)

            def values(h):
                pe.wait_ge(p_ready, TT * (h + 1))
                if h:
                    pe.wait_ge(t_ready, 16 + 2 * h)
                for t in range(TT):
                    if t >= 2:
                        pe.wait_ge(hb_ready, TT * h + t - 1)
                    for d in range(2):
                        keys = range(0, t + 1) if d == 0 else range(t, TT)
                        for j in keys:
                            ins = mm(aux[:, 2 * (t % 2) + d, 0:VW], prob[:, d, j, P * t:P * t + P],
                                     vrow[:, j, VW * h:VW * h + VW], start=j == keys[0], stop=j == keys[-1])
                    ins.then_inc(pv_ready, 1)

            def output_transposes(h):
                pe.wait_ge(hbn_ready, h + 1)
                if h + 1 < HEADS:
                    pe.wait_ge(p_ready, TT * (h + 2))
                for e in range(2):
                    for t in range(TT):
                        ins = nc.tensor.transpose(aux[:, e, P * t:P * t + P], hrow[:, t, P * e:P * e + P], ident[:])
                    ins.then_inc(hT_ready, 1)

            n0, a0, _ = plan["ozb"]
            pe.wait_ge(acc_free, a0)
            pe.wait_ge(consts_in, 32)
            scores(0)
            for h in range(HEADS):
                n, a = n0 + 2 * h, a0 + 2 * h
                unit_waits(n, a)
                channel_half(n % 2, a % 2, 0, ht_hi, ht_lo)
                if h == 0:
                    score_tiles(0, (2, 3))
                channel_half(n % 2, a % 2, 1, ht_hi, ht_lo)
                values(h)
                n, a = n + 1, a + 1
                unit_waits(n, a)
                channel_half(n % 2, a % 2, 0, ht_hi, ht_lo)
                if h + 1 < HEADS:
                    scores(h + 1)
                channel_half(n % 2, a % 2, 1, ht_hi, ht_lo)
                if h + 1 < HEADS:
                    score_tiles(h + 1, (2, 3))
                output_transposes(h)
            stage("gb", by_channels, ht_hi, ht_lo)
            pe.wait_ge(lo_ready, 24)
            stage("pb", by_channels, op_hi, op_lo)
            rows_stage("wout", 24, 0)

            def sum_squares(cols):
                n = seen["hn"]
                pe.wait_ge(sq_split, n + 1)
                if n >= 2:
                    pe.wait_ge(ln_done, n - 1)
                mm(aux[:, n % 2, 0:cols], bones_r[:], hn_hi[:, n % 2, 0:cols], start=True, stop=False)
                mm(aux[:, n % 2, 0:cols], bones_r[:], hn_lo[:, n % 2, 0:cols], start=False, stop=True).then_inc(ssq_ready, 1)
                seen["hn"] += 1

            done = 0
            for L, name in enumerate("eo"):
                qk, vv = LAYERS[L]
                pe.wait_ge(tr_lo, seen["tr"])
                if L == 0:
                    pe.wait_ge(masks_r, 1)
                n0, a0, _ = plan[name + "_mem"]
                by_channels(n0, a0, n0 % 2, a0 % 2, memT_hi, memT_lo, MEM)
                by_rows(n0 + 1, a0 + 1, (n0 + 1) % 2, (a0 + 1) % 2, memT_hi, memT_lo, MT)
                transposes(xnrow, TT)
                split_before = seen["tr"] - KT
                if L:
                    n, a, _ = plan["o_f"]
                    unit_waits(n, a)
                    for k in range(KT):
                        pe.wait_ge(tr_lo, split_before + k + 1)
                        ins = product(acc[:, 2 * (a % 2), :], whi[:, n % 2, P * k:P * k + P],
                                      wlo[:, n % 2, P * k:P * k + P], ht_hi[:, k, :], ht_lo[:, k, :], k == 0, k == KT - 1)
                    ins.then_inc(acc_ready, 2)
                n0, a0, units = plan[name + "_qk"]
                for u in range(units):
                    if L or u:
                        if u == 0:
                            sum_squares(MEM)
                            sum_squares(MEM)
                        by_channels(n0 + u, a0 + u, (n0 + u) % 2, (a0 + u) % 2, ht_hi, ht_lo)
                    else:
                        unit_waits(n0, a0)
                        for half in range(2):
                            channel_half(n0 % 2, a0 % 2, half, ht_hi, ht_lo, S, split_before)
                        sum_squares(MEM)
                        sum_squares(MEM)
                    if u:
                        sum_squares(S)
                        sum_squares(S)
                n0, a0, units = plan[name + "_v"]
                for u in range(units):
                    by_rows(n0 + u, a0 + u, (n0 + u) % 2, (a0 + u) % 2, ht_hi, ht_lo)
                    if u == 0:
                        sum_squares(S)
                        sum_squares(S)

                def z_product(i):
                    u, half, k = i // (2 * KT), i // KT % 2, i % KT
                    n0, a0, _ = plan[name + "_z"]
                    n, a = n0 + u, a0 + u
                    if k == 0 and half == 0:
                        pe.wait_ge(w_split, n + 1)
                        if u:
                            pe.wait_ge(z_half, 4 * L + u)
                    if k == 0 and half and u:
                        pe.wait_ge(acc_free, a)
                    c = k * UC + half * P
                    ins = product(acc[:, half, :], whi[:, n % 2, c:c + P], wlo[:, n % 2, c:c + P],
                                  ht_hi[:, k, :], ht_lo[:, k, :], k == 0, k == KT - 1)
                    if k == KT - 1:
                        ins.then_inc(acc_ready, 1)

                jobs = JOBS[L]
                pe.wait_ge(acc_free, plan[name + "_z"][1])
                pe.wait_ge(hn_done, seen["hn"])
                for i in range(len(jobs) + 3):
                    if i < len(jobs):
                        job, g = jobs[i], done + i
                        if i >= 2:
                            pe.wait_ge(pr_ready, g - 1)
                        (qt, qp), (kt_, kp) = job.q, job.k
                        keysT = mkT if job.bias is None else qk
                        out_ = logit_bank(i)[:, 0:job.keys]
                        k0 = P * job.k0
                        forget = job.bias is not None and job.bias[0] == "forget"
                        ins = mm(out_, qk[qp:qp + HD2, qt, P * job.t:P * job.t + P],
                                 keysT[kp:kp + HD2, kt_, k0:k0 + job.keys], start=True, stop=not forget)
                        if forget:
                            ins = mm(out_[:, job.keys - P:job.keys], ident_r[:], causal_r[:], start=False, stop=True)
                        ins.then_inc(logit_ready, 1)
                        z_product(i)
                    if 2 <= i < len(jobs) + 2:
                        k = i - 2
                        pe.wait_ge(pr_ready, done + k + 1)
                        if done + k >= 2:
                            pe.wait_ge(prT_copied, done + k - 1)
                        for b in range(jobs[k].keys // P):
                            ins = nc.tensor.transpose(trans_bank(k)[:, P * b:P * b + P], pr[:, k % 3, P * b:P * b + P], ident[:])
                        ins.then_inc(prT_ready, 1)
                    if i >= 3:
                        k = i - 3
                        job = jobs[k]
                        pe.wait_ge(prT_copied, done + k + 1)
                        if done + k >= 2:
                            pe.wait_ge(o_done, done + k - 1)
                        nb = job.keys // P
                        for b in range(nb):
                            vals = (mv if job.bias is None else vv)[:, job.k0 + b, job.v:job.v + HD2]
                            ins = mm(out_bank(k)[:, 0:HD2], prT[:, k % 2, P * b:P * b + P], vals, start=b == 0, stop=b == nb - 1)
                        ins.then_inc(o_ready, 1)
                done += len(jobs)
                pe.wait_ge(o_done, done)
                for k in range(KT):
                    if k >= 4:
                        pe.wait_ge(t_ready, 32 + 8 * L + k - 3)
                    for t in range(TT):
                        ins = nc.tensor.transpose(aux[:, k % 4, P * t:P * t + P], arow[:, t, P * k:P * k + P], ident[:])
                    ins.then_inc(arow_T, 1)
                pe.wait_ge(acc_free, plan[name + "_out"][1])
                rows_stage(name + "_out", 32 + 8 * L, 1 if L == 0 else None)


def columns(v):
    return np.ascontiguousarray(np.reshape(v, (-1, P)).T)


def pack(inputs):
    vecs = np.zeros((P, NVEC), np.float32)

    def put(name, block, rows=slice(None)):
        vecs[rows, VC[name]:VC[name] + block.shape[1]] = block
    put("pre_g", columns(inputs["norm_pre_g"][0]))
    put("conv_w", inputs["conv_qk_w"][0].reshape(TAPS, 16, P).transpose(2, 1, 0).reshape(P, 16 * TAPS))
    put("conv_b", columns(inputs["conv_qk_b"][0]))
    put("pool_scale", columns(inputs["pool_scale"][0]))
    put("mlstm_g", columns(inputs["mlstm_norm_g"][0]))
    put("b_merge", columns(inputs["b_merge"][0]))
    put("e_norm", columns(inputs["e_norm_2"][0]))
    put("e_mem", columns(inputs["e_mem_norm_2"][0]))
    put("o_norm", columns(inputs["o_norm_2"][0]))
    put("o_mem", columns(inputs["o_mem_norm_2"][0]))
    for half in range(2):
        put("e_qk", inputs["e_qk_norm_2"][0].T, slice(HD2 * half, HD2 * half + HD2))
        put("o_qk", inputs["o_qk_norm_2"][0].T, slice(HD2 * half, HD2 * half + HD2))
        put("b_i", inputs["b_igate"][0, half][:, None], slice(32 * half, 32 * half + HEADS))
        put("b_f", inputs["b_fgate"][0, half][:, None], slice(32 * half, 32 * half + HEADS))
    put("sinks", np.broadcast_to(inputs["e_sinks_2"][0][None, :], (P, A_HEADS)))
    put("o_bf", inputs["o_b_f_2"][0][:, None], slice(0, C_HEADS))
    put("eps", np.full((P, 1), EPS, np.float32))
    put("edge", np.broadcast_to(edge_constants()[None, :], (P, 2 * PAD * len(WINDOWS))))
    return vecs


DIRECT = ["x", "w_in", "pool_mix_w", "w_proj_pool", "w_proj_mlstm", "w_out", "norm_post_g", "mem_2",
          "e_w_in_2", "e_w_mem_kv_2", "e_w_out_2", "o_w_in_2", "o_w_mem_kv_2", "o_w_out_2"]


def kernel(**inputs):
    import concourse.bacc as bacc
    from concourse.bass_utils import run_bass_kernel_spmd

    nc = bacc.Bacc("TRN2", target_bir_lowering=False, num_devices=1)
    inputs = {k: np.asarray(v) for k, v in inputs.items()}
    arrays = {k: np.ascontiguousarray(inputs[k]) for k in DIRECT}
    arrays["vecs"] = pack(inputs)
    arrays["consts"] = shape_constants()
    aps = {k: nc.dram_tensor(k + "_dram", a.shape, F32, kind="ExternalInput").ap() for k, a in arrays.items()}
    out = nc.dram_tensor("out_dram", (1, S, D), F32, kind="ExternalOutput").ap()
    hybrid_block_then_two_attention_layers(nc, aps, aps["vecs"], aps["consts"], out)
    result = run_bass_kernel_spmd(nc, [{k + "_dram": a for k, a in arrays.items()}], core_ids=[0])
    return result.results[0]["out_dram"]
```

```python
from collections import namedtuple
from contextlib import ExitStack

import numpy as np
import concourse.bass as bass
from concourse import mybir

F32 = mybir.dt.float32
F32R = mybir.dt.float32r
ACT = mybir.ActivationFunctionType
ALU = mybir.AluOpType
AX = mybir.AxisListType

P = 128
D = 1024
KT = D // P
S = 512
TT = S // P
UC = 256
SLOT = KT * UC
EPS = 1e-6
BIG = 1e30
FLOOR = -3e38

HEADS, HD = 4, 256
WINDOWS = (2, 4, 8, 16)
TAPS = 5
PAD = max(WINDOWS) // 2
UW = S + 2 * PAD
CW = S + TAPS - 1
VW = HD + 1
COL_U, COL_ZA, COL_QK, COL_V, COL_O, COL_ZB, COL_GATES, COL_GA, COL_GB = (
    0, D, 2 * D, 4 * D, 5 * D, 6 * D, 7 * D, 7 * D + 16, 8 * D + 16)

HD2 = 64
WIN = 128
MEM = 256
MT = MEM // P
A_HEADS, B_HEADS, C_HEADS, M_HEADS = 6, 6, 12, 4
SLOPES = [2.0 ** (-8.0 * (h + 1) / (A_HEADS + B_HEADS)) for h in range(A_HEADS + B_HEADS)]

_widths = [("pre_g", KT), ("conv_w", 16 * TAPS), ("conv_b", 16), ("pool_scale", KT), ("mlstm_g", KT),
           ("b_merge", 2 * KT), ("e_norm", KT), ("e_mem", KT), ("o_norm", KT), ("o_mem", KT),
           ("e_qk", 6), ("o_qk", 4), ("b_i", 1), ("b_f", 1), ("sinks", A_HEADS), ("o_bf", 1),
           ("eps", 1), ("edge", 2 * PAD * len(WINDOWS))]
VC = {}
_at = 0
for _name, _w in _widths:
    VC[_name] = _at
    _at += _w
NVEC = 256
assert _at <= NVEC


E_COLS = tuple(int(c) for c in np.cumsum([0, A_HEADS * HD2, 2 * HD2, 2 * HD2, B_HEADS * HD2, B_HEADS * HD2,
                                          B_HEADS * HD2, M_HEADS * HD2]))
O_COLS = tuple(int(c) for c in np.cumsum([0, C_HEADS * HD2, C_HEADS * HD2, C_HEADS * HD2, C_HEADS, M_HEADS * HD2]))
Job = namedtuple("Job", "t k0 keys q k bias v sink slot")
QK_GAINS = ([0, 0, 0, 1, 2, 2, 2, 3, 3, 3, 4, 4], [0] * 6 + [1] * 6 + [2] * 2)


def shape_constants():
    p = np.arange(P)[:, None]
    c = np.arange(S)[None, :]
    ident = np.eye(P)
    bones = (p // HD2 == np.arange(P)[None, :] // HD2) * 1.0
    fwd = np.where(c >= p, 0.0, BIG)
    bwd = np.where(c - (S - P) <= p, 0.0, BIG)
    dist = np.where(c - (S - P) <= p, p - (c - (S - P)), BIG)
    causal = np.where(np.arange(P)[None, :] <= p, 0.0, BIG)
    w = np.arange(2 * WIN)[None, :]
    back = WIN + p - w
    window = np.where((back >= 0) & (back < WIN), back, BIG)
    return np.concatenate([ident, bones, fwd, bwd, dist, causal, window], axis=1).astype(np.float32)


def edge_constants():
    out = []
    for w in WINDOWS:
        for t0 in (0, S - PAD):
            for t in range(t0, t0 + PAD):
                lo, hi = max(t - w // 2, 0), min(t + w - 1 - w // 2, S - 1)
                out.append(w / (hi - lo + 1))
    return np.array(out, np.float32)


class Steps:

    def __init__(self, eng, sem):
        self.eng, self.sem, self.n, self.it, self.per = eng, sem, 0, None, 0

    def __call__(self, ins):
        ins.then_inc(self.sem, 1)
        self.n += 1
        self.eng.wait_ge(self.sem, self.n if self.it is None else self.it * self.per + self.n)

    def loop(self, count, per, body):
        n0 = self.n
        with self.eng.Fori(0, count) as i:
            self.it, self.per = i, per
            body(i)
        assert self.n == n0 + per
        self.n, self.it = n0 + per * count, None


def hybrid_block_then_two_attention_layers(nc, A, vecs_d, consts_d, out):
    stack = ExitStack()
    with stack:
        base = (nc.sbuf_base + 63) // 64 * 64
        K = 1024

        def at(name, shape, offset, dt=F32):
            return nc.alloc_sbuf_tensor_at(name, shape, dt, offset=base + offset)

        def sem(name):
            return stack.enter_context(nc.semaphore(name))

        HT, OP, RAW, WHI, WLO, R0, R1, R2, R3, R4, CST = (
            0, 32 * K, 64 * K, 80 * K, 96 * K, 112 * K, 128 * K, 144 * K, 160 * K, 177 * K, 193 * K)
        ht_hi = at("ht_hi", [P, KT, S], HT, F32R)
        ht_lo = at("ht_lo", [P, KT, S], HT + 16 * K, F32R)
        op_hi = at("op_hi", [P, KT, S], OP, F32R)
        op_lo = at("op_lo", [P, KT, S], OP + 16 * K, F32R)
        raw = at("raw", [P, 2, SLOT], RAW)
        whi = at("whi", [P, 2, SLOT], WHI, F32R)
        wlo = at("wlo", [P, 2, SLOT], WLO, F32R)

        ident = at("ident", [P, P], CST)
        bones = at("bones", [P, P], CST + 512)
        vecs = at("vecs", [P, NVEC], CST + K)
        masks1 = at("masks1", [P, 2, S], CST + 2 * K)
        masks2 = at("masks2", [P, S + P + 2 * WIN], CST + 2 * K)
        causal_r = at("causal_r", [P, P], CST + 2 * K + 3584, F32R)
        ident_r = at("ident_r", [P, P], CST + 2 * K + 4096, F32R)
        bones_r = at("bones_r", [P, P], CST + 2 * K + 4608, F32R)
        rowmax = at("rowmax", [64, S], CST + 11 * K)
        csum = at("csum", [C_HEADS, S], CST + 7 * K)
        mkT = at("mkT", [P, 2, MEM], CST + 9 * K)
        mv = at("mv", [P, MT, MEM], CST + 11 * K)
        stats = at("stats", [P, 6, 64], CST + 13 * K)
        gcol = at("gcol", [P, TT, 2, HEADS], CST + 14 * K + 512)
        floorc = at("floorc", [P, TT, 2, HEADS], CST + 14 * K + 640)
        small = at("small", [P, 24], CST + 14 * K + 768)

        xrow = at("xrow", [P, TT, D], R4)
        xnrow = at("xnrow", [P, TT, D], R0)
        rowmax_hi = at("rowmax_hi", [64, S], CST + 7 * K, F32R)
        rowmax_lo = at("rowmax_lo", [64, S], CST + 9 * K, F32R)
        zaT = at("zaT", [P, KT, S], R0)
        uT = at("uT", [P, KT, UW], R1)
        win_s = at("win_s", [P, 2, UW], R3)
        win_t = at("win_t", [P, 4, S], R3 + 5 * K)
        grow = at("grow", [P, 7, S], R2 + 2 * K)
        mergedT = at("mergedT", [P, KT, S], R4)
        cpad = at("cpad", [P, 4, CW + 12], OP)
        cacc = at("cacc", [P, 4, S], OP + 10 * K)
        qkT = at("qkT", [P, 2 * KT, S], R1)
        vrow = at("vrow", [P, TT, HEADS * VW], R3)
        ogT = at("ogT", [P, KT, S], R0)
        decay = at("decay", [P, 4, S], OP)
        prob = at("prob", [P, 2, TT, S], OP + 8 * K)
        hrow = at("hrow", [P, TT, HD], OP + 24 * K)
        hfwd = at("hfwd", [P, 2, HD], OP + 28 * K)
        hsq = at("hsq", [P, HD], OP + 30 * K)
        gbT = at("gbT", [P, KT, S], R2)
        orow1 = at("orow1", [P, TT, D], R0)
        xagain = at("xagain", [P, TT, D], R1)
        gpost = at("gpost", [P, D], R2)
        junk = at("junk", [P, D], R2 + 4 * K)
        memrow = at("memrow", [P, MT, D], R3)
        memn = at("memn", [P, MT, D], R3 + 8 * K)
        memT = [(at(f"memT_hi{i}", [P, KT, MEM], place, F32R), at(f"memT_lo{i}", [P, KT, MEM], place + 8 * K, F32R))
                for i, place in enumerate((OP, HT))]
        hn_sq = at("hn_sq", [P, 2, S], OP + 16 * K)
        hn_rs = at("hn_rs", [P, 2, S], OP + 20 * K)
        hn_hi = at("hn_hi", [P, 2, S], OP + 24 * K, F32R)
        hn_lo = at("hn_lo", [P, 2, S], OP + 28 * K, F32R)
        zT = at("zT", [P, 2, S], R0)
        frow = at("frow", [P, 3, S], R0)
        pr = at("pr", [P, 4, S], R0 + 4 * K)
        prT = [at(f"prT{i}", [P, S], place) for i, place in
               enumerate((R0 + 12 * K, R0 + 14 * K, CST + 7 * K, R3 + 14 * K))]
        csum_all = at("csum_all", [P, 3, S], R3 + 8 * K)
        bias_h = at("bias_h", [P, 2, S], R3)
        LAYERS = []
        for name, ntile, vcols, voff in (("e", 12, 512, 24 * K), ("o", 14, 768, 28 * K)):
            LAYERS.append((at("qk_" + name, [P, ntile, S], R1), at("v_" + name, [P, TT, vcols], R1 + voff)))

        csum_dram = nc.dram_tensor("csum_rows", (C_HEADS, S), F32, kind="Internal").ap()
        acc = stack.enter_context(nc.psum_tensor("acc", [P, 4, S], F32))
        aux = stack.enter_context(nc.psum_tensor("aux", [P, 4, S], F32))

        def V(name, j=0, n=1):
            return vecs[:, VC[name] + j:VC[name] + j + n]

        def Vd(name, j):
            return vecs[:, bass.ds(j + VC[name], 1)]

        act_first = sem("act_first")
        ident_in = sem("ident_in")
        vecs_in = sem("vecs_in")
        consts_in = sem("consts_in")
        x_in = [sem(f"x_in{t}") for t in range(TT)]
        w_loaded = [sem("w_loaded_0"), sem("w_loaded_1")]
        w_hi = sem("w_hi")
        w_split = sem("w_split")
        acc_ready = sem("acc_ready")
        acc_free = sem("acc_evacuated")
        pool_step = sem("pool_step")
        units_begun = sem("units_begun")
        act_step = sem("act_step")
        dve_step = sem("dve_step")
        rssq_ready = sem("rssq_ready")
        rvar_ready = sem("rvar_ready")
        rsd_ready = sem("rsd_ready")
        xn_ready = sem("xn_ready")
        tr_ready = sem("tr_ready")
        tr_hi = sem("tr_hi")
        tr_lo = sem("tr_lo")
        t_ready = sem("t_ready")
        hi_ready = sem("hi_ready")
        lo_ready = sem("lo_ready")
        conv_ready = sem("conv_ready")
        silu_ready = sem("silu_ready")
        gate_rows = sem("gate_rows")
        gate_exp = sem("gate_exp")
        gm_ready = sem("gm_ready")
        rowmax_split = sem("rowmax_split")
        last_rows = sem("last_rows")
        gmT_ready = sem("gmT_ready")
        gcol_ready = sem("gcol_ready")
        floor_ready = sem("floor_ready")
        mbc_ready = sem("mbc_ready")
        s_ready = sem("s_ready")
        arg_ready = sem("arg_ready")
        d_ready = sem("d_ready")
        p_ready = sem("p_ready")
        pv_ready = sem("pv_ready")
        den_ready = sem("den_ready")
        rden_ready = sem("rden_ready")
        hf_ready = sem("hf_ready")
        hb_ready = sem("hb_ready")
        hssq_ready = sem("hssq_ready")
        hrs_ready = sem("hrs_ready")
        hbn_ready = sem("hbn_ready")
        hT_ready = sem("hT_ready")
        zb_ready = sem("zb_ready")
        post_in = sem("post_in")
        post_ssq = sem("post_ssq")
        post_var = sem("post_var")
        post_sd = sem("post_sd")
        mem_in = sem("mem_in")
        sq_ready = sem("sq_ready")
        sq_split = sem("sq_split")
        ssq_ready = sem("ssq_ready")
        ln_done = sem("ln_done")
        rs_ready = sem("rs_ready")
        hn_done = sem("hn_done")
        csum_ready = sem("csum_ready")
        csum_out = sem("csum_out")
        nm_ready = sem("nm_ready")
        es_ready = sem("es_ready")
        pr_ready = sem("pr_ready")
        prT_ready = sem("prT_ready")
        prT_copied = sem("prT_copied")
        ri_ready = sem("ri_ready")
        norm_ready = sem("norm_ready")
        o_ready = sem("o_ready")
        x_rows = sem("x_rows")
        logit_ready = sem("logit_ready")
        stored = sem("stored")
        masks2_in = sem("masks2_in")
        th_ready = sem("th_ready")
        z_half = sem("z_half")
        consts_r_ready = sem("consts_r_ready")
        csum_in = [sem(f"csum_in{i}") for i in range(3)]

        block = stack.enter_context(nc.Block())

        plan = {}
        n_, a_ = 0, 0
        for name, units, accs in (("gates", 1, 1), ("u", 4, 4), ("za", 4, 4), ("mix", 1, 4), ("ga", 4, 4), ("pa", 4, 4),
                                  ("qk", 8, 8), ("v", 4, 4), ("ozb", 8, 8), ("gb", 4, 4), ("pb", 4, 4),
                                  ("wout", 4, 4), ("e_mem", 2, 2), ("e_qk", 6, 6), ("e_v", 2, 2),
                                  ("e_z", 4, 4), ("e_out", 4, 4), ("o_mem", 2, 2), ("o_f", 1, 1),
                                  ("o_qk", 7, 7), ("o_v", 3, 3), ("o_z", 4, 4), ("o_out", 4, 4)):
            plan[name] = (n_, a_, units)
            n_ += units
            a_ += accs
        UNITS = n_
        more = {plan["e_qk"][0]: 4, plan["e_qk"][0] + 1: 3, plan["e_z"][0]: 4, plan["e_z"][0] + 1: 3}
        more.update({plan["e_out"][0] + u: 3 for u in range(4)})

        def loaded(n):
            return 16 * sum(more.get(m, 2) for m in range(n % 2, n + 1, 2))

        def pairs(eng, units, body, peel=0):
            for i in range(min(peel, units // 2)):
                body(2 * i, 0)
                body(2 * i + 1, 1)
            if units // 2 > peel:
                with eng.Fori(peel, units // 2) as i:
                    body(2 * i, 0)
                    body(2 * i + 1, 1)
            if units % 2:
                body(units - 1, 0)


        def wview(w):
            return w.rearrange("(k p) n -> p k n", p=P)

        W1 = wview(A["w_in"][0])
        E_IN, O_IN = wview(A["e_w_in_2"][0]), wview(A["o_w_in_2"][0])
        raw3 = raw[:, :, :].rearrange("p s (k c) -> p s k c", k=KT)

        def tr_bank(k):
            return aux[:, k % 4, :]

        def first_bank(k):
            return acc[:, k, :] if k < 4 else aux[:, k - 4, :]

        def logit_bank(i):
            return acc[:, 2 + i % 2, :]

        def trans_bank(i):
            return aux[:, i % 2, :]

        def out_bank(j):
            return aux[:, 2 + j % 2, :]

        JOBS = [[], []]
        for j in range(A_HEADS // 2):
            for t in range(TT):
                for kv in range(2):
                    h = j + kv * (A_HEADS // 2)
                    k0 = max(t - 1, 0)
                    JOBS[0].append(Job(t, k0, P * (t + 1 - k0), (j, HD2 * kv), (3, HD2 * kv),
                                       ("window", h, SLOPES[h]), HD2 * kv, h, kv))
        for j in range(B_HEADS // 2):
            for t in range(TT):
                for e in range(2):
                    h = 2 * j + e
                    JOBS[0].append(Job(t, 0, P * (t + 1), (4 + j, HD2 * e), (7 + j, HD2 * e),
                                       ("dist", A_HEADS + h, SLOPES[A_HEADS + h]), P + HD2 * h, None, e))
        for j in range(C_HEADS // 2):
            for t in range(TT):
                for e in range(2):
                    h = 2 * j + e
                    JOBS[1].append(Job(t, 0, P * (t + 1), (j, HD2 * e), (6 + j, HD2 * e), ("forget", h, 1.0),
                                       HD2 * h, None, h % 3))
        for L, q0 in enumerate((10, 12)):
            for j in range(M_HEADS // 2):
                for t in range(TT):
                    for e in range(2):
                        h = 2 * j + e
                        JOBS[L].append(Job(t, 0, MEM, (q0 + j, HD2 * e), (j, HD2 * e), None,
                                           HD2 * h, None, e))
        assert len(JOBS[0]) == len(JOBS[1]) == 4 * 2 * KT

        def z_due(i):
            return i // KT - 1 if i >= KT and i % KT == 1 and i // KT <= KT else None

        @block.sync
        def _(sp):
            def slot_free(n):
                if isinstance(n, int) and n < 2:
                    return
                sp.wait_ge(w_split, n - 1)

            def load(view, col, n, slot):
                slot_free(n)
                for kh in range(2):
                    sp.dma_start(raw3[:, slot, 4 * kh:4 * kh + 4, :],
                                 view[:, 4 * kh:4 * kh + 4, bass.ds(col, UC)]).then_inc(w_loaded[slot], 16)

            def stage(name, view, col0, step=UC, peel=0):
                n0, _, units = plan[name]
                pairs(sp, units, lambda u, q: load(view, u * step + col0, u + n0, (n0 + q) % 2), peel)

            def halves(n, view, cols):
                slot_free(n)
                for half, col in enumerate(cols):
                    dst = raw3[:, n % 2, :, P * half:P * half + P]
                    if isinstance(col, tuple):
                        for part, c in enumerate(col):
                            sp.dma_start(dst[:, :, HD2 * part:HD2 * part + HD2],
                                         view[:, :, c:c + HD2]).then_inc(w_loaded[n % 2], 16)
                    else:
                        sp.dma_start(dst, view[:, :, col:col + P]).then_inc(w_loaded[n % 2], 16)

            def narrow(n, view, col, width):
                slot_free(n)
                dst = raw[:, n % 2, 0:KT * width].rearrange("p (k c) -> p k c", k=KT)
                for kh in range(2):
                    sp.dma_start(dst[:, 4 * kh:4 * kh + 4, :],
                                 view[:, 4 * kh:4 * kh + 4, col:col + width]).then_inc(w_loaded[n % 2], 16)

            narrow(0, W1, COL_GATES, 16)
            xv = A["x"][0].rearrange("(t p) d -> p t d", p=P)
            sp.dma_start(ident[:], consts_d[:, 0:P]).then_inc(ident_in, 16)
            for t in range(2, TT):
                sp.dma_start(xrow[:, t, :], xv[:, t, :]).then_inc(x_in[t], 16)
            sp.dma_start(vecs[:], vecs_d).then_inc(vecs_in, 16)
            stage("u", W1, COL_U, peel=1)
            sp.dma_start(bones[:], consts_d[:, P:2 * P]).then_inc(consts_in, 16)
            sp.dma_start(masks1[:], consts_d[:, 2 * P:2 * P + 2 * S].rearrange("p (a c) -> p a c", a=2)).then_inc(consts_in, 16)
            stage("za", W1, COL_ZA)
            n = plan["mix"][0]
            slot_free(n)
            mixw = A["pool_mix_w"][0].rearrange("g (kk p) n -> p (g kk) n", p=P)
            for kh in range(2):
                sp.dma_start(raw3[:, n % 2, 4 * kh:4 * kh + 4, :], mixw[:, 4 * kh:4 * kh + 4, :]).then_inc(w_loaded[n % 2], 16)
            stage("ga", W1, COL_GA)
            stage("pa", wview(A["w_proj_pool"][0]), 0)
            stage("qk", W1, COL_QK)
            stage("v", W1, COL_V)
            n = plan["ozb"][0]
            with sp.Fori(0, HEADS) as h:
                load(W1, h * UC + COL_O, 2 * h + n, n % 2)
                load(W1, h * UC + COL_ZB, 2 * h + n + 1, (n + 1) % 2)
            stage("gb", W1, COL_GB)
            stage("pb", wview(A["w_proj_mlstm"][0]), 0)
            stage("wout", wview(A["w_out"][0]), 0)

            stage("e_mem", wview(A["e_w_mem_kv_2"][0]), 0)
            n = plan["e_qk"][0]
            AQ, AK, AV, BQ, BK, BV, MQ, Z = E_COLS
            tiles = [(AQ + HD2 * j, AQ + HD2 * (j + 3)) for j in range(3)] + [AK]
            tiles += [BQ + P * j for j in range(3)] + [BK + P * j for j in range(3)] + [MQ, MQ + P]
            for u in range(6):
                halves(n + u, E_IN, tiles[2 * u:2 * u + 2])
            halves(plan["e_v"][0], E_IN, [AV, BV])
            halves(plan["e_v"][0] + 1, E_IN, [BV + P, BV + 2 * P])
            n = plan["e_z"][0]
            tiles = [(Z + HD2 * j, Z + HD2 * (j + 3)) for j in range(3)] + [Z + P * j for j in range(3, KT)]
            for u in range(4):
                halves(n + u, E_IN, tiles[2 * u:2 * u + 2])
            n = plan["e_out"][0]
            half_rows = A["e_w_out_2"][0][0:3 * P].rearrange("(e k p) n -> e p k n", e=2, p=HD2)
            for u in range(4):
                slot_free(n + u)
                cols = slice(UC * u, UC * u + UC)
                for e in range(2):
                    sp.dma_start(raw3[HD2 * e:HD2 * e + HD2, (n + u) % 2, 0:3, :],
                                 half_rows[e, :, :, cols]).then_inc(w_loaded[(n + u) % 2], 16)
                sp.dma_start(raw3[:, (n + u) % 2, 3:KT, :],
                             wview(A["e_w_out_2"][0])[:, 3:KT, cols]).then_inc(w_loaded[(n + u) % 2], 16)

            stage("o_mem", wview(A["o_w_mem_kv_2"][0]), 0)
            CQ, CK, CV, CF, MQ, Z = O_COLS
            narrow(plan["o_f"][0], O_IN, CF, C_HEADS)
            n = plan["o_qk"][0]
            for u in range(6):
                load(O_IN, CQ + UC * u, n + u, (n + u) % 2)
            load(O_IN, MQ, n + 6, (n + 6) % 2)
            n0 = plan["o_v"][0]
            for u in range(3):
                load(O_IN, CV + UC * u, n0 + u, (n0 + u) % 2)
            sp.wait_ge(csum_ready, 1)
            sp.dma_start(csum_dram, csum[:]).then_inc(csum_out, 16)
            sp.wait_ge(csum_out, 16)

            def spread(h):
                if h >= 3:
                    last = max(i for i, job in enumerate(JOBS[1]) if job.bias is not None and job.bias[1] == h - 3)
                    sp.wait_ge(nm_ready, len(JOBS[0]) + last + 1)
                sp.dma_start(csum_all[:, h % 3, :], csum_dram[h:h + 1, :].to_broadcast([P, S])).then_inc(csum_in[h % 3], 16)
            for u, heads in enumerate(((0, 1, 2), (), (3, 4, 5, 6), (7, 8))):
                for h in heads:
                    spread(h)
                n = plan["o_z"][0] + u
                load(O_IN, Z + UC * u, n, n % 2)
            for h in (9, 10, 11):
                spread(h)
            stage("o_out", wview(A["o_w_out_2"][0]), 0)

            outv = out[0].rearrange("(t p) d -> p t d", p=P)
            for u in range(4):
                cols = slice(UC * u, UC * u + UC)
                rows = slice(0, TT)
                if u == 3:
                    sp.wait_ge(last_rows, 1)
                    sp.dma_start(outv[:, 0:TT // 2, cols], xrow[:, 0:TT // 2, cols]).then_inc(stored, 16)
                    rows = slice(TT // 2, TT)
                sp.wait_ge(acc_free, plan["o_out"][1] + u + 1)
                sp.dma_start(outv[:, rows, cols], xrow[:, rows, cols]).then_inc(stored, 16)
            sp.wait_ge(stored, 80)

        @block.gpsimd
        def _(pool):
            step = Steps(pool, pool_step)

            def split(n, slot, loads, a_before):
                pool.wait_ge(w_loaded[slot], loads)
                if a_before is not None:
                    pool.wait_ge(acc_ready, a_before * 2 + 2)
                pool.sem_inc(units_begun, 1)
                nc.gpsimd.tensor_scalar(whi[:, slot, :], raw[:, slot, :], 1.0, 1.0, ALU.mult, ALU.mult).then_inc(w_hi, 1)
                pool.wait_ge(w_hi, n + 1)
                nc.gpsimd.tensor_tensor(wlo[:, slot, :], raw[:, slot, :], whi[:, slot, :].bitcast(F32),
                                        ALU.subtract).then_inc(w_split, 1)

            def split_narrow(n, a_before, width, groups):
                slot = n % 2
                if a_before is not None:
                    pool.wait_ge(acc_ready, 2 * (a_before + 1))
                nc.gpsimd.memset(whi[:, slot, 0:KT * P].bitcast(F32), 0.0)
                step(nc.gpsimd.memset(wlo[:, slot, 0:KT * P].bitcast(F32), 0.0))
                pool.wait_ge(w_loaded[slot], loaded(n))
                src = raw[:, slot, 0:KT * width].rearrange("p (k c) -> p k c", k=KT)
                hi = whi[:, slot, 0:KT * P].rearrange("p (k c) -> p k c", k=KT)
                lo = wlo[:, slot, 0:KT * P].rearrange("p (k c) -> p k c", k=KT)
                for g, (c, d, w) in enumerate(groups):
                    ins = nc.gpsimd.tensor_copy(hi[:, :, d:d + w], src[:, :, c:c + w])
                    if g == len(groups) - 1:
                        ins.then_inc(w_hi, 1)
                pool.wait_ge(w_hi, n + 1)
                for g, (c, d, w) in enumerate(groups):
                    ins = nc.gpsimd.tensor_tensor(lo[:, :, d:d + w], src[:, :, c:c + w],
                                                  hi[:, :, d:d + w].bitcast(F32), ALU.subtract)
                    if g == len(groups) - 1:
                        ins.then_inc(w_split, 1)

            split_narrow(0, None, 16, [(8 * d + 4 * kind, 64 * kind + 32 * d, 4) for d in range(2) for kind in range(2)])
            mix = plan["mix"][0]
            split(1, 1, loaded(1), None)
            split(2, 0, loaded(2), 0)
            with pool.Fori(0, (mix - 3) // 2) as i:
                split(2 * i + 3, 1, i * 32 + loaded(3), 2 * i + 1)
                split(2 * i + 4, 0, i * 32 + loaded(4), 2 * i + 2)
            assert mix % 2
            for n in (mix, mix + 1):
                split(n, n % 2, loaded(n), n - 2)

            def run(lo, hi):
                assert not any(n in more for n in range(lo, hi))

                def one(i, d):
                    split(2 * i + lo + d, (lo + d) % 2, i * 32 + loaded(lo + d), 2 * i + lo + d + 1)
                if (hi - lo) // 2:
                    with pool.Fori(0, (hi - lo) // 2) as i:
                        one(i, 0)
                        one(i, 1)
                if (hi - lo) % 2:
                    split(hi - 1, (hi - 1) % 2, loaded(hi - 1), hi)
            n = plan["e_qk"][0]
            run(mix + 2, n)
            for m in (n, n + 1):
                split(m, m % 2, loaded(m), m + 1)
            run(n + 2, plan["e_z"][0])
            for m in range(plan["e_z"][0], plan["o_mem"][0]):
                split(m, m % 2, loaded(m), m + 1)
            n = plan["o_f"][0]
            run(plan["o_mem"][0], n)
            split_narrow(n, n + 1, C_HEADS, [(0, 0, C_HEADS)])
            run(n + 1, UNITS)

        @block.scalar
        def _(act):
            step = Steps(act, act_step)
            xv = A["x"][0].rearrange("(t p) d -> p t d", p=P)
            for t in range(0, 2):
                act.dma_start(xrow[:, t, :], xv[:, t, :]).then_inc(x_in[t], 16)

            seen = {"rssq": 0, "rvar": 0, "tr": 0, "hi": 0, "hn": 0, "exp": 0}

            def squares(src, dst, tiles, col, wait, lag=1):
                for t in range(tiles):
                    wait(t)
                    nc.scalar.activation(dst[:, t, :], src[:, t, :], ACT.Square,
                                         accum_out=small[:, col + t:col + t + 1]).then_inc(rssq_ready, 1)
                    if t >= lag:
                        root(col + t - lag)
                if lag:
                    root(col + tiles - 1)

            def root(c):
                seen["rvar"] += 1
                act.wait_ge(rvar_ready, seen["rvar"])
                nc.scalar.activation(small[:, c:c + 1], small[:, c:c + 1], ACT.Sqrt).then_inc(rsd_ready, 1)

            def heads_of_transposes(gain, dst, cols, bank=tr_bank):
                for k in range(KT):
                    seen["tr"] += 1
                    act.wait_ge(tr_ready, seen["tr"])
                    nc.scalar.activation(dst[:, k, :], bank(k)[:, 0:cols], ACT.Copy,
                                         scale=V(gain, k)).then_inc(tr_hi, 1)

            def head(src, dst):
                seen["hi"] += 1
                act.wait_ge(t_ready, seen["hi"])
                nc.scalar.activation(dst, src, ACT.Copy).then_inc(hi_ready, 1)

            def evac(a, s, half, dst, func, **kw):
                act.wait_ge(acc_ready, a * 2 + 1 + half)
                ins = nc.scalar.activation(dst, acc[:, 2 * s + half:2 * s + half + 1, :], func, **kw)
                if half:
                    ins.then_inc(acc_free, 1)

            def stage(name, dst, func, bias=None, peel=0):
                _, a0, units = plan[name]
                act.wait_ge(acc_free, a0)

                def body(u, q):
                    for half in range(2):
                        kw = {} if bias is None else {"bias": Vd(*bias, u * 2 + half)} if len(bias) == 1 else \
                            {"bias": Vd(bias[0], u * 2 + half + bias[1])}
                        evac(u + a0, (a0 + q) % 2, half, dst[:, bass.ds(u * 2 + half, 1), :], func, **kw)
                pairs(act, units, body, peel)

            act.wait_ge(act_first, 1)
            nc.scalar.activation(small[:, 13:14], small[:, 12:13], ACT.Sqrt)
            squares(xrow, xnrow, TT, 0, lambda t: act.wait_ge(x_in[t], 16), lag=0)
            act.wait_ge(vecs_in, 16)
            heads_of_transposes("pre_g", ht_hi, S, first_bank)

            def softplus_of_minus_abs(src, tmp):
                step(nc.scalar.activation(tmp, src, ACT.Abs))
                step(nc.scalar.activation(tmp, tmp, ACT.Exp, scale=-1.0))
                nc.scalar.activation(tmp, tmp, ACT.Ln, bias=1.0).then_inc(gate_exp, 1)
            act.wait_ge(gate_rows, 1)
            softplus_of_minus_abs(grow[0:64, 1, :], grow[0:64, 2, :])

            _, a0, units = plan["u"]
            act.wait_ge(acc_free, a0)
            for u in range(units):
                for half in range(2):
                    evac(a0 + u, (a0 + u) % 2, half, uT[:, 2 * u + half:2 * u + half + 1, PAD:PAD + S], ACT.Copy)
                if u:
                    for j in (2 * u - 2, 2 * u - 1):
                        head(win_t[:, j % 4, :], op_hi[:, j, :])
            for j in (2 * units - 2, 2 * units - 1):
                head(win_t[:, j % 4, :], op_hi[:, j, :])
            act.wait_ge(gmT_ready, 1)
            act.wait_ge(gcol_ready, 1)
            gmT = aux[:, 3, :].rearrange("p (t k d r) -> p t k d r", t=TT, k=2, d=2)
            for d in range(2):
                nc.scalar.activation(floorc[:, :, d, :], gmT[:, :, 1, d, 0:HEADS], ACT.Exp, scale=-1.0).then_inc(floor_ready, 1)

            stage("za", zaT, ACT.Silu)
            for j in range(KT):
                head(win_t[:, j % 4, :], op_hi[:, j, :])
            stage("ga", mergedT, ACT.Sigmoid, ("b_merge", 0))

            _, a0, units = plan["qk"]

            def qk_body(u, q, first=False):
                for half in range(2):
                    slot = 2 * q + half
                    if not first:
                        act.wait_ge(conv_ready, u * 2 + half - 3)
                    evac(u + a0, (a0 + q) % 2, half, cpad[:, slot:slot + 1, 2:2 + S], ACT.Copy)

            def qk_silu(u, q):
                for half in range(2):
                    slot = 2 * q + half
                    act.wait_ge(conv_ready, u * 2 + half + 1)
                    nc.scalar.activation(qkT[:, bass.ds(u * 2 + half, 1), :], cacc[:, slot:slot + 1, :], ACT.Silu,
                                         bias=Vd("conv_b", u * 2 + half)).then_inc(silu_ready, 1)
            act.wait_ge(lo_ready, 16)
            act.wait_ge(acc_free, a0)
            qk_body(0, 0, True)
            qk_body(1, 1, True)
            qk_silu(0, 0)
            with act.Fori(1, units // 2) as i:
                qk_body(2 * i, 0)
                qk_silu(2 * i - 1, 1)
                qk_body(2 * i + 1, 1)
                qk_silu(2 * i, 0)
            qk_silu(units - 1, 1)

            _, a0, units = plan["v"]

            def v_body(u, q):
                s = (a0 + q) % 2
                for half in range(2):
                    act.wait_ge(acc_ready, u * 2 + 2 * a0 + 1 + half)
                    ins = nc.scalar.activation(vrow[:, 2 * half:2 * half + 2, bass.ds(u * VW, HD)],
                                               acc[:, 2 * s + half, :].rearrange("p (t c) -> p t c", t=2), ACT.Copy)
                    if half:
                        ins.then_inc(acc_free, 1)
            pairs(act, units, v_body)

            def decays():
                for j in range(TT):
                    for d in range(2):
                        n = seen["exp"]
                        seen["exp"] += 1
                        w = S - P * j if d == 0 else P * (j + 1)
                        act.wait_ge(arg_ready, n + 1)
                        tile = decay[:, n % 4, 0:w]
                        nc.scalar.activation(tile, tile, ACT.Exp, scale=-1.0).then_inc(d_ready, 1)

            _, a0, _ = plan["ozb"]
            decays()
            for h in range(HEADS):
                a = a0 + 2 * h
                act.wait_ge(acc_free, a)
                for half in range(2):
                    evac(a, a % 2, half, ogT[:, 2 * h + half:2 * h + half + 1, :], ACT.Sigmoid)
                for t in range(TT):
                    i = TT * h + t
                    b = 2 * (t % 2)
                    act.wait_ge(pv_ready, i + 1)
                    nc.scalar.activation(small[:, 16 + 2 * (t % 2):18 + 2 * (t % 2)], aux[:, b:b + 2, HD],
                                         ACT.Abs).then_inc(den_ready, 1)
                    act.wait_ge(rden_ready, i + 1)
                    nc.scalar.activation(hfwd[:, t % 2, :], aux[:, b, 0:HD], ACT.Copy,
                                         scale=small[:, 16 + 2 * (t % 2):17 + 2 * (t % 2)]).then_inc(hf_ready, 1)
                    act.wait_ge(hb_ready, i + 1)
                    nc.scalar.activation(hsq[:], hrow[:, t, :], ACT.Square,
                                         accum_out=small[:, t:t + 1]).then_inc(hssq_ready, 1)
                act.wait_ge(hssq_ready, TT * (h + 1))
                step(nc.scalar.activation(small[:, 4:8], small[:, 0:4], ACT.Ln, scale=1.0 / HD, bias=V("eps")))
                nc.scalar.activation(small[:, 8:12], small[:, 4:8], ACT.Exp, scale=-0.5).then_inc(hrs_ready, 1)
                if h + 1 < HEADS:
                    decays()
                a += 1
                for half in range(2):
                    act.wait_ge(acc_ready, 2 * a + 1 + half)
                    bank = acc[:, 2 * (a % 2) + half, :]
                    nc.scalar.activation(bank, bank, ACT.Silu).then_inc(zb_ready, 1)
            for j in range(KT):
                head(ogT[:, j, :], op_hi[:, j, :])
            memv = A["mem_2"][0].rearrange("(t p) d -> p t d", p=P)
            act.dma_start(memrow[:], memv).then_inc(mem_in, 16)
            act.dma_start(masks2[:], consts_d[:, 2 * P + 2 * S:]).then_inc(masks2_in, 16)
            stage("gb", gbT, ACT.Sigmoid, ("b_merge", KT))
            squares(memrow, memn, MT, 20, lambda t: act.wait_ge(mem_in, 16))
            for j in range(KT):
                head(mergedT[:, j, :], ht_hi[:, j, :])

            act.dma_start(xagain[:], xv).then_inc(post_in, 16)
            act.dma_start(gpost[:], A["norm_post_g"][0:1, :].to_broadcast([P, D])).then_inc(post_in, 16)
            heads_of_transposes("e_mem", memT[0][0], MEM)
            _, a0, units = plan["wout"]
            for u in range(units):
                for t in range(TT):
                    act.wait_ge(acc_ready, 2 * (a0 + u) + 1 + t // 2)
                    bank = acc[:, 2 * ((a0 + u) % 2) + t // 2, :]
                    c = UC * (t % 2)
                    nc.scalar.activation(junk[:, UC * t:UC * t + UC], bank[:, c:c + UC], ACT.Square,
                                         accum_out=stats[:, 5, units * t + u:units * t + u + 1]).then_inc(post_ssq, 1)
                act.wait_ge(post_ssq, TT * (u + 1))
            act.wait_ge(post_var, 1)
            nc.scalar.activation(small[:, 0:4], small[:, 0:4], ACT.Sqrt).then_inc(post_sd, 1)

            def head_norm_squares(a, half, cols, ahead=0):
                n = seen["hn"] + ahead + half
                act.wait_ge(acc_ready, 2 * a + 1 + half)
                if n >= 2:
                    act.wait_ge(sq_split, n - 1)
                nc.scalar.activation(hn_sq[:, n % 2, 0:cols], acc[:, 2 * (a % 2) + half, 0:cols], ACT.Square).then_inc(sq_ready, 1)

            def head_norm_rsqrt(cols):
                n0 = seen["hn"]
                for n in (n0, n0 + 1):
                    act.wait_ge(ssq_ready, n + 1)
                    if n >= 2:
                        act.wait_ge(hn_done, n - 1)
                    nc.scalar.activation(hn_rs[:, n % 2, 0:cols], aux[:, n % 2, 0:cols], ACT.Ln, scale=1.0 / HD2,
                                         bias=V("eps")).then_inc(ln_done, 1)
                for n in (n0, n0 + 1):
                    act.wait_ge(ln_done, n + 1)
                    nc.scalar.activation(hn_rs[:, n % 2, 0:cols], hn_rs[:, n % 2, 0:cols], ACT.Exp, scale=-0.5).then_inc(rs_ready, 1)
                seen["hn"] += 2

            def value_rows(a, dst, tiles, u):
                act.wait_ge(acc_free, a)
                for half in range(2):
                    act.wait_ge(acc_ready, 2 * a + 1 + half)
                    src = acc[:, 2 * (a % 2) + half, :]
                    if tiles == TT:
                        ins = nc.scalar.activation(dst[:, 2 * half:2 * half + 2, UC * u:UC * u + UC],
                                                   src.rearrange("p (t c) -> p t c", t=2), ACT.Copy)
                    else:
                        ins = nc.scalar.activation(dst[:, half, :], src[:, 0:UC], ACT.Copy)
                    if half:
                        ins.then_inc(acc_free, 1)

            jobs_done = 0
            for L, name in enumerate("eo"):
                qk, vv = LAYERS[L]
                _, a0, _ = plan[name + "_mem"]
                if L == 0:
                    for half in range(2):
                        head_norm_squares(a0, half, MEM)
                squares(xrow, xnrow, TT, 0,
                        lambda t: act.wait_ge(*((x_rows, t + 1) if L == 0 else (acc_free, plan["e_out"][1] + 4))))
                if L:
                    for half in range(2):
                        head_norm_squares(a0, half, MEM)
                heads_of_transposes(name + "_norm", ht_hi, S)
                value_rows(a0 + 1, mv, MT, 0)
                head_norm_rsqrt(MEM)
                if L:
                    act.wait_ge(gate_rows, 2)
                    softplus_of_minus_abs(frow[0:C_HEADS, 0, :], frow[0:C_HEADS, 1, :])
                _, a0, units = plan[name + "_qk"]
                for u in range(units):
                    for half in range(2):
                        head_norm_squares(a0 + u, half, S, 2 if u else 0)
                    if u:
                        head_norm_rsqrt(S)
                _, a0, units = plan[name + "_v"]
                for u in range(units):
                    value_rows(a0 + u, vv, TT, u)
                    if u == 0:
                        head_norm_rsqrt(S)
                az = plan[name + "_z"][1]

                jobs = JOBS[L]
                for i in range(len(jobs) + 7):
                    if L == 0 and i == 52:
                        act.dma_start(memrow[:], memv).then_inc(mem_in, 16)
                    if i < len(jobs):
                        job = jobs[i]
                        g = jobs_done + i
                        act.wait_ge(nm_ready, g + 1)
                        tile = pr[:, i % 4, 0:job.keys]
                        src = tile if job.bias is not None else logit_bank(i)[:, 0:job.keys]
                        if job.bias is None:
                            act.wait_ge(prT_ready, g - 3)
                        nc.scalar.activation(tile, src, ACT.Exp, scale=-1.0, bias=stats[:, 1, i:i + 1],
                                             accum_out=stats[:, 2, i:i + 1]).then_inc(pr_ready, 1)
                        if job.sink is not None:
                            nc.scalar.activation(stats[:, 3, i:i + 1], V("sinks", job.sink), ACT.Exp,
                                                 scale=-1.0, bias=stats[:, 1, i:i + 1]).then_inc(es_ready, 1)
                    if 1 <= i <= len(jobs):
                        k = i - 1
                        act.wait_ge(ri_ready, jobs_done + k + 1)
                        tile = pr[:, k % 4, 0:jobs[k].keys]
                        nc.scalar.activation(tile, tile, ACT.Copy, scale=stats[:, 4, k:k + 1]).then_inc(norm_ready, 1)
                    if z_due(i) is not None:
                        hu = z_due(i)
                        act.wait_ge(acc_ready, 2 * az + hu + 1)
                        if hu >= 2:
                            act.wait_ge(lo_ready, 32 + 8 * L + hu - 1)
                        nc.scalar.activation(zT[:, hu % 2, :], acc[:, hu % 2, :], ACT.Tanh, scale=0.5).then_inc(th_ready, 1)
                    if i >= 14 and (i - 14) % KT == 0:
                        j = (i - 14) // KT
                        head(zT[:, j % 2, :], op_hi[:, j, :])
                jobs_done += len(jobs)
                if L == 0:
                    squares(memrow, memn, MT, 20, lambda t: act.wait_ge(mem_in, 32))
                    heads_of_transposes("o_mem", memT[1][0], MEM)

        @block.vector
        def _(dve):
            step = Steps(dve, dve_step)
            seen = {"rssq": 0, "rsd": 0, "tr": 0, "t": 0, "lo": 0, "hn": 0, "arg": 0}
            v = nc.vector

            def normalise(src, dst, tiles, col, lag=1):
                for t in range(tiles):
                    c = small[:, col + t:col + t + 1]
                    seen["rssq"] += 1
                    dve.wait_ge(rssq_ready, seen["rssq"])
                    v.tensor_scalar(c, c, 1.0 / D, EPS, ALU.mult, ALU.add).then_inc(rvar_ready, 1)
                    if t >= lag:
                        scale_rows(src, dst, t - lag, col)
                if lag:
                    scale_rows(src, dst, tiles - 1, col)

            def scale_rows(src, dst, t, col):
                c = small[:, col + t:col + t + 1]
                seen["rsd"] += 1
                dve.wait_ge(rsd_ready, seen["rsd"])
                step(v.reciprocal(c, c))
                v.tensor_scalar(dst[:, t, :], src[:, t, :], c, None, ALU.mult).then_inc(xn_ready, 1)

            def rests_of_transposes(gain, hi, lo, cols, bank=tr_bank):
                for k in range(KT):
                    seen["tr"] += 1
                    dve.wait_ge(tr_hi, seen["tr"])
                    v.scalar_tensor_tensor(lo[:, k, :], bank(k)[:, 0:cols], V(gain, k),
                                           hi[:, k, :].bitcast(F32), ALU.mult, ALU.subtract).then_inc(tr_lo, 1)

            def rest(src, hi, lo):
                seen["lo"] += 1
                dve.wait_ge(hi_ready, seen["lo"])
                v.tensor_tensor(lo, src, hi.bitcast(F32), ALU.subtract).then_inc(lo_ready, 1)

            def tile_written(ins):
                ins.then_inc(t_ready, 1)
                seen["t"] += 1

            v.memset(small[:, 12:13], 1.0).then_inc(act_first, 1)
            v.memset(uT[:, :, 0:PAD], 0.0)
            step(v.memset(uT[:, :, PAD + S:UW], 0.0))
            normalise(xrow, xnrow, TT, 0, lag=0)
            dve.wait_ge(vecs_in, 16)
            rests_of_transposes("pre_g", ht_hi, ht_lo, S, first_bank)

            G = lambda i, lo=0, hi=64: grow[lo:hi, i, :]
            dve.wait_ge(acc_ready, 2)
            v.tensor_scalar(G(0), acc[0:64, 0, :], vecs[0:64, VC["b_i"]:VC["b_i"] + 1], None, ALU.add)
            v.tensor_copy(G(1), acc[64:128, 0, :]).then_inc(acc_free, 1)
            dve.wait_ge(acc_free, 1)
            v.tensor_scalar(G(1), G(1), vecs[0:64, VC["b_f"]:VC["b_f"] + 1], None, ALU.add).then_inc(gate_rows, 1)
            dve.wait_ge(gate_rows, 1)
            dve.wait_ge(gate_exp, 1)
            step(v.scalar_tensor_tensor(G(1), G(1), 0.0, G(2), ALU.min, ALU.subtract))
            step(v.tensor_tensor_scan(G(3), G(1), G(1), 0.0, ALU.add, ALU.bypass))
            v.tensor_copy(G(4, 0, 32), G(3, 0, 32))
            step(v.tensor_tensor(G(4, 32, 64), G(1, 32, 64), G(3, 32, 64), ALU.subtract))
            step(v.tensor_tensor(G(5), G(0), G(4), ALU.subtract))
            v.tensor_tensor_scan(rowmax[0:32, :], G(5, 0, 32), G(5, 0, 32), FLOOR, ALU.max, ALU.bypass)
            back = G(5, 32, 64)[:, ::-1]
            step(v.tensor_tensor_scan(rowmax[32:64, ::-1], back, back, FLOOR, ALU.max, ALU.bypass))
            v.tensor_tensor(G(5, 64, 128), G(4), rowmax[:], ALU.add).then_inc(gm_ready, 1)
            v.tensor_copy(ident_r[:], ident[:])
            step(v.tensor_copy(rowmax_hi[:], rowmax[:]))
            v.tensor_tensor(rowmax_lo[:], rowmax[:], rowmax_hi[:].bitcast(F32), ALU.subtract).then_inc(rowmax_split, 1)

            _, a0, units = plan["u"]
            for g, w in enumerate(WINDOWS):
                dve.wait_ge(acc_free, a0 + g + 1)
                for j in (2 * g, 2 * g + 1):
                    u = uT[:, j, :]
                    src, margin = u, 1
                    step(v.tensor_tensor(win_s[:, 0, 1:UW], u[:, 0:UW - 1], u[:, 1:UW], ALU.add))
                    cur, lo, hi, shift = 0, 1, UW, 1
                    while 2 * shift < w:
                        lo, hi = lo + shift, hi - shift
                        step(v.tensor_tensor(win_s[:, 1 - cur, lo:hi], win_s[:, cur, lo - shift:hi - shift],
                                             win_s[:, cur, lo + shift:hi + shift], ALU.add))
                        cur, shift = 1 - cur, 2 * shift
                    sums = win_s[:, cur, PAD:PAD + S]
                    ends = sums.rearrange("p (b c) -> p b c", c=PAD)[:, 0:S // PAD:S // PAD - 1, :]
                    edge = V("edge", 2 * PAD * g, 2 * PAD).rearrange("p (b c) -> p b c", c=PAD)
                    step(v.tensor_tensor(ends, ends, edge, ALU.mult))
                    if j >= 4:
                        dve.wait_ge(hi_ready, j - 3)
                    tile_written(v.scalar_tensor_tensor(win_t[:, j % 4, :], sums, 1.0 / w, u[:, PAD:PAD + S],
                                                        ALU.mult, ALU.subtract))
                    dve.wait_ge(t_ready, seen["t"])
                    if j:
                        rest(win_t[:, (j - 1) % 4, :], op_hi[:, j - 1, :], op_lo[:, j - 1, :])
            rest(win_t[:, (KT - 1) % 4, :], op_hi[:, KT - 1, :], op_lo[:, KT - 1, :])
            dve.wait_ge(gmT_ready, 1)
            gmT = aux[:, 3, :].rearrange("p (t k d r) -> p t k d r", t=TT, k=2, d=2)
            for d in range(2):
                ins = v.tensor_copy(gcol[:, :, d, :], gmT[:, :, 0, d, 0:HEADS])
            ins.then_inc(gcol_ready, 1)

            for name, j in (("e_qk", 0), ("e_qk", 2), ("e_qk", 4), ("o_qk", 0), ("o_qk", 2)):
                step(v.tensor_scalar(V(name, j), V(name, j), -HD2 ** -0.5, None, ALU.mult))
            step(v.tensor_scalar(V("sinks", 0, A_HEADS), V("sinks", 0, A_HEADS), -1.0, None, ALU.mult))

            _, a0, _ = plan["mix"]
            dve.wait_ge(acc_free, a0)
            for g in range(4):
                s = (a0 + g) % 2
                dve.wait_ge(acc_ready, 2 * (a0 + g + 1))
                for half in range(2):
                    j = 2 * g + half
                    dve.wait_ge(hi_ready, 8 + j - 3)
                    tile_written(v.scalar_tensor_tensor(win_t[:, j % 4, :], acc[:, 2 * s + half, :], V("pool_scale", j),
                                                        zaT[:, j, :], ALU.mult, ALU.mult))
                dve.wait_ge(t_ready, seen["t"])
                dve.sem_inc(acc_free, 1)
                for j in (2 * g, 2 * g + 1):
                    rest(win_t[:, j % 4, :], op_hi[:, j, :], op_lo[:, j, :])

            _, a0, units = plan["pa"]
            dve.wait_ge(acc_free, a0)

            def pa_body(u, q):
                for half in range(2):
                    dve.wait_ge(acc_ready, u * 2 + 2 * a0 + 1 + half)
                    m = mergedT[:, bass.ds(u * 2 + half, 1), :]
                    b = 2 * ((a0 + q) % 2) + half
                    ins = v.tensor_tensor(m, acc[:, b:b + 1, :], m, ALU.mult)
                    if half:
                        ins.then_inc(acc_free, 1)
            pairs(dve, units, pa_body)

            _, a0, units = plan["qk"]
            dve.wait_ge(acc_free, a0)
            v.memset(cpad[:, :, 0:2], 0.0)
            step(v.memset(cpad[:, :, 2 + S:CW], 0.0))

            def conv(u, q, first=False):
                dve.wait_ge(acc_free, u + a0 + 1)
                for half in range(2):
                    slot = 2 * q + half
                    if not first:
                        dve.wait_ge(silu_ready, u * 2 + half - 3)
                    out_ = cacc[:, slot, :]
                    tap = lambda k: Vd("conv_w", u * (2 * TAPS) + half * TAPS + k)
                    step(v.tensor_scalar(out_, cpad[:, slot, 0:S], tap(0), None, ALU.mult))
                    for k in range(1, TAPS):
                        ins = v.scalar_tensor_tensor(out_, cpad[:, slot, k:k + S], tap(k), out_, ALU.mult, ALU.add)
                        if k < TAPS - 1:
                            step(ins)
                        else:
                            ins.then_inc(conv_ready, 1)
            conv(0, 0, True)
            conv(1, 1, True)

            def conv_pair(i):
                conv(2 * i + 2, 0)
                conv(2 * i + 3, 1)
            step.loop(units // 2 - 1, 4 * (TAPS - 1), conv_pair)
            step(v.memset(vrow[:, :, :].rearrange("p t (h c) -> p t h c", h=HEADS)[:, :, :, HD:VW], 1.0))

            def decay_args(h, j):
                if TT * h + j >= 2:
                    dve.wait_ge(p_ready, TT * h + j - 1)
                for d in range(2):
                    lo, hi = (P * j, S) if d == 0 else (0, P * (j + 1))
                    w = hi - lo
                    dve.wait_ge(mbc_ready, h + 1)
                    mask = masks1[:, 0, 0:w] if d == 0 else masks1[:, 1, S - w:S]
                    v.scalar_tensor_tensor(decay[:, seen["arg"] % 4, 0:w], aux[:, d, lo:hi], gcol[:, j, d, h:h + 1],
                                           mask, ALU.subtract, ALU.max).then_inc(arg_ready, 1)
                    seen["arg"] += 1

            def probabilities(h):
                if h:
                    dve.wait_ge(pv_ready, TT * h)
                decay_args(h, 0)
                for j in range(TT):
                    if j + 1 < TT:
                        decay_args(h, j + 1)
                    dve.wait_ge(s_ready, TT * h + j + 1)
                    for d in range(2):
                        n = 2 * (TT * h + j) + d
                        lo, hi = (P * j, S) if d == 0 else (0, P * (j + 1))
                        dve.wait_ge(d_ready, n + 1)
                        ins = v.scalar_tensor_tensor(prob[:, d, j, lo:hi], aux[:, 2 + j % 2, lo:hi], HD ** -0.5,
                                                     decay[:, n % 4, 0:hi - lo], ALU.mult, ALU.mult)
                    ins.then_inc(p_ready, 1)

            dve.wait_ge(consts_in, 32)
            probabilities(0)
            _, a0, _ = plan["ozb"]
            for h in range(HEADS):
                for t in range(TT):
                    i = TT * h + t
                    b = 2 * (t % 2)
                    c = 16 + 2 * (t % 2)
                    dve.wait_ge(den_ready, i + 1)
                    if i == 0:
                        dve.wait_ge(floor_ready, 2)
                    step(v.tensor_tensor(small[:, c:c + 2], small[:, c:c + 2], floorc[:, t, :, h], ALU.max))
                    v.reciprocal(small[:, c:c + 2], small[:, c:c + 2]).then_inc(rden_ready, 1)
                    dve.wait_ge(rden_ready, i + 1)
                    dve.wait_ge(hf_ready, i + 1)
                    v.scalar_tensor_tensor(hrow[:, t, :], aux[:, b + 1, 0:HD], small[:, c + 1:c + 2], hfwd[:, t % 2, :],
                                           ALU.mult, ALU.add).then_inc(hb_ready, 1)
                dve.wait_ge(hrs_ready, h + 1)
                for t in range(TT):
                    ins = v.tensor_scalar(hrow[:, t, :], hrow[:, t, :], small[:, 8 + t:9 + t], None, ALU.mult)
                ins.then_inc(hbn_ready, 1)
                if h + 1 < HEADS:
                    probabilities(h + 1)
                a = a0 + 2 * h + 1
                dve.wait_ge(acc_free, a)
                for half in range(2):
                    dve.wait_ge(zb_ready, 2 * h + half + 1)
                    og = ogT[:, 2 * h + half, :]
                    ins = v.tensor_tensor(og, acc[:, 2 * (a % 2) + half, :], og, ALU.mult)
                ins.then_inc(acc_free, 1)
                dve.wait_ge(acc_free, a + 1)
                for e in range(2):
                    j = 2 * h + e
                    dve.wait_ge(hT_ready, j + 1)
                    tile_written(v.scalar_tensor_tensor(ogT[:, j, :], aux[:, e, :], V("mlstm_g", j), ogT[:, j, :],
                                                        ALU.mult, ALU.mult))
            for j in range(KT):
                rest(ogT[:, j, :], op_hi[:, j, :], op_lo[:, j, :])

            normalise(memrow, memn, MT, 20)
            _, a0, units = plan["pb"]
            dve.wait_ge(acc_free, a0)
            for u in range(units):
                for half in range(2):
                    j = 2 * u + half
                    dve.wait_ge(acc_ready, 2 * (a0 + u) + 1 + half)
                    ins = v.tensor_tensor(gbT[:, j, :], acc[:, 2 * ((a0 + u) % 2) + half, :], gbT[:, j, :], ALU.mult)
                    if half:
                        ins.then_inc(acc_free, 1)
                        dve.wait_ge(acc_free, a0 + u + 1)
                    else:
                        step(ins)
                    tile_written(v.tensor_tensor(mergedT[:, j, :], mergedT[:, j, :], gbT[:, j, :], ALU.add))
                for j in (2 * u, 2 * u + 1):
                    rest(mergedT[:, j, :], ht_hi[:, j, :], ht_lo[:, j, :])
            rests_of_transposes("e_mem", *memT[0], MEM)
            dve.wait_ge(masks2_in, 16)
            v.tensor_copy(causal_r[:], masks2[:, S:S + P])
            v.tensor_copy(bones_r[:], bones[:]).then_inc(consts_r_ready, 1)

            _, a0, units = plan["wout"]
            dve.wait_ge(post_in, 32)
            dve.wait_ge(acc_free, a0)

            def gain(u, half):
                dve.wait_ge(post_ssq, TT * u + 2 * half + 2)
                cols = slice(UC * u, UC * u + UC)
                for t in (2 * half, 2 * half + 1):
                    c = UC * (t % 2)
                    ins = v.tensor_tensor(orow1[:, t, cols], acc[:, 2 * ((a0 + u) % 2) + half, c:c + UC],
                                          gpost[:, cols], ALU.mult)
                if half:
                    ins.then_inc(acc_free, 1)
            for u in range(units):
                gain(u, 0)
                if u < units - 1:
                    gain(u, 1)
            dve.wait_ge(post_ssq, TT * units)
            step(v.reduce_sum(small[:, 0:4], stats[:, 5, 0:16].rearrange("p (t u) -> p t u", t=TT), AX.X))
            v.tensor_scalar(small[:, 0:4], small[:, 0:4], 1.0 / D, EPS, ALU.mult, ALU.add).then_inc(post_var, 1)
            gain(units - 1, 1)
            dve.wait_ge(acc_free, a0 + units)
            dve.wait_ge(post_sd, 1)
            step(v.reciprocal(small[:, 4:8], small[:, 0:4]))
            for t in range(TT):
                v.scalar_tensor_tensor(xrow[:, t, :], orow1[:, t, :], small[:, 4 + t:5 + t], xagain[:, t, :],
                                       ALU.mult, ALU.add).then_inc(x_rows, 1)

            def head_norm_raw(a, half, dst, split_now=True):
                n = seen["hn"] + half
                dve.wait_ge(sq_ready, n + 1)
                dve.wait_ge(acc_free, a)
                ins = v.tensor_copy(dst, acc[:, 2 * (a % 2) + half, 0:dst.shape[-1]])
                if half:
                    ins.then_inc(acc_free, 1)
                if split_now:
                    head_norm_split(half, dst.shape[-1])

            def head_norm_split(half, cols):
                n = seen["hn"] + half
                if n >= 2:
                    dve.wait_ge(ssq_ready, n - 1)
                step(v.tensor_copy(hn_hi[:, n % 2, 0:cols], hn_sq[:, n % 2, 0:cols]))
                v.tensor_tensor(hn_lo[:, n % 2, 0:cols], hn_sq[:, n % 2, 0:cols], hn_hi[:, n % 2, 0:cols].bitcast(F32),
                                ALU.subtract).then_inc(sq_split, 1)

            def head_norm_scale(n, a, dst, gain):
                dve.wait_ge(acc_free, a + 1)
                dve.wait_ge(rs_ready, n + 1)
                v.scalar_tensor_tensor(dst, dst, gain, hn_rs[:, n % 2, 0:dst.shape[-1]],
                                       ALU.mult, ALU.mult).then_inc(hn_done, 1)

            done = 0
            for L, name in enumerate("eo"):
                qk, _ = LAYERS[L]
                a0 = plan[name + "_mem"][1]
                if L == 0:
                    for half in range(2):
                        head_norm_raw(a0, half, mkT[:, half, :], split_now=False)
                    normalise(xrow, xnrow, TT, 0)
                else:
                    normalise(xrow, xnrow, TT, 0)
                    for half in range(2):
                        head_norm_raw(a0, half, mkT[:, half, :])
                rests_of_transposes(name + "_norm", ht_hi, ht_lo, S)
                if L == 0:
                    for half in range(2):
                        head_norm_split(half, MEM)
                for half in range(2):
                    head_norm_scale(seen["hn"] + half, a0, mkT[:, half, :], V(name + "_qk", 5 if L == 0 else 3))
                seen["hn"] += 2
                if L:
                    a = plan["o_f"][1]
                    dve.wait_ge(acc_ready, 2 * (a + 1))
                    dve.wait_ge(acc_free, a)
                    R = lambda i: frow[0:C_HEADS, i, :]
                    v.tensor_copy(R(0), acc[0:C_HEADS, 2 * (a % 2), :]).then_inc(acc_free, 1)
                    dve.wait_ge(acc_free, a + 1)
                    v.tensor_scalar(R(0), R(0), vecs[0:C_HEADS, VC["o_bf"]:VC["o_bf"] + 1], None, ALU.add).then_inc(gate_rows, 1)
                    dve.wait_ge(gate_rows, 2)
                    dve.wait_ge(gate_exp, 2)
                    step(v.scalar_tensor_tensor(R(1), R(0), 0.0, R(1), ALU.min, ALU.subtract))
                    step(v.tensor_tensor_scan(R(2), R(1), R(1), 0.0, ALU.add, ALU.bypass))
                    v.tensor_copy(csum[:], R(2)).then_inc(csum_ready, 1)
                _, a0, units = plan[name + "_qk"]

                def scale_unit(u):
                    for half in range(2):
                        j = 2 * u + half
                        head_norm_scale(seen["hn"] - 2 + half, a0 + u, qk[:, j, :], V(name + "_qk", QK_GAINS[L][j]))
                for u in range(units):
                    for half in range(2):
                        head_norm_raw(a0 + u, half, qk[:, 2 * u + half, :])
                    if u:
                        scale_unit(u - 1)
                    seen["hn"] += 2
                scale_unit(units - 1)

                jobs = JOBS[L]
                az = plan[name + "_z"][1]
                DIST, WINDOW = masks2[:, 0:S], masks2[:, S + P:S + P + 2 * WIN]
                for i in range(len(jobs) + 8):
                    if i < len(jobs):
                        job, g = jobs[i], done + i
                        logits = logit_bank(i)[:, 0:job.keys]
                        least = stats[:, 1, i:i + 1]
                        if job.bias is not None:
                            kind, h, slope = job.bias
                            if kind == "forget":
                                if job.t == 0:
                                    dve.wait_ge(csum_in[job.slot], 16 * (h // 3 + 1))
                                tile = csum_all[:, job.slot, 0:job.keys]
                            else:
                                full = DIST if kind == "dist" else WINDOW
                                tile = bias_h[:, job.slot, 0:full.shape[-1]]
                                if job.t == 0:
                                    step(v.tensor_scalar(tile, full, slope, None, ALU.mult))
                            width = tile.shape[-1]
                            if g >= 4:
                                dve.wait_ge(prT_ready, g - 3)
                            dve.wait_ge(logit_ready, g + 1)
                            ins = v.tensor_tensor_reduce(out=pr[:, i % 4, 0:job.keys], in0=logits,
                                                         in1=tile[:, width - job.keys:width], scale=1.0, scalar=-FLOOR,
                                                         op0=ALU.add, op1=ALU.min, accum_out=least)
                        else:
                            dve.wait_ge(logit_ready, g + 1)
                            ins = v.tensor_reduce(least, logits, AX.X, ALU.min)
                        if job.sink is not None:
                            step(ins)
                            ins = v.tensor_scalar(least, least, V("sinks", job.sink), None, ALU.min)
                        ins.then_inc(nm_ready, 1)
                    if 1 <= i <= len(jobs):
                        k = i - 1
                        dve.wait_ge(pr_ready, done + k + 1)
                        if jobs[k].sink is not None:
                            dve.wait_ge(es_ready, k + 1)
                            step(v.tensor_tensor(stats[:, 2, k:k + 1], stats[:, 2, k:k + 1], stats[:, 3, k:k + 1], ALU.add))
                        v.reciprocal(stats[:, 4, k:k + 1], stats[:, 2, k:k + 1]).then_inc(ri_ready, 1)
                    if 4 <= i < len(jobs) + 4:
                        k = i - 4
                        dve.wait_ge(prT_ready, done + k + 1)
                        if done + k >= 4:
                            dve.wait_ge(o_ready, (done + k) // 2 - 1)
                        v.tensor_copy(prT[k % 4][:, 0:jobs[k].keys], trans_bank(k)[:, 0:jobs[k].keys]).then_inc(prT_copied, 1)
                    if z_due(i) is not None:
                        hu = z_due(i)
                        dve.wait_ge(th_ready, 8 * L + hu + 1)
                        tile = zT[:, hu % 2, :]
                        ins = v.scalar_tensor_tensor(tile, tile, 1.0, acc[:, hu % 2, :], ALU.add, ALU.mult)
                        if hu % 2 == 0:
                            ins.then_inc(z_half, 1)
                        else:
                            if hu == 1:
                                dve.wait_ge(acc_free, az)
                            ins.then_inc(acc_free, 1)
                    if i >= 13 and (i - 13) % KT == 0 and i < len(jobs) + 7:
                        j = (i - 13) // KT
                        dve.wait_ge(o_ready, done // 2 + TT * (j + 1))
                        if j % 2:
                            dve.wait_ge(acc_free, az + j // 2 + 1)
                        else:
                            dve.wait_ge(z_half, 4 * L + j // 2 + 1)
                        tile_written(v.scalar_tensor_tensor(zT[:, j % 2, :], out_bank(j), 0.5, zT[:, j % 2, :],
                                                            ALU.mult, ALU.mult))
                    if i >= 15 and (i - 15) % KT == 0:
                        j = (i - 15) // KT
                        rest(zT[:, j % 2, :], op_hi[:, j, :], op_lo[:, j, :])
                done += len(jobs)
                if L == 0:
                    normalise(memrow, memn, MT, 20)
                _, a0, units = plan[name + "_out"]

                def residual(u, q):
                    for half in range(2):
                        dve.wait_ge(acc_ready, u * 2 + 2 * a0 + 1 + half)
                        rows = xrow[:, 2 * half:2 * half + 2, bass.ds(u * UC, UC)]
                        bank = acc[:, 2 * ((a0 + q) % 2) + half, :].rearrange("p (t c) -> p t c", t=2)
                        ins = v.tensor_tensor(rows, bank, rows, ALU.add)
                        if half:
                            ins.then_inc(acc_free, 1)
                        elif L == 1 and u == units - 1:
                            ins.then_inc(last_rows, 1)
                for u in range(units):
                    residual(u, u % 2)
                    if L == 0 and u == 0:
                        rests_of_transposes("o_mem", *memT[1], MEM)

        @block.tensor
        def _(pe):
            seen = {"xn": 0, "tr": 0, "hn": 0}
            mm = nc.tensor.matmul

            def product(out_, w_hi_, w_lo_, x_hi, x_lo, first, last):
                mm(out_, w_hi_, x_hi, start=first, stop=False)
                mm(out_, w_hi_, x_lo, start=False, stop=False)
                return mm(out_, w_lo_, x_hi, start=False, stop=last)

            def unit_waits(n, a):
                pe.wait_ge(w_split, n + 1)
                if not (isinstance(a, int) and a < 2):
                    pe.wait_ge(acc_free, a - 1)

            def by_channels(n, a, s, b, x_hi, x_lo, cols=S):
                unit_waits(n, a)
                for half in range(2):
                    channel_half(s, b, half, x_hi, x_lo, cols)

            def channel_half(s, b, half, x_hi, x_lo, cols=S, tiles_split=None):
                for k in range(KT):
                    if tiles_split is not None and half == 0:
                        next_tile(tiles_split, k)
                    c = k * UC + half * P
                    ins = product(acc[:, 2 * b + half, 0:cols], whi[:, s, c:c + P], wlo[:, s, c:c + P],
                                  x_hi[:, k, :], x_lo[:, k, :], k == 0, k == KT - 1)
                ins.then_inc(acc_ready, 1)

            def by_rows(n, a, s, b, x_hi, x_lo, tiles=TT):
                unit_waits(n, a)
                per = tiles // 2
                for t in range(tiles):
                    out_ = acc[:, 2 * b + t // per, UC * (t % per):UC * (t % per) + UC]
                    for k in range(KT):
                        ins = product(out_, x_hi[:, k, P * t:P * t + P], x_lo[:, k, P * t:P * t + P],
                                      whi[:, s, k * UC:k * UC + UC], wlo[:, s, k * UC:k * UC + UC], k == 0, k == KT - 1)
                    if t % per == per - 1:
                        ins.then_inc(acc_ready, 1)

            def rows_as_tiles_come(n, a, s, b, x_hi, x_lo, rests_before, tiles=range(KT)):
                if tiles[0] == 0:
                    unit_waits(n, a)
                for k in tiles:
                    pe.wait_ge(lo_ready, rests_before + k + 1)
                    for t in range(TT):
                        ins = product(acc[:, 2 * b + t // 2, UC * (t % 2):UC * (t % 2) + UC],
                                      x_hi[:, k, P * t:P * t + P], x_lo[:, k, P * t:P * t + P],
                                      whi[:, s, k * UC:k * UC + UC], wlo[:, s, k * UC:k * UC + UC],
                                      k == 0 and t % 2 == 0, k == KT - 1 and t % 2 == 1)
                        if k == KT - 1 and t % 2:
                            ins.then_inc(acc_ready, 1)

            def rows_stage(name, x_hi, x_lo, rests_before, mem_after, first=0):
                n0, a0, units = plan[name]
                for u in range(units):
                    n, a = n0 + u, a0 + u
                    if u == 0:
                        rows_as_tiles_come(n, a, n % 2, a % 2, x_hi, x_lo, rests_before, range(first, KT))
                    else:
                        by_rows(n, a, n % 2, a % 2, x_hi, x_lo)
                    if u == mem_after:
                        transposes(memn, MT)

            def stage(name, kind, x_hi, x_lo, peel=0):
                n0, a0, units = plan[name]
                pairs(pe, units, lambda u, q: kind(u + n0, u + a0, (n0 + q) % 2, (a0 + q) % 2, x_hi, x_lo), peel)

            def row_transpose(t, k):
                return nc.tensor.transpose(aux[:, k % 4, P * t:P * t + P], xnrow[:, t, P * k:P * k + P], ident[:])

            def next_tile(before, k):
                if 1 <= k and k + 3 < KT:
                    for t in range(TT):
                        ins = row_transpose(t, k + 3)
                    ins.then_inc(tr_ready, 1)
                pe.wait_ge(tr_lo, before + k + 1)

            def transposes(rows, tiles):
                seen["xn"] += tiles
                pe.wait_ge(xn_ready, seen["xn"])
                for k in range(KT):
                    if seen["tr"] >= 4:
                        pe.wait_ge(tr_lo, seen["tr"] - 3)
                    for t in range(tiles):
                        ins = nc.tensor.transpose(aux[:, k % 4, P * t:P * t + P], rows[:, t, P * k:P * k + P], ident[:])
                    ins.then_inc(tr_ready, 1)
                    seen["tr"] += 1

            pe.wait_ge(ident_in, 16)
            for t in range(TT):
                seen["xn"] += 1
                pe.wait_ge(xn_ready, seen["xn"])
                for k in range(KT):
                    ins = nc.tensor.transpose(first_bank(k)[:, P * t:P * t + P], xnrow[:, t, P * k:P * k + P], ident[:])
                    if t == TT - 1:
                        ins.then_inc(tr_ready, 1)
            seen["tr"] += KT
            pe.wait_ge(w_split, 1)
            for k in range(KT):
                pe.wait_ge(tr_lo, k + 1)
                ins = product(acc[:, 0, :], whi[:, 0, P * k:P * k + P], wlo[:, 0, P * k:P * k + P],
                              ht_hi[:, k, :], ht_lo[:, k, :], k == 0, k == KT - 1)
            ins.then_inc(acc_ready, 2)
            stage("u", by_channels, ht_hi, ht_lo, peel=1)
            pe.wait_ge(gm_ready, 1)
            for t in range(TT):
                ins = nc.tensor.transpose(aux[:, 3, P * t:P * t + P], grow[:, 5, P * t:P * t + P], ident[:])
            ins.then_inc(gmT_ready, 1)
            stage("za", by_channels, ht_hi, ht_lo)
            n, a0, _ = plan["mix"]
            pe.wait_ge(lo_ready, 8)
            for g in range(4):
                unit_waits(n, a0 + g)
                for m in range(2):
                    for kk in range(2):
                        c = (2 * g + kk) * UC + P * m
                        ins = product(acc[:, 2 * ((a0 + g) % 2) + m, :], whi[:, n % 2, c:c + P], wlo[:, n % 2, c:c + P],
                                      op_hi[:, 2 * g + kk, :], op_lo[:, 2 * g + kk, :], kk == 0, kk == 1)
                    ins.then_inc(acc_ready, 1)
            stage("ga", by_channels, ht_hi, ht_lo)
            pe.wait_ge(lo_ready, 16)
            stage("pa", by_channels, op_hi, op_lo)
            stage("qk", by_channels, ht_hi, ht_lo)
            stage("v", by_rows, ht_hi, ht_lo)

            def scores(h):
                if h:
                    pe.wait_ge(hb_ready, TT * h)
                    if h > 1:
                        pe.wait_ge(t_ready, 16 + 2 * (h - 1))
                else:
                    pe.wait_ge(silu_ready, 2 * KT)
                    pe.wait_ge(floor_ready, 2)
                for d in range(2):
                    r = 32 * d + h
                    one_row = ident_r[0:64, r:r + 1].to_broadcast([64, P])
                    mm(aux[:, d, :], one_row, rowmax_hi[0:64, :], start=True, stop=False)
                    ins = mm(aux[:, d, :], one_row, rowmax_lo[0:64, :], start=False, stop=True)
                ins.then_inc(mbc_ready, 1)
                score_tiles(h, (0, 1))

            def score_tiles(h, tiles):
                for j in tiles:
                    if j >= 2:
                        pe.wait_ge(p_ready, TT * h + j - 1)
                    for kk in range(2):
                        ins = mm(aux[:, 2 + j % 2, :], qkT[:, KT + 2 * h + kk, P * j:P * j + P], qkT[:, 2 * h + kk, :],
                                 start=kk == 0, stop=kk == 1)
                    ins.then_inc(s_ready, 1)

            def values(h):
                pe.wait_ge(p_ready, TT * (h + 1))
                if h:
                    pe.wait_ge(t_ready, 16 + 2 * h)
                for t in range(TT):
                    if t >= 2:
                        pe.wait_ge(hb_ready, TT * h + t - 1)
                    for d in range(2):
                        keys = range(0, t + 1) if d == 0 else range(t, TT)
                        for j in keys:
                            ins = mm(aux[:, 2 * (t % 2) + d, 0:VW], prob[:, d, j, P * t:P * t + P],
                                     vrow[:, j, VW * h:VW * h + VW], start=j == keys[0], stop=j == keys[-1])
                    ins.then_inc(pv_ready, 1)

            def output_transposes(h):
                pe.wait_ge(hbn_ready, h + 1)
                if h + 1 < HEADS:
                    pe.wait_ge(p_ready, TT * (h + 2))
                for e in range(2):
                    for t in range(TT):
                        ins = nc.tensor.transpose(aux[:, e, P * t:P * t + P], hrow[:, t, P * e:P * e + P], ident[:])
                    ins.then_inc(hT_ready, 1)

            n0, a0, _ = plan["ozb"]
            pe.wait_ge(acc_free, a0)
            pe.wait_ge(consts_in, 32)
            pe.wait_ge(rowmax_split, 1)
            scores(0)
            for h in range(HEADS):
                n, a = n0 + 2 * h, a0 + 2 * h
                unit_waits(n, a)
                channel_half(n % 2, a % 2, 0, ht_hi, ht_lo)
                if h == 0:
                    score_tiles(0, (2, 3))
                else:
                    output_transposes(h - 1)
                channel_half(n % 2, a % 2, 1, ht_hi, ht_lo)
                values(h)
                n, a = n + 1, a + 1
                unit_waits(n, a)
                channel_half(n % 2, a % 2, 0, ht_hi, ht_lo)
                if h + 1 < HEADS:
                    scores(h + 1)
                channel_half(n % 2, a % 2, 1, ht_hi, ht_lo)
                if h + 1 < HEADS:
                    score_tiles(h + 1, (2, 3))
            output_transposes(HEADS - 1)
            stage("gb", by_channels, ht_hi, ht_lo)
            pe.wait_ge(lo_ready, 24)
            stage("pb", by_channels, op_hi, op_lo)
            rows_stage("wout", ht_hi, ht_lo, 24, 0)

            def sum_squares(cols):
                n = seen["hn"]
                pe.wait_ge(sq_split, n + 1)
                if n >= 2:
                    pe.wait_ge(ln_done, n - 1)
                mm(aux[:, n % 2, 0:cols], bones_r[:], hn_hi[:, n % 2, 0:cols], start=True, stop=False)
                mm(aux[:, n % 2, 0:cols], bones_r[:], hn_lo[:, n % 2, 0:cols], start=False, stop=True).then_inc(ssq_ready, 1)
                seen["hn"] += 1

            done = 0
            for L, name in enumerate("eo"):
                qk, vv = LAYERS[L]
                pe.wait_ge(tr_lo, seen["tr"])
                if L == 0:
                    pe.wait_ge(consts_r_ready, 1)
                n0, a0, _ = plan[name + "_mem"]
                by_channels(n0, a0, n0 % 2, a0 % 2, *memT[L], MEM)
                early = 2 * L
                if early:
                    pe.wait_ge(xn_ready, seen["xn"] + early)
                    for k in range(4):
                        for t in range(early):
                            row_transpose(t, k)
                by_rows(n0 + 1, a0 + 1, (n0 + 1) % 2, (a0 + 1) % 2, *memT[L], MT)
                seen["xn"] += TT
                pe.wait_ge(xn_ready, seen["xn"])
                for k in range(4):
                    for t in range(early, TT):
                        ins = row_transpose(t, k)
                    ins.then_inc(tr_ready, 1)
                split_before = seen["tr"]
                seen["tr"] += KT
                if L:
                    n, a, _ = plan["o_f"]
                    unit_waits(n, a)
                    for k in range(KT):
                        next_tile(split_before, k)
                        ins = product(acc[:, 2 * (a % 2), :], whi[:, n % 2, P * k:P * k + P],
                                      wlo[:, n % 2, P * k:P * k + P], ht_hi[:, k, :], ht_lo[:, k, :], k == 0, k == KT - 1)
                    ins.then_inc(acc_ready, 2)
                n0, a0, units = plan[name + "_qk"]
                for u in range(units):
                    if L or u:
                        if u == 0:
                            sum_squares(MEM)
                            sum_squares(MEM)
                        by_channels(n0 + u, a0 + u, (n0 + u) % 2, (a0 + u) % 2, ht_hi, ht_lo)
                    else:
                        unit_waits(n0, a0)
                        for half in range(2):
                            channel_half(n0 % 2, a0 % 2, half, ht_hi, ht_lo, S, split_before)
                        sum_squares(MEM)
                        sum_squares(MEM)
                    if u:
                        sum_squares(S)
                        sum_squares(S)
                n0, a0, units = plan[name + "_v"]
                for u in range(units):
                    by_rows(n0 + u, a0 + u, (n0 + u) % 2, (a0 + u) % 2, ht_hi, ht_lo)
                    if u == 0:
                        sum_squares(S)
                        sum_squares(S)

                def z_product(i):
                    u, half, k = i // (2 * KT), i // KT % 2, i % KT
                    n0, a0, _ = plan[name + "_z"]
                    n, a = n0 + u, a0 + u
                    if k == 0 and half == 0:
                        pe.wait_ge(w_split, n + 1)
                        if u:
                            pe.wait_ge(z_half, 4 * L + u)
                    if k == 0 and half and u:
                        pe.wait_ge(acc_free, a)
                    c = k * UC + half * P
                    ins = product(acc[:, half, :], whi[:, n % 2, c:c + P], wlo[:, n % 2, c:c + P],
                                  ht_hi[:, k, :], ht_lo[:, k, :], k == 0, k == KT - 1)
                    if k == KT - 1:
                        ins.then_inc(acc_ready, 1)

                jobs = JOBS[L]
                n_out, a_out, _ = plan[name + "_out"]
                pe.wait_ge(acc_free, plan[name + "_z"][1])
                pe.wait_ge(hn_done, seen["hn"])
                for i in range(len(jobs) + 5):
                    if i < len(jobs):
                        job, g = jobs[i], done + i
                        if i >= 2:
                            pe.wait_ge(nm_ready if jobs[i - 2].bias is not None else pr_ready, g - 1)
                        (qt, qp), (kt_, kp) = job.q, job.k
                        keysT = mkT if job.bias is None else qk
                        out_ = logit_bank(i)[:, 0:job.keys]
                        k0 = P * job.k0
                        forget = job.bias is not None and job.bias[0] == "forget"
                        ins = mm(out_, qk[qp:qp + HD2, qt, P * job.t:P * job.t + P],
                                 keysT[kp:kp + HD2, kt_, k0:k0 + job.keys], start=True, stop=not forget)
                        if forget:
                            ins = mm(out_[:, job.keys - P:job.keys], ident_r[:], causal_r[:], start=False, stop=True)
                        ins.then_inc(logit_ready, 1)
                        z_product(i)
                    if 3 <= i < len(jobs) + 3:
                        k = i - 3
                        pe.wait_ge(norm_ready, done + k + 1)
                        if done + k >= 2:
                            pe.wait_ge(prT_copied, done + k - 1)
                        for b in range(jobs[k].keys // P):
                            ins = nc.tensor.transpose(trans_bank(k)[:, P * b:P * b + P], pr[:, k % 4, P * b:P * b + P], ident[:])
                        ins.then_inc(prT_ready, 1)
                    if i == len(jobs) + 2:
                        pe.wait_ge(acc_free, a_out)
                        pe.wait_ge(pr_ready, done + len(jobs))
                        rows_as_tiles_come(n_out, a_out, n_out % 2, a_out % 2, op_hi, op_lo, 32 + 8 * L, range(0, 3))
                    if i >= 6 and i % 2 == 0:
                        pair = (i - 6, i - 5)
                        pe.wait_ge(prT_copied, done + i - 4)
                        job = jobs[pair[0]]
                        j, nb = pair[0] // KT, job.keys // P
                        if job.t == 0 and (L or j >= 2):
                            pe.wait_ge(t_ready, 31 + 8 * L + j)
                        for b in range(nb):
                            for e, k in enumerate(pair):
                                vals = (mv if job.bias is None else vv)[:, job.k0 + b, jobs[k].v:jobs[k].v + HD2]
                                ins = mm(out_bank(j)[HD2 * e:HD2 * e + HD2, P * job.t:P * job.t + P], vals,
                                         prT[k % 4][:, P * b:P * b + P], start=b == 0, stop=b == nb - 1)
                        ins.then_inc(o_ready, 1)
                done += len(jobs)
                rows_stage(name + "_out", op_hi, op_lo, 32 + 8 * L, 1 if L == 0 else None, 3)


def columns(v):
    return np.ascontiguousarray(np.reshape(v, (-1, P)).T)


def pack(inputs):
    vecs = np.zeros((P, NVEC), np.float32)

    def put(name, block, rows=slice(None)):
        vecs[rows, VC[name]:VC[name] + block.shape[1]] = block
    put("pre_g", columns(inputs["norm_pre_g"][0]))
    put("conv_w", inputs["conv_qk_w"][0].reshape(TAPS, 16, P).transpose(2, 1, 0).reshape(P, 16 * TAPS))
    put("conv_b", columns(inputs["conv_qk_b"][0]))
    put("pool_scale", columns(inputs["pool_scale"][0]))
    put("mlstm_g", columns(inputs["mlstm_norm_g"][0]))
    put("b_merge", columns(inputs["b_merge"][0]))
    put("e_norm", columns(inputs["e_norm_2"][0]))
    put("e_mem", columns(inputs["e_mem_norm_2"][0]))
    put("o_norm", columns(inputs["o_norm_2"][0]))
    put("o_mem", columns(inputs["o_mem_norm_2"][0]))
    for half in range(2):
        put("e_qk", inputs["e_qk_norm_2"][0].T, slice(HD2 * half, HD2 * half + HD2))
        put("o_qk", inputs["o_qk_norm_2"][0].T, slice(HD2 * half, HD2 * half + HD2))
        put("b_i", inputs["b_igate"][0, half][:, None], slice(32 * half, 32 * half + HEADS))
        put("b_f", inputs["b_fgate"][0, half][:, None], slice(32 * half, 32 * half + HEADS))
    put("sinks", np.broadcast_to(inputs["e_sinks_2"][0][None, :], (P, A_HEADS)))
    put("o_bf", inputs["o_b_f_2"][0][:, None], slice(0, C_HEADS))
    put("eps", np.full((P, 1), EPS, np.float32))
    put("edge", np.broadcast_to(edge_constants()[None, :], (P, 2 * PAD * len(WINDOWS))))
    return vecs


DIRECT = ["x", "w_in", "pool_mix_w", "w_proj_pool", "w_proj_mlstm", "w_out", "norm_post_g", "mem_2",
          "e_w_in_2", "e_w_mem_kv_2", "e_w_out_2", "o_w_in_2", "o_w_mem_kv_2", "o_w_out_2"]


def kernel(**inputs):
    import concourse.bacc as bacc
    from concourse.bass_utils import run_bass_kernel_spmd

    nc = bacc.Bacc("TRN2", target_bir_lowering=False, num_devices=1)
    inputs = {k: np.asarray(v) for k, v in inputs.items()}
    arrays = {k: np.ascontiguousarray(inputs[k]) for k in DIRECT}
    arrays["vecs"] = pack(inputs)
    arrays["consts"] = shape_constants()
    aps = {k: nc.dram_tensor(k + "_dram", a.shape, F32, kind="ExternalInput").ap() for k, a in arrays.items()}
    out = nc.dram_tensor("out_dram", (1, S, D), F32, kind="ExternalOutput").ap()
    hybrid_block_then_two_attention_layers(nc, aps, aps["vecs"], aps["consts"], out)
    result = run_bass_kernel_spmd(nc, [{k + "_dram": a for k, a in arrays.items()}], core_ids=[0])
    return result.results[0]["out_dram"]
```
